# Optimizing a Trainium2 kernel written in Bass

```python
import math
import jax, jax.numpy as jnp
from jax import lax
import numpy as np

D_MODEL = 1024
BATCH = 1
SEQ = 512
DEPTH = 1

MEM_LEN = 256

SSM_WIDTH = 512
SSM_GROUP = 16
SSM_GROUPS = SSM_WIDTH // SSM_GROUP
SSM_STATE = 64
SSM_DT_MIN = 1e-3
SSM_DT_MAX = 1e-1
SSM_EIG_CLIP = -1e-4

N_HEADS = 16
N_KV_HEADS = 4
HEAD_DIM = 64
GQA_GROUP = N_HEADS // N_KV_HEADS
CMP_BLOCK = 32
CMP_STRIDE = 16
CMP_HIDDEN = 256
SLC_BLOCK = 64
SLC_TOP_N = 8
WINDOW = 512
Q_BLOCK = 64
SEL_BIG = 1e9

X_HEADS = 4
X_HEAD_DIM = D_MODEL // X_HEADS

D_FF = 256 * ((8 * D_MODEL + 3 * 256 - 1) // (3 * 256))

DEEPNORM_ALPHA = (2.0 * DEPTH) ** 0.25
DEEPNORM_BETA = (8.0 * DEPTH) ** -0.25
LN_EPS = 1e-5

Q_WIDTH = N_HEADS * HEAD_DIM
KV_WIDTH = 2 * N_KV_HEADS * HEAD_DIM
IN_SPLITS = (SSM_WIDTH, Q_WIDTH, KV_WIDTH, KV_WIDTH, KV_WIDTH, 3 * N_HEADS, 2 * D_MODEL)
IN_WIDTH = sum(IN_SPLITS)

kernel_name = "hybrid_s5_nsa_deepnorm_layer"

def _layer_norm(x, g, b):
    xf = x.astype(jnp.float32)
    mu = jnp.mean(xf, axis=-1, keepdims=True)
    var = jnp.mean(jnp.square(xf - mu), axis=-1, keepdims=True)
    return ((xf - mu) * lax.rsqrt(var + LN_EPS) * g + b).astype(x.dtype)

def _masked_softmax(s, mask):
    s = jnp.where(mask, s, -jnp.inf)
    m = jnp.max(s, axis=-1, keepdims=True)
    m = jnp.where(jnp.isfinite(m), m, 0.0)
    p = jnp.exp(s - m)
    return p / jnp.maximum(jnp.sum(p, axis=-1, keepdims=True), 1e-30)

def _alibi_slopes():
    h = jnp.arange(1, N_HEADS + 1, dtype=jnp.float32)
    return jnp.exp2(-8.0 * h / N_HEADS)

def _s5_branch(u, a_re, a_im, b_re, b_im, c_re, c_im, d_skip, log_dt, w_glu, b_glu, w_o):
    bsz, L, _ = u.shape
    uf = u.astype(jnp.float32)
    ug = uf.reshape(bsz, L, SSM_GROUPS, SSM_GROUP)
    lam_re = jnp.minimum(a_re.astype(jnp.float32), SSM_EIG_CLIP)
    lam_im = a_im.astype(jnp.float32)
    dt = jnp.exp(log_dt.astype(jnp.float32))[:, None]
    mag = jnp.exp(lam_re * dt)
    lb_re = mag * jnp.cos(lam_im * dt)
    lb_im = mag * jnp.sin(lam_im * dt)
    den = jnp.square(lam_re) + jnp.square(lam_im)
    nr = lb_re - 1.0
    f_re = (nr * lam_re + lb_im * lam_im) / den
    f_im = (lb_im * lam_re - nr * lam_im) / den
    br = b_re.astype(jnp.float32)
    bi = b_im.astype(jnp.float32)
    bb_re = f_re[..., None] * br - f_im[..., None] * bi
    bb_im = f_re[..., None] * bi + f_im[..., None] * br
    bu_re = jnp.einsum('blgc,gnc->blgn', ug, bb_re)
    bu_im = jnp.einsum('blgc,gnc->blgn', ug, bb_im)
    shape_a = (1, L, SSM_GROUPS, SSM_STATE)
    a_seq_re = jnp.broadcast_to(lb_re[None, None], shape_a)
    a_seq_im = jnp.broadcast_to(lb_im[None, None], shape_a)

    def combine(e1, e2):
        a1r, a1i, b1r, b1i = e1
        a2r, a2i, b2r, b2i = e2
        return (a1r * a2r - a1i * a2i,
                a1r * a2i + a1i * a2r,
                a2r * b1r - a2i * b1i + b2r,
                a2r * b1i + a2i * b1r + b2i)

    _, _, h_re, h_im = lax.associative_scan(combine, (a_seq_re, a_seq_im, bu_re, bu_im), axis=1)
    y = (jnp.einsum('blgn,gcn->blgc', h_re, c_re.astype(jnp.float32))
         - jnp.einsum('blgn,gcn->blgc', h_im, c_im.astype(jnp.float32)))
    y = y.reshape(bsz, L, SSM_WIDTH) + d_skip.astype(jnp.float32) * uf
    g = jax.nn.gelu(y)
    y = g * jax.nn.sigmoid(g @ w_glu.astype(jnp.float32) + b_glu.astype(jnp.float32))
    return y.astype(u.dtype) @ w_o

def _nsa_branch(q, kv_cmp, kv_slc, kv_win, gate_logits, cmp_pos, cmp_w1, cmp_b1, cmp_w2, w_o):
    bsz, L = q.shape[0], q.shape[1]
    n_cmp = L // CMP_STRIDE - CMP_BLOCK // CMP_STRIDE + 1
    n_slc = L // SLC_BLOCK
    n_sel = min(SLC_TOP_N, n_slc)
    scale = HEAD_DIM ** -0.5
    slopes = _alibi_slopes().reshape(N_KV_HEADS, GQA_GROUP)

    kv = jnp.moveaxis(kv_cmp, 2, 0)
    chunks = kv.reshape(2, bsz, L // CMP_STRIDE, CMP_STRIDE, N_KV_HEADS, HEAD_DIM)
    blocks = jnp.concatenate([chunks[:, :, r:r + n_cmp] for r in range(CMP_BLOCK // CMP_STRIDE)], axis=3)
    blocks = blocks + cmp_pos[:, None, None, :, None, :]
    flat = jnp.moveaxis(blocks, 3, 4).reshape(2, bsz, n_cmp, N_KV_HEADS, CMP_BLOCK * HEAD_DIM)
    hid = jax.nn.gelu(jnp.einsum('zbnhf,zfe->zbnhe', flat, cmp_w1) + cmp_b1[:, None, None, None, :])
    comp = jnp.einsum('zbnhe,zed->zbnhd', hid, cmp_w2)
    k_c, v_c = comp[0], comp[1]
    cmp_start = jnp.arange(n_cmp) * CMP_STRIDE
    cmp_end = cmp_start + CMP_BLOCK - 1
    slc_start = jnp.arange(n_slc) * SLC_BLOCK
    overlap = ((cmp_start[:, None] < slc_start[None, :] + SLC_BLOCK)
               & (cmp_end[:, None] >= slc_start[None, :])).astype(jnp.float32)

    k_s = kv_slc[:, :, 0].reshape(bsz, n_slc, SLC_BLOCK, N_KV_HEADS, HEAD_DIM).transpose(0, 3, 1, 2, 4)
    v_s = kv_slc[:, :, 1].reshape(bsz, n_slc, SLC_BLOCK, N_KV_HEADS, HEAD_DIM).transpose(0, 3, 1, 2, 4)

    pad = ((0, 0), (WINDOW, 0), (0, 0), (0, 0))
    k_w = jnp.pad(kv_win[:, :, 0], pad)
    v_w = jnp.pad(kv_win[:, :, 1], pad)

    qg = q.reshape(bsz, L, N_KV_HEADS, GQA_GROUP, HEAD_DIM)
    b_idx = jnp.arange(bsz)[:, None, None, None]
    h_idx = jnp.arange(N_KV_HEADS)[None, :, None, None]
    blk = jnp.arange(n_slc)
    in_blk = jnp.arange(SLC_BLOCK)
    win_off = jnp.arange(WINDOW + Q_BLOCK) - WINDOW

    def query_block(c):
        t0 = c * Q_BLOCK
        t = t0 + jnp.arange(Q_BLOCK)
        qc = lax.dynamic_slice_in_dim(qg, t0, Q_BLOCK, axis=1)

        s = jnp.einsum('bqhgd,bnhd->bhgqn', qc, k_c, preferred_element_type=jnp.float32) * scale
        dist = t[:, None] - cmp_end[None, :]
        s = s - slopes[:, :, None, None] * dist
        p_cmp = _masked_softmax(s, dist >= 0)
        o_cmp = jnp.einsum('bhgqn,bnhd->bqhgd', p_cmp, v_c)

        imp = jnp.einsum('bhgqn,nj->bhqj', p_cmp, overlap)
        cur = t // SLC_BLOCK
        forced = (blk[None, :] == 0) | (blk[None, :] == cur[:, None]) | (blk[None, :] == cur[:, None] - 1)
        future = blk[None, :] * SLC_BLOCK > t[:, None]
        imp = jnp.where(forced, SEL_BIG, jnp.where(future, -SEL_BIG, imp))
        _, idx = lax.top_k(imp, n_sel)
        k_sel = k_s[b_idx, h_idx, idx].reshape(bsz, N_KV_HEADS, Q_BLOCK, n_sel * SLC_BLOCK, HEAD_DIM)
        v_sel = v_s[b_idx, h_idx, idx].reshape(bsz, N_KV_HEADS, Q_BLOCK, n_sel * SLC_BLOCK, HEAD_DIM)
        s_pos = (idx[..., None] * SLC_BLOCK + in_blk).reshape(bsz, N_KV_HEADS, Q_BLOCK, n_sel * SLC_BLOCK)
        dist = t[:, None] - s_pos
        s = jnp.einsum('bqhgd,bhqsd->bhgqs', qc, k_sel, preferred_element_type=jnp.float32) * scale
        s = s - slopes[:, :, None, None] * dist[:, :, None]
        p = _masked_softmax(s, (dist >= 0)[:, :, None])
        o_slc = jnp.einsum('bhgqs,bhqsd->bqhgd', p, v_sel)

        k_wc = lax.dynamic_slice_in_dim(k_w, t0, WINDOW + Q_BLOCK, axis=1)
        v_wc = lax.dynamic_slice_in_dim(v_w, t0, WINDOW + Q_BLOCK, axis=1)
        w_pos = t0 + win_off
        dist = t[:, None] - w_pos[None, :]
        mask = (dist >= 0) & (dist < WINDOW) & (w_pos[None, :] >= 0)
        s = jnp.einsum('bqhgd,bkhd->bhgqk', qc, k_wc, preferred_element_type=jnp.float32) * scale
        s = s - slopes[:, :, None, None] * dist
        p = _masked_softmax(s, mask)
        o_win = jnp.einsum('bhgqk,bkhd->bqhgd', p, v_wc)
        return jnp.stack([o_cmp, o_slc, o_win], axis=0).astype(q.dtype)

    o = lax.map(query_block, jnp.arange(L // Q_BLOCK))
    o = jnp.moveaxis(o, 0, 2).reshape(3, bsz, L, N_HEADS, HEAD_DIM)
    g = jax.nn.sigmoid(gate_logits.astype(jnp.float32)).reshape(bsz, L, N_HEADS, 3)
    o = jnp.einsum('zblhd,blhz->blhd', o, g)
    return o.reshape(bsz, L, Q_WIDTH).astype(q.dtype) @ w_o

def _memory_cross_attention(h, mem, w_q, w_kv, w_o):
    bsz, L, _ = h.shape
    m = mem.shape[1]
    q = (h @ w_q).reshape(bsz, L, X_HEADS, X_HEAD_DIM)
    kv = (mem @ w_kv).reshape(bsz, m, 2, X_HEADS, X_HEAD_DIM)
    s = jnp.einsum('blhd,bmhd->bhlm', q, kv[:, :, 0], preferred_element_type=jnp.float32) * (X_HEAD_DIM ** -0.5)
    p = jax.nn.softmax(s, axis=-1)
    o = jnp.einsum('bhlm,bmhd->blhd', p, kv[:, :, 1]).astype(h.dtype)
    return o.reshape(bsz, L, D_MODEL) @ w_o

def _swiglu(h, w_in, w_out):
    gate, up = jnp.split(h @ w_in, 2, axis=-1)
    return (jax.nn.silu(gate) * up) @ w_out

def setup_inputs(seed: int = 0) -> dict:
    key = jax.random.key(seed)
    keys = iter(jax.random.split(key, 40))

    def nrm(shape, std):
        return std * jax.random.normal(next(keys), shape, jnp.float32)

    G, N = SSM_GROUPS, SSM_STATE
    n_idx = jnp.arange(N, dtype=jnp.float32)
    return {
        "x": nrm((BATCH, SEQ, D_MODEL), 1.0),
        "mem": nrm((BATCH, MEM_LEN, D_MODEL), 1.0),
        "ln_emb_g": 1.0 + nrm((D_MODEL,), 0.02),
        "ln_emb_b": nrm((D_MODEL,), 0.02),
        "w_in": nrm((DEPTH, D_MODEL, IN_WIDTH), D_MODEL ** -0.5),
        "ssm_a_re": -0.5 + nrm((DEPTH, G, N), 0.01),
        "ssm_a_im": jnp.pi * n_idx + nrm((DEPTH, G, N), 0.01),
        "ssm_b_re": nrm((DEPTH, G, N, SSM_GROUP), (2.0 * SSM_GROUP) ** -0.5),
        "ssm_b_im": nrm((DEPTH, G, N, SSM_GROUP), (2.0 * SSM_GROUP) ** -0.5),
        "ssm_c_re": nrm((DEPTH, G, SSM_GROUP, N), (2.0 * N) ** -0.5),
        "ssm_c_im": nrm((DEPTH, G, SSM_GROUP, N), (2.0 * N) ** -0.5),
        "ssm_d": nrm((DEPTH, SSM_WIDTH), 1.0),
        "ssm_log_dt": jax.random.uniform(next(keys), (DEPTH, G), jnp.float32,
                                         minval=math.log(SSM_DT_MIN), maxval=math.log(SSM_DT_MAX)),
        "ssm_w_glu": nrm((DEPTH, SSM_WIDTH, SSM_WIDTH), SSM_WIDTH ** -0.5),
        "ssm_b_glu": nrm((DEPTH, SSM_WIDTH), 0.01),
        "ssm_w_out": nrm((DEPTH, SSM_WIDTH, D_MODEL), SSM_WIDTH ** -0.5),
        "cmp_pos": nrm((DEPTH, 2, CMP_BLOCK, HEAD_DIM), 0.02),
        "cmp_w1": nrm((DEPTH, 2, CMP_BLOCK * HEAD_DIM, CMP_HIDDEN), (CMP_BLOCK * HEAD_DIM) ** -0.5),
        "cmp_b1": nrm((DEPTH, 2, CMP_HIDDEN), 0.01),
        "cmp_w2": nrm((DEPTH, 2, CMP_HIDDEN, HEAD_DIM), CMP_HIDDEN ** -0.5),
        "nsa_w_out": nrm((DEPTH, Q_WIDTH, D_MODEL), Q_WIDTH ** -0.5),
        "w_out": nrm((DEPTH, D_MODEL, D_MODEL), DEEPNORM_BETA * D_MODEL ** -0.5),
        "ln1_g": 1.0 + nrm((DEPTH, D_MODEL), 0.02),
        "ln1_b": nrm((DEPTH, D_MODEL), 0.02),
        "xattn_w_q": nrm((DEPTH, D_MODEL, D_MODEL), D_MODEL ** -0.5),
        "xattn_w_kv": nrm((DEPTH, D_MODEL, 2 * D_MODEL), D_MODEL ** -0.5),
        "xattn_w_o": nrm((DEPTH, D_MODEL, D_MODEL), DEEPNORM_BETA * D_MODEL ** -0.5),
        "ln2_g": 1.0 + nrm((DEPTH, D_MODEL), 0.02),
        "ln2_b": nrm((DEPTH, D_MODEL), 0.02),
        "ffn_w_in": nrm((DEPTH, D_MODEL, 2 * D_FF), D_MODEL ** -0.5),
        "ffn_w_out": nrm((DEPTH, D_FF, D_MODEL), DEEPNORM_BETA * D_FF ** -0.5),
        "ln3_g": 1.0 + nrm((DEPTH, D_MODEL), 0.02),
        "ln3_b": nrm((DEPTH, D_MODEL), 0.02),
    }

def reference(x, mem, ln_emb_g, ln_emb_b, w_in, ssm_a_re, ssm_a_im, ssm_b_re, ssm_b_im,
              ssm_c_re, ssm_c_im, ssm_d, ssm_log_dt, ssm_w_glu, ssm_b_glu, ssm_w_out,
              cmp_pos, cmp_w1, cmp_b1, cmp_w2, nsa_w_out, w_out, ln1_g, ln1_b,
              xattn_w_q, xattn_w_kv, xattn_w_o, ln2_g, ln2_b,
              ffn_w_in, ffn_w_out, ln3_g, ln3_b):
    bsz, L, _ = x.shape
    cuts = np.cumsum(IN_SPLITS)[:-1].tolist()
    h = _layer_norm(x, ln_emb_g, ln_emb_b)
    for l in range(DEPTH):
        z = h @ w_in[l]
        u, q, kv_c, kv_s, kv_w, g_nsa, g_mix = jnp.split(z, cuts, axis=-1)
        y_ssm = _s5_branch(u, ssm_a_re[l], ssm_a_im[l], ssm_b_re[l], ssm_b_im[l],
                           ssm_c_re[l], ssm_c_im[l], ssm_d[l], ssm_log_dt[l],
                           ssm_w_glu[l], ssm_b_glu[l], ssm_w_out[l])
        kv_shape = (bsz, L, 2, N_KV_HEADS, HEAD_DIM)
        y_nsa = _nsa_branch(q.reshape(bsz, L, N_HEADS, HEAD_DIM), kv_c.reshape(kv_shape),
                            kv_s.reshape(kv_shape), kv_w.reshape(kv_shape), g_nsa,
                            cmp_pos[l], cmp_w1[l], cmp_b1[l], cmp_w2[l], nsa_w_out[l])
        gate_ssm, gate_nsa = jnp.split(jax.nn.sigmoid(g_mix), 2, axis=-1)
        mixed = (gate_ssm * y_ssm + gate_nsa * y_nsa) @ w_out[l]
        h = _layer_norm(DEEPNORM_ALPHA * h + mixed, ln1_g[l], ln1_b[l])
        h = _layer_norm(DEEPNORM_ALPHA * h + _memory_cross_attention(h, mem, xattn_w_q[l], xattn_w_kv[l], xattn_w_o[l]),
                        ln2_g[l], ln2_b[l])
        h = _layer_norm(DEEPNORM_ALPHA * h + _swiglu(h, ffn_w_in[l], ffn_w_out[l]), ln3_g[l], ln3_b[l])
    return h


_drawn_inputs = setup_inputs


def setup_inputs(seed=0):
    import zlib

    import numpy as np

    out = dict(_drawn_inputs(seed))
    spreads = {}
    factors = {'ln_emb_b': 2.817,
     'ssm_a_re': 64.0,
     'ssm_a_im': 64.0,
     'ssm_b_re': 64.0,
     'ssm_b_im': 64.0,
     'ssm_c_re': 64.0,
     'ssm_c_im': 64.0,
     'ssm_log_dt': 64.0,
     'ssm_b_glu': 64.0,
     'cmp_pos': 24.276,
     'cmp_b1': 55.29,
     'ln1_g': 2.715,
     'ln1_b': 2.818,
     'ln2_g': 2.997,
     'ln3_g': 8.424,
     'ln3_b': 7.957,
     'ln2_b': 6.688}
    for name, (base, spread) in spreads.items():
        noise = np.random.default_rng([zlib.crc32(name.encode()), seed]).standard_normal(out[name].shape)
        drawn = base * np.exp(spread * noise) if base else spread * noise
        out[name] = __import__('jax').numpy.asarray(drawn.astype(out[name].dtype))
    for name, factor in factors.items():
        out[name] = (out[name] * factor).astype(out[name].dtype)
    return out
```

```python
import math
from contextlib import ExitStack

import concourse.bass as bass
from concourse import mybir

ALU = mybir.AluOpType
ACT = mybir.ActivationFunctionType
AX = mybir.AxisListType
F32 = mybir.dt.float32
F32R = mybir.dt.float32r

P = 128
D = 1024
T = 512
KT = D // P
MEM = 256
NG, GC, NS = 32, 16, 64
NGP = NG // 2
CH = 8
NCH = T // CH
NH, NKV, HD = 16, 4, 64
NCMP = 31
DFF = 2816
KF = DFF // P
XH = 4
ALPHA = 2.0 ** 0.25
EPS = 1e-5
MASKED = -1e30
MAX_FLOOR = -1e25
SLOPES = [2.0 ** (-8.0 * (h + 1) / NH) for h in range(NH)]
TWO_PI = 2 * math.pi
PI_A = 6.28125
PI_B = 0.0019340515136719
PI_C = TWO_PI - PI_A - PI_B
ROUND = 1.5 * 2.0 ** 23

C_U, C_Q, C_KVC, C_KVS, C_KVW, C_GN, C_GM = 0, 512, 1536, 2048, 2560, 3072, 3120

STAGES = [("u", 4), ("gmix", 16), ("glu", 2), ("sso", 4), ("v", 4), ("kq", 16), ("nsa", 8), ("wout", 8),
          ("xk", 8), ("xv", 8), ("xq", 8), ("xo", 8), ("fin", 2 * KF), ("fout", KF)]
BLOCKS = {}
UNITS = 4 * NH * 2
CMP_TURN, CMP_PV, COMBINE, O_STEP = 3, 5, 3, 6


def unit(u):
    g = u // 16
    return g, u % 2, 8 * (g % 2) + u % 16 // 2, g // 2


_at = 0
for _n, _c in STAGES:
    BLOCKS[_n] = _at
    _at += _c
NBLOCKS = _at


def build(nc, I, out):
    KB = 1024
    BASE = 16512
    RG = 72 * KB
    RX = 104 * KB
    RC = 202 * KB

    def at(name, shape, off, dt=F32):
        return nc.alloc_sbuf_tensor_at(name, shape, dt, offset=BASE + int(off))

    wraw = [at(f"wraw{s}", [P, 1024], s * 4 * KB) for s in range(2)]
    whi = [at(f"whi{s}", [P, 1024], (8 + s * 4) * KB, F32R) for s in range(2)]
    wlo = [at(f"wlo{s}", [P, 1024], (16 + s * 4) * KB, F32R) for s in range(2)]
    hF = at("hF", [P, KT, T], 24 * KB)
    hHi = at("hHi", [P, KT, T], 40 * KB, F32R)
    hLo = at("hLo", [P, KT, T], 56 * KB, F32R)
    G = at("G", [P, 2 * KT, T], RG)
    ident = at("ident", [P, P], RC)
    mean_w = at("mean_w", [P, P], RC + 512)
    vecT = at("vecT", [P, 72], RC + 1024)
    ET = at("ET", [P, 2, 8, NGP], RC + 1536)
    kcT = at("kcT", [P, 2, 2, 32], RC + 2560)
    gates = at("gates", [P, 4, 3 * NH], RC + 3072)
    cdist = at("cdist", [P, 4, 32], RC + 3840)
    c2 = RC + 4352
    slope_row = at("slope_row", [P, NH], c2)
    posT = at("posT", [P, 2, 16], c2 + 64)
    hidb = at("hidb", [P, 4], c2 + 192)
    Dcol = at("Dcol", [P, NG], c2 + 224)
    nmax = at("nmax", [P, 8], c2 + 352)
    sums = at("sums", [P, 2, 3, NH], c2 + 384)
    cmax = at("cmax", [P, NH], c2 + 768)
    wbr = at("wbr", [P, 3, 8], c2 + 832)
    xmax = at("xmax", [P, 4], c2 + 928)
    xsum = at("xsum", [P, 4], c2 + 960)
    bnst = at("bnst", [P, 4, 2, 6], c2 + 992)
    bnmv = at("bnmv", [P, 4, 2], c2 + 1184)
    rinv = at("rinv", [P, 4], c2 + 1216)

    xtok = at("xtok", [P, 4, D], RX + 16 * KB)
    FP = at("FP", [NGP, 2, 8, P], RG)
    LP = at("LP", [NGP, 2, 8, P], RG + 8 * KB)
    EP = at("EP", [NGP, 2, 8, P], RG + 16 * KB)
    sp = {n: at("sp_" + n, [NGP, P], RG + 24 * KB + i * 512) for i, n in enumerate(
        ["are", "aim", "th", "er", "k", "s", "s2", "den", "nr", "fr", "fi", "a", "b", "c", "d"])}
    ldt = at("ldt", [NGP, 2], RG + 24 * KB + 15 * 512)
    dtt = at("dtt", [NGP, 2], RG + 24 * KB + 15 * 512 + 32)
    TP = 65 * KB
    cm = [at(f"cm{i}", [NGP, 4, P], RX + TP + i * 2 * KB) for i in range(4)]
    vrows = at("vrows", [72, P], RX + TP + 8 * KB)
    dl = at("dl", [NG, GC], RX + TP + 8 * KB + 512)
    posl = at("posl", [16, 2, P], RX + TP + 9 * KB)
    rep16 = at("rep16", [GC, 8, GC], RX + TP + 10 * KB)
    dT = at("dT", [GC, NG], RX + TP + 10 * KB + 512)
    Bt = at("Bt", [P, 2, NGP, GC], RX)
    Craw = at("Craw", [P, 2, 4, 2, NS], RX + 2 * KB)
    Ct = at("Ct", [P, 2, NGP, GC], RX + 6 * KB)
    LT = at("LT", [P, 2, 2, 8, NGP], RX + 8 * KB)
    Cbd = at("Cbd", [P, 2, NGP, 2, GC], RX + 10 * KB)
    Wst = at("Wst", [P, 2, NGP, P], RX)
    Mst = at("Mst", [P, NG, P], RX + 16 * KB)
    Ost = at("Ost", [P, 2, NGP, 8, GC], RX + 32 * KB)
    H = at("H", [P, 2, NGP, NCH + 1], RX + 48 * KB)
    Otmp = at("Otmp", [P, NGP, 8, GC], RX + 48 * KB)
    UT = at("UT", [P, NG, NCH], RX + 57 * KB)
    Ptmp = at("Ptmp", [P, NGP, 8, GC], RX + 57 * KB)
    Pw = at("Pw", [P, 2, NGP, 15, GC], RX + TP)
    U8 = at("U8", [NCH, NG, 8, GC], RX + TP)
    U1 = at("U1", [P, NG, 4, GC], RX + 81 * KB)
    st1 = at("st1", [P, 2, NGP, 8], RX + 81 * KB)
    st2 = at("st2", [P, 2, NGP, 8], RX + 82 * KB)
    Yt = at("Yt", [NCH, 8, 512], RX + TP)
    gF = at("gF", [P, 4, T], RX)
    gHi = at("gHi", [P, 4, T], RX + 8 * KB, F32R)
    gLo = at("gLo", [P, 4, T], RX + 16 * KB, F32R)
    yF = at("yF", [P, 4, T], RX + 24 * KB)
    yHi = at("yHi", [P, 4, T], RX + 32 * KB, F32R)
    yLo = at("yLo", [P, 4, T], RX + 40 * KB, F32R)
    kqT = at("kqT", [P, 16, T], RX)
    qT, kvcT, kT = kqT[:, 0:8, :], kqT[:, 8:12, :], kqT[:, 12:16, :]
    VA = at("VA", [P, 4, 512], RX + 32 * KB)
    Xc = at("Xc", [P, 2, NKV, T], RX + 40 * KB)
    w1 = at("w1", [P, 2, 16, 256], RX + 56 * KB)
    w2 = at("w2", [P, 2, 2, 2 * HD], RX + 88 * KB)
    wg = at("wg", [P, KT, 3 * NH], RX + 92 * KB)
    hidK = at("hidK", [P, 2, NKV, 32], RX + 90 * KB)
    hidV = at("hidV", [P, 2, NKV, 4, 32], RX + 56 * KB)
    Dh = at("Dh", [P, NH, T], RX + 56 * KB)
    Dc = at("Dc", [P, NH, 32], RX + 88 * KB)
    PTc = at("PTc", [P, NKV, P], RX + 90 * KB)
    Vbd = at("Vbd", [P, NKV, 4, HD], RX + 92 * KB)
    Tr = [at(f"Tr{i}", [P, T], RX + (40 + 2 * i) * KB) for i in range(3)]
    Pr = [at(f"Pr{i}", [P, T], RX + (46 + 2 * i) * KB) for i in range(3)]
    PTr = [at(f"PTr{i}", [P, T], RX + (16 + 2 * i) * KB) for i in range(3)]
    Tc = at("Tc", [P, NH, 32], RX + 22 * KB)
    oS = [at(f"oS{i}", [P, 8, HD], RX + (52 + 2 * i) * KB) for i in range(2)]
    otmp = at("otmp", [P, 8, HD], RX + 96 * KB)
    mHi = at("mHi", [P, KT, T], RX, F32R)
    mLo = at("mLo", [P, KT, T], RX + 16 * KB, F32R)
    mF = [at(f"mF{i}", [P, T], RX + (32 + 2 * i) * KB) for i in range(2)]
    xc = at("xc", [P, KT, T], RX + 36 * KB)
    rstd = at("rstd", [P, T], RX + 52 * KB)
    sq = at("sq", [P, KT, T], RG)
    memHi = at("memHi", [P, KT, MEM], RX + 58 * KB, F32R)
    memLo = at("memLo", [P, KT, MEM], RX + 66 * KB, F32R)
    memF = at("memF", [P, 2, D], RX + 74 * KB)
    kxT = at("kxT", [P, KT, MEM], RX + 82 * KB)
    vx = at("vx", [P, 2, D], RX + 90 * KB)
    qx = at("qx", [P, KT, T], RG)
    xP = [at(f"xP{i}", [P, MEM], RG + (16 + i) * KB) for i in range(2)]
    xPT = [at(f"xPT{i}", [P, 2, T], RG + (18 + 4 * i) * KB) for i in range(2)]
    sHi = at("sHi", [P, KF, T], RG, F32R)
    sLo = at("sLo", [P, KF, T], RG + 44 * KB, F32R)
    sg = [at(f"sg{i}", [P, T], RX + (56 + 2 * i) * KB) for i in range(2)]
    sF = [at(f"sF{i}", [P, T], RX + (60 + 2 * i) * KB) for i in range(2)]
    xc3 = at("xc3", [P, KT, T], RX + 64 * KB)
    rstd3 = at("rstd3", [P, T], RX + 80 * KB)
    otok = [at(f"otok{i}", [P, D], (40 + 4 * i) * KB) for i in range(4)]

    ctx = ExitStack()
    with ctx:
        def sem(name):
            return ctx.enter_context(nc.semaphore(name))

        bank = [ctx.enter_context(nc.psum_tensor(f"bank{i}", [P, 512], F32)) for i in range(8)]

        w_landed = [sem("w_landed0"), sem("w_landed1")]
        w_hi_ready, w_lo_ready, w_used = sem("w_hi_ready"), sem("w_lo_ready"), sem("w_used")
        tile_act, tile_dve = sem("tile_act"), sem("tile_dve")
        hhi_ready, hlo_ready = sem("hhi_ready"), sem("hlo_ready")
        x_landed, par_landed, vec_landed = sem("x_landed"), sem("par_landed"), sem("vec_landed")
        b_landed, c_landed, w1_landed = sem("b_landed"), sem("c_landed"), sem("w1_landed")
        xc_landed, mem_landed, u1_moved = sem("xc_landed"), sem("mem_landed"), sem("u1_moved")
        ident_ready, pool_const, dve_step = sem("ident_ready"), sem("pool_const"), sem("dve_step")
        pool_step = sem("pool_step")
        rep_ready, dt_ready, er_ready, mag_ready = (
            sem("rep_ready"), sem("dt_ready"), sem("er_ready"), sem("mag_ready"))
        angle_ready, sin_ready, powers_ready = sem("angle_ready"), sem("sin_ready"), sem("powers_ready")
        var0_ready, sd0_ready, xn_ready, h0_turned = (
            sem("var0_ready"), sem("sd0_ready"), sem("xn_ready"), sem("h0_turned"))
        hf0_ready = sem("hf0_ready")
        vec_turned, vec_ready, dcol_done = sem("vec_turned"), sem("vec_ready"), sem("dcol_done")
        lt_turned, lt_ready, ct_turned, ct_ready = sem("lt_turned"), sem("lt_ready"), sem("ct_turned"), sem("ct_ready")
        pw_ready, cbd_ready, o_ready = sem("pw_ready"), sem("cbd_ready"), sem("o_ready")
        m_built, m_ready, wst_turned, wst_ready = sem("m_built"), sem("m_ready"), sem("wst_turned"), sem("wst_ready")
        u1_ready, ut_turned, ut_ready = sem("u1_ready"), sem("ut_turned"), sem("ut_ready")
        s_done, h_loaded, scan_done = sem("s_done"), sem("h_loaded"), sem("scan_done")
        y_done, y_ready, yt_turned, gelu_done = sem("y_done"), sem("y_ready"), sem("yt_turned"), sem("gelu_done")
        ghi_ready, glo_ready = sem("ghi_ready"), sem("glo_ready")
        glu_sig, yf_ready, yhi_ready, ylo_ready = (
            sem("glu_sig"), sem("yf_ready"), sem("yhi_ready"), sem("ylo_ready"))
        sso_tile = sem("sso_tile")
        v_ready, gate_done, gate_ready = sem("v_ready"), sem("gate_done"), sem("gate_ready")
        hid_done, hidb_ready, hid_ready, pos_done = sem("hid_done"), sem("hidb_ready"), sem("hid_ready"), sem("pos_done")
        hid_padded = sem("hid_padded")
        kc_done, kc_ready, vc_done, vc_ready = sem("kc_done"), sem("kc_ready"), sem("vc_done"), sem("vc_ready")
        dist_ready, dh_ready = sem("dist_ready"), sem("dh_ready")
        dc_ready = sem("dc_ready")
        score_done, max_done, exp_done, turned, turned_dve, turned_act, pv_done = (
            sem("score_done"), sem("max_done"), sem("exp_done"), sem("turned"), sem("turned_dve"),
            sem("turned_act"), sem("pv_done"))
        cscore_done, tc_ready, pc_ready, csum_ready, cturned, ptc_ready, cpv_done = (
            sem("cscore_done"), sem("tc_ready"), sem("pc_ready"), sem("csum_ready"), sem("cturned"),
            sem("ptc_ready"), sem("cpv_done"))
        os_ready, o_turned, ohi_ready, olo_ready = (
            sem("os_ready"), sem("o_turned"), sem("ohi_ready"), sem("olo_ready"))
        mf_ready, mhi_ready, mlo_ready = sem("mf_ready"), sem("mhi_ready"), sem("mlo_ready")
        mu_ready, xc_ready, sq_ready, var_done, var_ready, sd_ready, nrm_ready, hf_ready = (
            sem("mu_ready"), sem("xc_ready"), sem("sq_ready"), sem("var_done"), sem("var_ready"),
            sem("sd_ready"), sem("nrm_ready"), sem("hf_ready"))
        mem_turned, memhi_ready, memlo_ready, xv_ready = (
            sem("mem_turned"), sem("memhi_ready"), sem("memlo_ready"), sem("xv_ready"))
        xs_done, xmax_ready, xexp_done, xp_ready, xt_done, xpt_ready, xo_done, xohi_ready, xolo_ready = (
            sem("xs_done"), sem("xmax_ready"), sem("xexp_done"), sem("xp_ready"), sem("xt_done"),
            sem("xpt_ready"), sem("xo_done"), sem("xohi_ready"), sem("xolo_ready"))
        sg_ready, sf_ready, shi_ready, slo_ready, fout_done = (
            sem("sg_ready"), sem("sf_ready"), sem("shi_ready"), sem("slo_ready"), sem("fout_done"))
        out_turned, out_copied_a, out_copied_d, out_stored = (
            sem("out_turned"), sem("out_copied_a"), sem("out_copied_d"), sem("out_stored"))

        block = ctx.enter_context(nc.Block())

        w_in, wX = I["w_in"][0], {k: I[k][0] for k in (
            "ssm_w_glu", "ssm_w_out", "nsa_w_out", "w_out", "xattn_w_q", "xattn_w_kv", "xattn_w_o",
            "ffn_w_in", "ffn_w_out")}

        def rows(w):
            return w.rearrange("(k p) n -> p k n", p=P)

        TA = {"gmix": 2}
        TD = {"sso": 2, "kq": 10, "nsa": 26, "wout": 34, "xk": 42, "xq": 50, "xo": 58, "fout": 66}
        TD_END = 74

        @block.sync
        def _(sp_):
            xt = I["x"][0].rearrange("(a p) n -> p a n", p=P)
            sp_.dma_start(xtok[:, :, :], xt).then_inc(x_landed, 16)

            def load(b, s, dst, src):
                if not (isinstance(b, int) and b < 2):
                    sp_.wait_ge(w_lo_ready, b - 1)
                for half in range(2):
                    sp_.dma_start(dst[half], src[half]).then_inc(w_landed[s], 16)

            def by_k(s, src):
                nk = src.shape[1]
                dst = wraw[s][:, :].rearrange("p (k n) -> p k n", k=nk)
                return [dst[:, 0:nk // 2], dst[:, nk // 2:nk]], [src[:, 0:nk // 2], src[:, nk // 2:nk]]

            def row_block(s, w, r0, c0):
                dst = [wraw[s][:, 512 * e:512 * e + 512] for e in range(2)]
                return dst, [w[bass.ds(r0, P), c0 + 512 * e:c0 + 512 * e + 512] for e in range(2)]

            def column_tiles(name, count, w, c0, first=0):
                b0 = BLOCKS[name] + first
                with sp_.Fori(0, count // 2) as i:
                    for s in range(2):
                        load(i * 2 + (b0 + s), s, *by_k(s, rows(w)[:, :, bass.ds(i * (2 * P) + (P * s + c0), P)]))

            def row_tiles(name, count, w, c0):
                b0 = BLOCKS[name]
                with sp_.Fori(0, count // 2) as i:
                    for s in range(2):
                        load(i * 2 + (b0 + s), s, *row_block(s, w, i * (2 * P) + P * s, c0))

            for b in range(4):
                load(b, b % 2, *by_k(b % 2, rows(w_in)[:, 2 * b:2 * b + 2, C_U:C_U + 512]))
            column_tiles("gmix", 16, w_in, C_GM)
            for b in range(2):
                load(BLOCKS["glu"] + b, b, *by_k(b, rows(wX["ssm_w_glu"])[:, 2 * b:2 * b + 2, :]))
            for b in range(4):
                load(BLOCKS["sso"] + b, b % 2, *by_k(b % 2, rows(wX["ssm_w_out"])[:, :, 256 * b:256 * b + 256]))
            for b in range(4):
                dst = wraw[b % 2][:, :].rearrange("p (k z n) -> p z k n", k=2, z=2)
                src = [rows(w_in)[:, 2 * b:2 * b + 2, c + 256:c + 512] for c in (C_KVS, C_KVW)]
                load(BLOCKS["v"] + b, b % 2, [dst[:, 0], dst[:, 1]], src)
            for group in range(2):
                b0 = BLOCKS["kq"] + 4 * group
                with sp_.Fori(0, 2) as i:
                    for s in range(2):
                        dst = wraw[s][:, :].rearrange("p (k e n) -> p e k n", k=KT, e=2)
                        src = [rows(w_in)[:, :, bass.ds(i * (2 * HD) + (C_Q + 512 * group + 256 * e + HD * s), HD)]
                               for e in range(2)]
                        load(i * 2 + (b0 + s), s, [dst[:, 0], dst[:, 1]], src)
            column_tiles("kq", 4, w_in, C_KVC, first=8)
            for t, c in enumerate((C_KVS, C_KVS + P, C_KVW, C_KVW + P)):
                load(BLOCKS["kq"] + 12 + t, t % 2, *by_k(t % 2, rows(w_in)[:, :, c:c + P]))
            column_tiles("nsa", 8, wX["nsa_w_out"], 0)
            column_tiles("wout", 8, wX["w_out"], 0)
            column_tiles("xk", 8, wX["xattn_w_kv"], 0)
            row_tiles("xv", 8, wX["xattn_w_kv"], D)
            column_tiles("xq", 8, wX["xattn_w_q"], 0)
            column_tiles("xo", 8, wX["xattn_w_o"], 0)
            b0 = BLOCKS["fin"]
            with sp_.Fori(0, KF) as i:
                for s in range(2):
                    load(i * 2 + (b0 + s), s, *by_k(s, rows(wX["ffn_w_in"])[:, :, bass.ds(i * P + s * DFF, P)]))
            row_tiles("fout", KF, wX["ffn_w_out"], 0)
            for tt in range(4):
                sp_.wait_ge(out_copied_a, tt + 1)
                sp_.wait_ge(out_copied_d, tt + 1)
                sp_.dma_start(out[0, tt * P:(tt + 1) * P, :], otok[tt][:, :]).then_inc(out_stored, 16)
            sp_.wait_ge(out_stored, 64)

        @block.scalar
        def _(act):
            for r0, name in ((0, "ln_emb_g"), (8, "ln_emb_b"), (16, "ln1_g"), (24, "ln1_b"), (32, "ln2_g"),
                             (40, "ln2_b"), (48, "ln3_g"), (56, "ln3_b")):
                v = I[name] if name.startswith("ln_emb") else I[name][0]
                act.dma_start(vrows[r0:r0 + 8, :], v.rearrange("(k p) -> k p", p=P)).then_inc(vec_landed, 16)
            act.dma_start(vrows[64:68, :], I["ssm_b_glu"][0].rearrange("(k p) -> k p", p=P)).then_inc(vec_landed, 16)
            act.dma_start(vrows[68:72, :], I["cmp_b1"][0].rearrange("z (k p) -> (z k) p", p=P)).then_inc(vec_landed, 16)
            act.dma_start(dl[:, :], I["ssm_d"][0].rearrange("(g c) -> g c", c=GC)).then_inc(vec_landed, 16)
            act.dma_start(posl[:, :, :], I["cmp_pos"][0].rearrange("z (r q) d -> r z (q d)", q=2)).then_inc(
                vec_landed, 16)
            act.dma_start(sp["are"][:, :], I["ssm_a_re"][0].rearrange("(g q) n -> g (q n)", q=2)).then_inc(par_landed, 16)
            act.dma_start(sp["aim"][:, :], I["ssm_a_im"][0].rearrange("(g q) n -> g (q n)", q=2)).then_inc(par_landed, 16)
            act.dma_start(ldt[:, :], I["ssm_log_dt"][0].rearrange("(g q) -> g q", q=2)).then_inc(par_landed, 16)
            for ri, name in enumerate(("ssm_b_re", "ssm_b_im")):
                act.dma_start(Bt[:, ri], I[name][0].rearrange("(g q) n c -> (q n) g c", q=2)).then_inc(b_landed, 16)
            for ri, name in enumerate(("ssm_c_re", "ssm_c_im")):
                for dup in range(2):
                    act.dma_start(Craw[:, ri, :, dup, :], I[name][0].rearrange("(t g) c n -> (g c) t n", t=4)).then_inc(
                        c_landed, 16)

            def split(b, s, pair=None):
                if pair is None:
                    pair = b // 2
                act.wait_ge(w_landed[s], pair * 32 + 32)
                if not (isinstance(b, int) and b < 2):
                    act.wait_ge(w_used, b - 1)
                act.activation(whi[s][:, :], wraw[s][:, :], ACT.Copy).then_inc(w_hi_ready, 1)

            def splits_ahead(b0, s, i):
                split(i * 2 + (b0 + s + 1), (s + 1) % 2, i + (b0 // 2 + s))

            def o_hi(a, g):
                a.wait_ge(o_turned, g + 1)
                a.activation(hHi[:, 4 * (g % 2):4 * (g % 2) + 4, g // 2 * P:(g // 2 + 1) * P],
                             bank[7][:, :].rearrange("p (k n) -> p k n", k=4), ACT.Copy).then_inc(ohi_ready, 1)

            def xo_hi(a, h):
                for dt in range(2):
                    a.wait_ge(xo_done, 2 * h + dt + 1)
                    a.activation(mHi[:, 2 * h + dt, :], bank[6 + dt][:, :], ACT.Copy).then_inc(xohi_ready, 1)

            def squares(a, n, centred):
                for m in range(KT):
                    a.wait_ge(xc_ready, KT * (n - 1) + m + 1)
                    a.activation(sq[:, m, :], centred[:, m, :], ACT.Square).then_inc(sq_ready, 1)

            def affine(a, n, m, centred, col):
                c = KT * (n - 1) + m
                a.wait_ge(nrm_ready, c + 1)
                a.activation(hF[:, m, :], centred[:, m, :], ACT.Identity, scale=vecT[:, col + m:col + m + 1],
                             bias=vecT[:, col + 8 + m:col + 9 + m]).then_inc(hf_ready, 1)
                if n < 3:
                    a.wait_ge(hf_ready, c + 1)
                    a.activation(hHi[:, m, :], hF[:, m, :], ACT.Copy).then_inc(hhi_ready, 1)

            act.wait_ge(par_landed, 48)
            act.activation(dtt[:, :], ldt[:, :], ACT.Exp).then_inc(dt_ready, 1)
            act.wait_ge(er_ready, 1)
            act.activation(sp["er"][:, :], sp["er"][:, :], ACT.Exp).then_inc(mag_ready, 1)
            act.wait_ge(angle_ready, 1)
            act.activation(sp["s"][:, :], sp["th"][:, :], ACT.Sin).then_inc(sin_ready, 1)
            act.activation(sp["s2"][:, :], sp["th"][:, :], ACT.Sin, scale=0.5).then_inc(sin_ready, 1)
            act.wait_ge(var0_ready, 1)
            act.activation(rinv[:, :], rinv[:, :], ACT.Sqrt).then_inc(sd0_ready, 1)
            split(0, 0)
            for k in range(KT):
                act.wait_ge(hf0_ready, k + 1)
                act.activation(hHi[:, k, :], hF[:, k, :], ACT.Copy).then_inc(hhi_ready, 1)
            for b in range(4):
                split(b + 1, (b + 1) % 2)
            act.wait_ge(u1_ready, 1)
            for half in range(2):
                act.dma_start(U8[:, :, 4 * half:4 * half + 4, :], U1[half:P:2, :, :, :]).then_inc(u1_moved, 16)
            b0 = BLOCKS["gmix"]
            with act.Fori(0, 8) as i:
                for s in range(2):
                    splits_ahead(b0, s, i)
                    act.wait_ge(w_used, i * 2 + (b0 + s + 1))
                    act.activation(G[:, i * 2 + s, :], bank[s][:, :], ACT.Sigmoid).then_inc(tile_act, 1)
            for ct in range(4):
                act.wait_ge(yt_turned, ct + 1)
                act.activation(gF[:, ct, :], bank[2 + ct][:, :], ACT.Gelu_apprx_tanh).then_inc(gelu_done, 1)
            act.dma_start(w1[:, :, :, :], I["cmp_w1"][0].rearrange("z (r p) e -> p z r e", p=P)).then_inc(w1_landed, 16)
            for e in range(2):
                for z in range(2):
                    act.dma_start(w2[:, z, :, HD * e:HD * e + HD], I["cmp_w2"][0, z].rearrange(
                        "(k p) d -> p k d", p=P)).then_inc(w1_landed, 16)
            act.dma_start(wg[:, :, :], rows(w_in)[:, :, C_GN:C_GN + 3 * NH]).then_inc(w1_landed, 16)
            for ct in range(4):
                act.wait_ge(gelu_done, ct + 1)
                act.activation(gHi[:, ct, :], gF[:, ct, :], ACT.Copy).then_inc(ghi_ready, 1)
            for b in range(2):
                split(BLOCKS["glu"] + b + 1, (b + 1) % 2)
            act.wait_ge(vec_ready, 1)
            for m in range(4):
                act.wait_ge(w_used, BLOCKS["glu"] + 2)
                act.activation(yF[:, m, :], bank[2 + m][:, :], ACT.Sigmoid, bias=vecT[:, 64 + m:65 + m]).then_inc(glu_sig, 1)
            for m in range(4):
                act.wait_ge(yf_ready, m + 1)
                act.activation(yHi[:, m, :], yF[:, m, :], ACT.Copy).then_inc(yhi_ready, 1)
            for b in range(8):
                split(BLOCKS["sso"] + b + 1, (b + 1) % 2)
            b0 = BLOCKS["kq"]
            with act.Fori(0, 8) as i:
                for s in range(2):
                    splits_ahead(b0, s, i)
            act.wait_ge(tile_dve, TD["kq"] + 12)
            for h2 in range(2):
                src = kvcT[64 * h2:64 * h2 + 64, :, :].rearrange("d (z h) t -> d z h t", z=2)
                dst = Xc[:, :, :, :].rearrange("d z (h e) t -> d z h e t", e=2)
                act.dma_start(dst[0:64, :, :, h2, :], src).then_inc(xc_landed, 16)
                act.dma_start(dst[64:128, :, :, h2, 0:T - 1], src[:, :, :, 1:T]).then_inc(xc_landed, 16)
            act.wait_ge(gate_done, 1)
            act.activation(gates[:, :, :], bank[6][:, 0:4 * 48].rearrange("p (a n) -> p a n", a=4), ACT.Sigmoid).then_inc(
                gate_ready, 1)
            act.wait_ge(hidb_ready, 1)
            for j in range(4):
                act.wait_ge(hid_done, j + 1)
                src = bank[2 + j][:, 0:NKV * NCMP].rearrange("p (h n) -> p h n", h=NKV)
                if j < 2:
                    dst = hidK[:, j, :, 0:NCMP]
                else:
                    dst, src = hidV[:, j - 2, :, :, 0:NCMP], src[:, :, None, :].to_broadcast([P, NKV, 4, NCMP])
                act.activation(dst, src, ACT.Gelu_apprx_tanh, bias=hidb[:, j:j + 1]).then_inc(hid_ready, 1)

            for u in range(UNITS + 3):
                if u % 32 == 1 and u < UNITS:
                    qi = u // 32
                    act.wait_ge(tc_ready, qi + 1)
                    act.activation(Tc[:, :, :], Tc[:, :, :], ACT.Exp).then_inc(pc_ready, 1)
                if u < UNITS:
                    g, br, h, qi = unit(u)
                    n = P * (qi + 1)
                    act.wait_ge(max_done, u + 1)
                    if u >= 3:
                        act.wait_ge(turned, u - 2)
                    act.activation(Pr[u % 3][:, 0:n], Tr[u % 3][:, 0:n], ACT.Exp, bias=nmax[:, u % 8:u % 8 + 1],
                                   scale=-1.0, accum_out=sums[:, qi % 2, 1 + br, h:h + 1]).then_inc(exp_done, 1)
                v = u - 2
                if 0 <= v < UNITS and v % 2 == 1:
                    n = P * (unit(v)[3] + 1)
                    act.wait_ge(turned, v + 1)
                    if v >= 3:
                        act.wait_ge(pv_done, v - 2)
                    act.activation(PTr[v % 3][:, 0:n], bank[3][:, 0:n], ACT.Copy).then_inc(turned_act, 1)
                if u % 16 == O_STEP and u > 16 or u == UNITS + 2:
                    o_hi(act, (u // 16) - 1)
            act.dma_start(memF[:, :, :], I["mem"][0].rearrange("(a p) n -> p a n", p=P)).then_inc(mem_landed, 16)
            for stage in ("nsa", "wout"):
                b0 = BLOCKS[stage]
                if stage == "wout":
                    for j in range(4):
                        act.wait_ge(mem_turned, j + 1)
                        act.activation(memHi[:, 2 * j:2 * j + 2, :], bank[2 + j][:, :].rearrange(
                            "p (k n) -> p k n", k=2), ACT.Copy).then_inc(memhi_ready, 1)
                with act.Fori(0, 4) as i:
                    for s in range(2):
                        splits_ahead(b0, s, i)
                        if stage == "nsa":
                            act.wait_ge(mf_ready, i * 2 + (s + 1))
                            act.activation(mHi[:, i * 2 + s, :], mF[s][:, :], ACT.Copy).then_inc(mhi_ready, 1)
            squares(act, 1, xc)
            b0 = BLOCKS["xk"]
            with act.Fori(0, 4) as i:
                for s in range(2):
                    splits_ahead(b0, s, i)
            act.wait_ge(var_ready, 1)
            act.activation(rstd[:, :], rstd[:, :], ACT.Sqrt).then_inc(sd_ready, 1)
            for b in range(8):
                split(BLOCKS["xv"] + b + 1, (b + 1) % 2)
                affine(act, 1, b, xc, 16)
            b0 = BLOCKS["xq"]
            with act.Fori(0, 4) as i:
                for s in range(2):
                    splits_ahead(b0, s, i)
            for n in range(4 * XH):
                h, qi = n // 4, n % 4
                act.wait_ge(xmax_ready, n + 1)
                if n >= 2:
                    act.wait_ge(xt_done, n - 1)
                act.activation(xP[n % 2][:, :], bank[2 + n % 2][:, 0:MEM], ACT.Exp, bias=xmax[:, n % 4:n % 4 + 1],
                               accum_out=xsum[:, n % 4:n % 4 + 1]).then_inc(xexp_done, 1)
                if qi == 1 and h >= 1:
                    xo_hi(act, h - 1)
            xo_hi(act, XH - 1)
            b0 = BLOCKS["xo"]
            with act.Fori(0, 4) as i:
                for s in range(2):
                    splits_ahead(b0, s, i)
            squares(act, 2, xc)
            act.wait_ge(var_ready, 2)
            act.activation(rstd[:, :], rstd[:, :], ACT.Sqrt).then_inc(sd_ready, 1)
            for m in range(KT):
                affine(act, 2, m, xc, 32)
            b0 = BLOCKS["fin"]
            with act.Fori(0, KF // 2) as i:
                for t in range(2):
                    for s in range(2):
                        split(i * 4 + (b0 + 2 * t + s + 1), (s + 1) % 2, i * 2 + (b0 // 2 + t + s))
                    act.wait_ge(w_used, i * 4 + (b0 + 2 * t + 1))
                    act.wait_ge(sf_ready, i * 2 + (t + 1))
                    act.activation(sg[t][:, :], bank[2 * t][:, :], ACT.Silu).then_inc(sg_ready, 1)
                    act.wait_ge(sf_ready, i * 2 + (t + 3))
                    act.activation(sHi[:, i * 2 + t, :], sF[t][:, :], ACT.Copy).then_inc(shi_ready, 1)
            b0 = BLOCKS["fout"]
            for s in range(2):
                splits_ahead(b0, s, 0)
            with act.Fori(1, KF // 2 - 1) as i:
                for s in range(2):
                    splits_ahead(b0, s, i)
            split(NBLOCKS - 1, 1)
            squares(act, 3, xc3)
            act.wait_ge(var_ready, 3)
            act.activation(rstd3[:, :], rstd3[:, :], ACT.Sqrt).then_inc(sd_ready, 1)
            for m in range(KT):
                affine(act, 3, m, xc3, 48)
            for tt in range(4):
                act.wait_ge(out_turned, 2 * tt + 1)
                act.activation(otok[tt][:, 0:512], bank[2 * (tt % 2)][:, :], ACT.Copy).then_inc(out_copied_a, 1)

        @block.gpsimd
        def _(pool):
            steps = [0]

            def link(ins):
                steps[0] += 1
                ins.then_inc(pool_step, 1)
                pool.wait_ge(pool_step, steps[0])

            link(pool.memset(ident[:, :], 0.0))
            pool.affine_select(out=ident[:, :], in_=ident[:, :], compare_op=ALU.not_equal, fill=1.0, base=0,
                               pattern=[[-1, P]], channel_multiplier=1).then_inc(ident_ready, 1)
            pool.memset(mean_w[:, :], 1.0 / D).then_inc(pool_const, 1)
            link(pool.iota(cdist[:, :, :], [[-P, 4], [16, 32]], base=31, channel_multiplier=-1,
                           allow_small_or_imprecise_dtypes=True))
            link(pool.affine_select(out=cdist[:, :, :], in_=cdist[:, :, :], compare_op=ALU.is_ge, fill=MASKED, base=-31,
                                    pattern=[[P, 4], [-16, 32]], channel_multiplier=1))
            for h in range(NH):
                link(pool.memset(slope_row[:, h:h + 1], SLOPES[h]))
            pool.wait_ge(lt_ready, 1)
            pool.wait_ge(ct_ready, 2)
            lam = [LT[:, 1, ri].rearrange("p j g -> p g j")[:, :, :, None].to_broadcast([P, NGP, 8, GC]) for ri in range(2)]
            cc = [Ct[:, ri][:, :, None, :].to_broadcast([P, NGP, 8, GC]) for ri in range(2)]
            link(pool.tensor_tensor(Ost[:, 0], cc[0], lam[0], ALU.mult))
            link(pool.tensor_tensor(Otmp[:, :, :, :], cc[1], lam[1], ALU.mult))
            link(pool.tensor_tensor(Ost[:, 0], Ost[:, 0], Otmp[:, :, :, :], ALU.subtract))
            link(pool.tensor_tensor(Ost[:, 1], cc[0], lam[1], ALU.mult))
            link(pool.tensor_tensor(Otmp[:, :, :, :], cc[1], lam[0], ALU.mult))
            link(pool.tensor_tensor(Ost[:, 1], Ost[:, 1], Otmp[:, :, :, :], ALU.add))
            pool.tensor_scalar(Ost[:, 1], Ost[:, 1], -1.0, None, ALU.mult).then_inc(o_ready, 1)

            def lo(b, s):
                pool.wait_ge(w_hi_ready, b + 1)
                pool.tensor_tensor(wlo[s][:, :], wraw[s][:, :], whi[s][:, :].bitcast(F32), ALU.subtract).then_inc(
                    w_lo_ready, 1)

            def h_lo(m, count):
                pool.wait_ge(hhi_ready, count + m + 1)
                pool.tensor_tensor(hLo[:, m, :], hF[:, m, :], hHi[:, m, :].bitcast(F32), ALU.subtract).then_inc(
                    hlo_ready, 1)

            lo(0, 0)
            for k in range(KT):
                h_lo(k, 0)
            lo(1, 1)
            with pool.Fori(1, BLOCKS["nsa"] // 2) as i:
                for s in range(2):
                    lo(i * 2 + s, s)
            pool.wait_ge(hid_done, 4)
            link(pool.iota(Dh[:, NH - 1, :], [[1, T]], base=P - T, channel_multiplier=-1,
                           allow_small_or_imprecise_dtypes=True))
            pool.affine_select(out=Dh[:, NH - 1, :], in_=Dh[:, NH - 1, :], compare_op=ALU.is_ge, fill=MASKED, base=T - P,
                               pattern=[[-1, T]], channel_multiplier=1).then_inc(dist_ready, 1)
            pool.wait_ge(kc_ready, 1)
            pool.wait_ge(vc_ready, 1)
            for qi in range(4):
                if qi >= 1:
                    pool.wait_ge(tc_ready, qi)
                pool.tensor_tensor(Dc[:, :, :], cdist[:, qi, None, :].to_broadcast([P, NH, 32]),
                                   slope_row[:, :, None].to_broadcast([P, NH, 32]), ALU.mult).then_inc(dc_ready, 1)
            with pool.Fori(BLOCKS["nsa"] // 2, (BLOCKS["xv"]) // 2) as i:
                for s in range(2):
                    lo(i * 2 + s, s)
            b = BLOCKS["xv"]
            lo(b, 0)
            for m in range(KT):
                if m < KT - 1:
                    lo(b + m + 1, (m + 1) % 2)
                h_lo(m, 8)
            with pool.Fori(BLOCKS["xq"] // 2, BLOCKS["fin"] // 2) as i:
                for s in range(2):
                    lo(i * 2 + s, s)
            lo(BLOCKS["fin"], 0)
            for m in range(KT):
                h_lo(m, 16)
            lo(BLOCKS["fin"] + 1, 1)
            with pool.Fori(BLOCKS["fin"] // 2 + 1, NBLOCKS // 2) as i:
                for s in range(2):
                    lo(i * 2 + s, s)

        @block.vector
        def _(dve):
            steps = [0]

            def link(ins):
                steps[0] += 1
                ins.then_inc(dve_step, 1)
                dve.wait_ge(dve_step, steps[0])

            def tt(o, a, b, op):
                return dve.tensor_tensor(o, a, b, op)

            dve.memset(nmax[:, :], 0.0).then_inc(tile_act, 2)
            dve.memset(cmax[:, :], 0.0).then_inc(tile_dve, 2)
            dve.memset(xmax[:, :], 0.0).then_inc(sf_ready, 2)
            dve.wait_ge(ident_ready, 1)
            dve.tensor_copy(rep16[:, :, :], ident[0:GC, None, 0:GC].to_broadcast([GC, 8, GC])).then_inc(rep_ready, 1)

            v = {n: t[:, :] for n, t in sp.items()}
            dve.wait_ge(par_landed, 48)
            link(dve.tensor_scalar(v["are"], v["are"], -1e-4, None, ALU.min))
            dve.wait_ge(dt_ready, 1)
            dtb = dtt[:, :, None].to_broadcast([NGP, 2, NS])

            def by_q(x):
                return x.rearrange("p (q n) -> p q n", q=2)

            tt(by_q(v["er"]), by_q(v["are"]), dtb, ALU.mult).then_inc(er_ready, 1)
            link(tt(by_q(v["th"]), by_q(v["aim"]), dtb, ALU.mult))
            link(dve.tensor_scalar(v["k"], v["th"], 1.0 / TWO_PI, ROUND, ALU.mult, ALU.add))
            link(dve.tensor_scalar(v["k"], v["k"], -ROUND, None, ALU.add))
            for part in (PI_A, PI_B, PI_C):
                link(dve.scalar_tensor_tensor(out=v["th"], in0=v["k"], scalar=-part, in1=v["th"], op0=ALU.mult, op1=ALU.add))
            dve.tensor_scalar(v["th"], v["th"], 3.1415925, -3.1415925, ALU.min, ALU.max).then_inc(angle_ready, 1)
            dve.wait_ge(sin_ready, 2)
            dve.wait_ge(mag_ready, 1)
            link(tt(v["s2"], v["s2"], v["s2"], ALU.mult))
            link(dve.tensor_scalar(v["s2"], v["s2"], -2.0, 1.0, ALU.mult, ALU.add))
            tt(LP[:, 0, 0, :], v["er"], v["s2"], ALU.mult)
            tt(v["den"], v["are"], v["are"], ALU.mult)
            tt(v["k"], v["aim"], v["aim"], ALU.mult)
            link(tt(LP[:, 1, 0, :], v["er"], v["s"], ALU.mult))
            link(tt(v["den"], v["den"], v["k"], ALU.add))
            dve.tensor_scalar(v["nr"], LP[:, 0, 0, :], -1.0, None, ALU.add)
            link(dve.reciprocal(v["den"], v["den"]))
            tt(v["a"], v["nr"], v["are"], ALU.mult)
            tt(v["b"], LP[:, 1, 0, :], v["aim"], ALU.mult)
            tt(v["c"], LP[:, 1, 0, :], v["are"], ALU.mult)
            link(tt(v["d"], v["nr"], v["aim"], ALU.mult))
            tt(v["fr"], v["a"], v["b"], ALU.add)
            link(tt(v["fi"], v["c"], v["d"], ALU.subtract))
            tt(FP[:, 0, 0, :], v["fr"], v["den"], ALU.mult)
            link(tt(FP[:, 1, 0, :], v["fi"], v["den"], ALU.mult))

            def cmul(dst, d0, n, a, a0, b, b0):
                x = [a[:, ri, a0:a0 + n, :] for ri in range(2)]
                y = [b[:, ri, b0:b0 + 1, :].to_broadcast([NGP, n, P]) for ri in range(2)]
                tt(cm[0][:, 0:n, :], x[0], y[0], ALU.mult)
                tt(cm[1][:, 0:n, :], x[1], y[1], ALU.mult)
                tt(cm[2][:, 0:n, :], x[0], y[1], ALU.mult)
                link(tt(cm[3][:, 0:n, :], x[1], y[0], ALU.mult))
                tt(dst[:, 0, d0:d0 + n, :], cm[0][:, 0:n, :], cm[1][:, 0:n, :], ALU.subtract)
                link(tt(dst[:, 1, d0:d0 + n, :], cm[2][:, 0:n, :], cm[3][:, 0:n, :], ALU.add))

            cmul(LP, 1, 1, LP, 0, LP, 0)
            cmul(LP, 2, 2, LP, 0, LP, 1)
            cmul(LP, 4, 4, LP, 0, LP, 3)
            cmul(FP, 1, 4, LP, 0, FP, 0)
            cmul(FP, 5, 3, LP, 4, FP, 0)
            link(dve.tensor_copy(EP[:, :, 0, :], LP[:, :, 7, :]))
            cmul(EP, 1, 1, EP, 0, EP, 0)
            cmul(EP, 2, 2, EP, 0, EP, 1)
            cmul(EP, 4, 4, EP, 0, EP, 3)
            dve.memset(sums[:, :, :, :], 0.0).then_inc(powers_ready, 1)

            dve.wait_ge(x_landed, 16)
            for a in range(4):
                for half in range(2):
                    last = dve.bn_stats(bnst[:, a, half, :], xtok[:, a, 512 * half:512 * half + 512])
            link(last)
            for a in range(4):
                last = dve.bn_aggr(bnmv[:, a, :], bnst[:, a, :, :])
            link(last)
            dve.tensor_scalar(rinv[:, :], bnmv[:, :, 1], EPS, None, ALU.add).then_inc(var0_ready, 1)
            dve.wait_ge(sd0_ready, 1)
            link(dve.reciprocal(rinv[:, :], rinv[:, :]))
            for a in range(4):
                dve.tensor_scalar(xtok[:, a, :], xtok[:, a, :], bnmv[:, a, 0:1], rinv[:, a:a + 1],
                                  ALU.subtract, ALU.mult).then_inc(xn_ready, 1)
            dve.wait_ge(vec_turned, 1)
            dve.tensor_copy(dT[:, :], bank[7][0:GC, 128:128 + NG])
            dve.tensor_copy(posT[:, :, :], bank[7][:, 160:192].rearrange("p (z r) -> p z r", z=2))
            dve.tensor_copy(vecT[:, :], bank[7][:, 0:72]).then_inc(vec_ready, 1)
            dve.wait_ge(vec_ready, 1)
            for k in range(KT):
                dve.wait_ge(h0_turned, k + 1)
                dve.tensor_scalar(hF[:, k, :], bank[k % 2][:, :], vecT[:, k:k + 1], vecT[:, 8 + k:9 + k],
                                  ALU.mult, ALU.add).then_inc(hf0_ready, 1)

            dve.wait_ge(dcol_done, 1)
            dve.tensor_copy(Dcol[:, :], bank[6][:, 0:NG])
            dve.wait_ge(lt_turned, 1)
            dve.tensor_copy(LT[:, :, :, :, :].rearrange("p a r s g -> p (a r s g)"), bank[2][:, :])
            dve.tensor_copy(ET[:, :, :, :].rearrange("p r s g -> p (r s g)"), bank[3][:, 0:256]).then_inc(lt_ready, 1)
            for ri in range(2):
                dve.wait_ge(ct_turned, ri + 1)
                for q in range(2):
                    last = dve.tensor_copy(Ct[64 * q:64 * q + 64, ri, :, :], bank[4 + ri][:, :].rearrange(
                        "p (g q c) -> p q g c", q=2, c=GC)[64 * q:64 * q + 64, q])
                last.then_inc(ct_ready, 1)
            dve.wait_ge(ct_ready, 2)
            dve.wait_ge(lt_ready, 1)
            link(dve.memset(Cbd[:, :, :, :, :], 0.0))
            for q in range(2):
                rows_q = slice(64 * q, 64 * q + 64)
                dve.tensor_copy(Cbd[rows_q, 0, :, q, :], Ct[rows_q, 0, :, :])
                last = dve.tensor_scalar(Cbd[rows_q, 1, :, q, :], Ct[rows_q, 1, :, :], -1.0, None, ALU.mult)
            last.then_inc(cbd_ready, 1)
            dve.wait_ge(b_landed, 32)
            dve.memset(Pw[:, 0, :, 8:15, :], 0.0)
            dve.memset(Pw[:, 1, :, 8:15, :], 0.0)
            f = [LT[:, 0, ri].rearrange("p s g -> p g s")[:, :, :, None].to_broadcast([P, NGP, 8, GC]) for ri in range(2)]
            bb = [Bt[:, ri][:, :, None, :].to_broadcast([P, NGP, 8, GC]) for ri in range(2)]
            for ri, (x, y, op) in enumerate(((0, 1, ALU.subtract), (1, 0, ALU.add))):
                dst = Pw[:, ri, :, 0:8, :]
                tt(dst, bb[x], f[0], ALU.mult)
                link(tt(Ptmp[:, :, :, :], bb[y], f[1], ALU.mult))
                link(tt(dst, dst, Ptmp[:, :, :, :], op))
            dve.memset(nmax[:, :], 0.0).then_inc(pw_ready, 1)
            for q in range(8):
                dve.wait_ge(m_built, q + 1)
                for e in range(4):
                    last = dve.scalar_tensor_tensor(out=Mst[:, 4 * q + e, :], in0=ident[:, :],
                                                    scalar=Dcol[:, 4 * q + e:4 * q + e + 1],
                                                    in1=bank[6 + q % 2][:, P * e:P * e + P], op0=ALU.mult, op1=ALU.add)
                last.then_inc(m_ready, 1)
            dve.wait_ge(o_ready, 1)
            for j in range(8):
                dve.wait_ge(wst_turned, j + 1)
                dve.tensor_copy(Wst[:, j // 4, 4 * (j % 4):4 * (j % 4) + 4, :], bank[4 + j % 2][:, :].rearrange(
                    "p (g n) -> p g n", g=4)).then_inc(wst_ready, 1)
            dve.wait_ge(w_used, 4)
            for r in range(4):
                last = dve.tensor_copy(U1[:, :, r, :], bank[2 + r][:, :].rearrange("p (g c) -> p g c", g=NG))
            last.then_inc(u1_ready, 1)
            for j in range(4):
                dve.wait_ge(ut_turned, j + 1)
                dve.tensor_copy(UT[:, 8 * j:8 * j + 8, :], bank[2 + j][:, :].rearrange("p (g n) -> p g n", g=8)).then_inc(
                    ut_ready, 1)
            dve.memset(H[:, :, :, 0:1], 0.0)
            for j in range(4):
                dve.wait_ge(s_done, j + 1)
                last = dve.tensor_copy(H[:, j // 2, 8 * (j % 2):8 * (j % 2) + 8, 1:NCH + 1], bank[2 + j][:, :].rearrange(
                    "p (g n) -> p g n", g=8))
                last.then_inc(h_loaded, 1)
            dve.wait_ge(h_loaded, 4)

            def advance(c1, c0, n, e):
                def col(c):
                    return H[:, :, :, c:c + 8 * (n - 1) + 1:8]

                cur, prev = col(c1), col(c0)
                er = ET[:, 0, e, :][:, None, :, None].to_broadcast([P, 2, NGP, n])
                ei = ET[:, 1, e, :][:, :, None].to_broadcast([P, NGP, n])
                tt(st1[:, :, :, 0:n], prev, er, ALU.mult)
                tt(st2[:, 0, :, 0:n], prev[:, 1], ei, ALU.mult)
                link(tt(st2[:, 1, :, 0:n], prev[:, 0], ei, ALU.mult))
                link(tt(cur, cur, st1[:, :, :, 0:n], ALU.add))
                tt(cur[:, 0], cur[:, 0], st2[:, 0, :, 0:n], ALU.subtract)
                link(tt(cur[:, 1], cur[:, 1], st2[:, 1, :, 0:n], ALU.add))

            for i in range(1, 8):
                advance(1 + i, i, 8, 0)
            for s in range(1, 8):
                advance(8 * s + 8, 8 * s, 1, 7)
            for i in range(7):
                advance(9 + i, 8, 7, i)
            dve.memset(nmax[:, :], 0.0).then_inc(scan_done, 1)
            for q in range(4):
                dve.wait_ge(y_done, q + 1)
                dst = Yt[:, :, P * q:P * q + P].rearrange("p j (g e c) -> p e g j c", g=4, e=2)
                for e in range(2):
                    dve.tensor_copy(dst[:, e], bank[2 + 2 * (q % 2) + e][0:64, :].rearrange(
                        "p (g j c) -> p g j c", g=4, j=8)).then_inc(y_ready, 1)
            for ct in range(4):
                dve.wait_ge(ghi_ready, ct + 1)
                tt(gLo[:, ct, :], gF[:, ct, :], gHi[:, ct, :].bitcast(F32), ALU.subtract).then_inc(glo_ready, 1)
            for m in range(4):
                dve.wait_ge(glu_sig, m + 1)
                tt(yF[:, m, :], yF[:, m, :], gF[:, m, :], ALU.mult).then_inc(yf_ready, 1)
            for m in range(4):
                dve.wait_ge(yhi_ready, m + 1)
                tt(yLo[:, m, :], yF[:, m, :], yHi[:, m, :].bitcast(F32), ALU.subtract).then_inc(ylo_ready, 1)
            dve.wait_ge(tile_act, TA["gmix"] + 16)
            for t in range(KT):
                if t % 2:
                    dve.wait_ge(w_used, BLOCKS["sso"] + t // 2 + 1)
                else:
                    dve.wait_ge(sso_tile, t // 2 + 1)
                gv = G[:, t, :].rearrange("p (c j) -> p j c", j=CH)
                tt(gv, gv, bank[t % 2][:, :].rearrange("p (j c) -> p j c", j=CH), ALU.mult).then_inc(tile_dve, 1)
            dve.wait_ge(w_used, BLOCKS["v"] + 4)
            for a in range(4):
                dve.tensor_copy(VA[:, a, :], bank[2 + a][:, :]).then_inc(v_ready, 1)
            b0 = BLOCKS["kq"]
            for first, scale in ((0, HD ** -0.5), (4, 1.0)):
                with dve.Fori(first, first + 4) as i:
                    for s in range(2):
                        dve.wait_ge(w_used, i * 2 + (b0 + s + 1))
                        dve.tensor_scalar(kqT[:, i * 2 + s, :], bank[s][:, :], scale, None, ALU.mult).then_inc(tile_dve, 1)
            link(dve.memset(hidK[:, :, :, :], 0.0))
            dve.wait_ge(pos_done, 1)
            tt(hidb[:, :], bank[7][:, 0:4], vecT[:, 68:72], ALU.add).then_inc(hidb_ready, 1)
            dve.wait_ge(gate_done, 1)
            dve.wait_ge(hid_done, 2)
            dve.memset(hidV[:, :, :, :, NCMP:32], 0.0).then_inc(hid_padded, 1)
            dve.memset(kcT[:, :, :, :], 0.0)
            link(dve.memset(Vbd[:, :, :, :], 0.0))
            dve.wait_ge(kc_done, 1)
            for e in range(2):
                last = dve.tensor_copy(kcT[64 * e:64 * e + 64, :, e, :], bank[6][64 * e:64 * e + 64, 0:P].rearrange(
                    "p (a e n) -> p a e n", a=2, e=2)[:, :, e, :])
            last.then_inc(kc_ready, 1)
            dve.wait_ge(vc_done, 1)
            for g in range(4):
                last = dve.tensor_copy(Vbd[32 * g:32 * g + 32, :, g, :], bank[7][32 * g:32 * g + 32, 0:256].rearrange(
                    "p (h d) -> p h d", h=NKV))
            last.then_inc(vc_ready, 1)
            dve.wait_ge(dist_ready, 1)
            for h in range(NH):
                last = dve.tensor_scalar(Dh[:, h, :], Dh[:, NH - 1, :], SLOPES[h], None, ALU.mult)
            last.then_inc(dh_ready, 1)
            dve.wait_ge(dh_ready, 1)

            def combine(g):
                qi, h0 = g // 2, 8 * (g % 2)
                dve.wait_ge(pv_done, 16 * (g + 1))
                dve.wait_ge(cpv_done, g + 1)
                if g >= 2:
                    dve.wait_ge(o_turned, g - 1)
                if g == 0:
                    dve.wait_ge(gate_ready, 1)
                link(dve.tensor_scalar(wbr[:, :, :], sums[:, qi % 2, :, h0:h0 + 8], 1e-30, None, ALU.max))
                link(dve.reciprocal(wbr[:, :, :], wbr[:, :, :]))
                link(tt(wbr[:, :, :], wbr[:, :, :], gates[:, qi, 3 * h0:3 * h0 + 24].rearrange("p (h z) -> p z h", z=3),
                        ALU.mult))
                o, tmp = oS[g % 2][:, :, :], otmp[:, :, :]
                for z, bk in ((0, 6), (1, 4), (2, 5)):
                    w = wbr[:, z, :, None].to_broadcast([P, 8, HD])
                    ins = tt(tmp if z else o, bank[bk][:, :].rearrange("p (h d) -> p h d", h=8), w, ALU.mult)
                    if z:
                        link(ins)
                        ins = tt(o, o, tmp, ALU.add)
                    if z < 2:
                        link(ins)
                ins.then_inc(os_ready, 1)

            def o_lo(g):
                dve.wait_ge(ohi_ready, g + 1)
                dst = slice(4 * (g % 2), 4 * (g % 2) + 4), slice(g // 2 * P, (g // 2 + 1) * P)
                tt(hLo[:, dst[0], dst[1]], bank[7][:, :].rearrange("p (k n) -> p k n", k=4),
                   hHi[:, dst[0], dst[1]].bitcast(F32), ALU.subtract).then_inc(olo_ready, 1)

            for u in range(UNITS + 3):
                qi = u // 32
                if u % 32 == 0 and u < UNITS:
                    dve.wait_ge(cscore_done, qi + 1)
                    dve.wait_ge(dc_ready, qi + 1)
                    if qi >= 1:
                        dve.wait_ge(cturned, qi)
                    link(tt(Tc[:, :, :], bank[7][:, :].rearrange("p (h n) -> p h n", h=NH), Dc[:, :, :], ALU.add))
                    link(dve.tensor_reduce(cmax[:, :], Tc[:, :, :], AX.X, ALU.max))
                    link(dve.tensor_scalar(cmax[:, :], cmax[:, :], MAX_FLOOR, None, ALU.max))
                    tt(Tc[:, :, :], Tc[:, :, :], cmax[:, :, None].to_broadcast([P, NH, 32]), ALU.subtract).then_inc(
                        tc_ready, 1)
                if u < UNITS:
                    g, br, h, qi = unit(u)
                    n = P * (qi + 1)
                    dve.wait_ge(score_done, u + 1)
                    if u >= 3:
                        dve.wait_ge(exp_done, u - 2)
                    dve.tensor_tensor_reduce(Tr[u % 3][:, 0:n], Dh[:, h, T - n:T], bank[u % 2][:, 0:n], -1.0, 3e38,
                                             ALU.add, ALU.min, nmax[:, u % 8:u % 8 + 1]).then_inc(max_done, 1)
                if u % 32 == 2 and u < UNITS:
                    qi = u // 32
                    dve.wait_ge(pc_ready, qi + 1)
                    dve.tensor_reduce(sums[:, qi % 2, 0, :], Tc[:, :, :], AX.X, ALU.add).then_inc(csum_ready, 1)
                if u % 32 == 4 and u < UNITS:
                    qi = u // 32
                    dve.wait_ge(cturned, qi + 1)
                    if qi >= 1:
                        dve.wait_ge(cpv_done, 2 * qi)
                    dve.tensor_copy(PTc[:, :, :], bank[7][:, :].rearrange("p (h n) -> p h n", h=NKV)).then_inc(ptc_ready, 1)
                w = u - 2
                if 0 <= w < UNITS and w % 2 == 0:
                    n = P * (unit(w)[3] + 1)
                    dve.wait_ge(turned, w + 1)
                    if w >= 3:
                        dve.wait_ge(pv_done, w - 2)
                    dve.tensor_copy(PTr[w % 3][:, 0:n], bank[2][:, 0:n]).then_inc(turned_dve, 1)
                if u % 16 == COMBINE and u > 16:
                    combine(u // 16 - 1)
                if u % 16 == O_STEP and u > 16:
                    o_lo(u // 16 - 1)
            combine(7)
            o_lo(7)

            b0 = BLOCKS["nsa"]
            with dve.Fori(0, 4) as i:
                for s in range(2):
                    dve.wait_ge(w_used, i * 2 + (b0 + s + 1))
                    tt(mF[s][:, :], bank[s][:, :], G[:, i * 2 + (s + KT), :], ALU.mult).then_inc(tile_dve, 1)
                    dve.wait_ge(tile_dve, i * 2 + (TD["nsa"] + s + 1))
                    tt(mF[s][:, :], mF[s][:, :], G[:, i * 2 + s, :], ALU.add).then_inc(mf_ready, 1)
                    dve.wait_ge(mhi_ready, i * 2 + (s + 1))
                    tt(mLo[:, i * 2 + s, :], mF[s][:, :], mHi[:, i * 2 + s, :].bitcast(F32), ALU.subtract).then_inc(
                        mlo_ready, 1)
            for j in range(4):
                dve.wait_ge(memhi_ready, j + 1)
                tt(memLo[:, 2 * j:2 * j + 2, :], bank[2 + j][:, :].rearrange("p (k n) -> p k n", k=2),
                   memHi[:, 2 * j:2 * j + 2, :].bitcast(F32), ALU.subtract).then_inc(memlo_ready, 1)

            def residual(name):
                b0 = BLOCKS[name]
                with dve.Fori(0, 4) as i:
                    for s in range(2):
                        dve.wait_ge(w_used, i * 2 + (b0 + s + 1))
                        dve.scalar_tensor_tensor(out=hF[:, i * 2 + s, :], in0=hF[:, i * 2 + s, :], scalar=ALPHA,
                                                 in1=bank[s][:, :], op0=ALU.mult, op1=ALU.add).then_inc(tile_dve, 1)

            def centre(n, centred):
                dve.wait_ge(mu_ready, n)
                for m in range(KT):
                    tt(centred[:, m, :], hF[:, m, :], bank[6][:, :], ALU.subtract).then_inc(xc_ready, 1)

            def scale(n, centred, rs):
                dve.wait_ge(var_done, n)
                dve.tensor_scalar(rs[:, :], bank[7][:, :], EPS, None, ALU.add).then_inc(var_ready, 1)
                dve.wait_ge(sd_ready, n)
                link(dve.reciprocal(rs[:, :], rs[:, :]))
                for m in range(KT):
                    tt(centred[:, m, :], centred[:, m, :], rs[:, :], ALU.mult).then_inc(nrm_ready, 1)

            residual("wout")
            centre(1, xc)
            b0 = BLOCKS["xk"]
            with dve.Fori(0, 4) as i:
                for s in range(2):
                    dve.wait_ge(w_used, i * 2 + (b0 + s + 1))
                    dve.tensor_copy(kxT[:, i * 2 + s, :], bank[s][:, 0:MEM]).then_inc(tile_dve, 1)
            scale(1, xc, rstd)
            dve.wait_ge(w_used, BLOCKS["xv"] + 8)
            for a in range(2):
                for half in range(2):
                    last = dve.tensor_copy(vx[:, a, 512 * half:512 * half + 512], bank[2 + 2 * a + half][:, :])
            last.then_inc(xv_ready, 1)
            b0 = BLOCKS["xq"]
            with dve.Fori(0, 4) as i:
                for s in range(2):
                    dve.wait_ge(w_used, i * 2 + (b0 + s + 1))
                    dve.tensor_scalar(qx[:, i * 2 + s, :], bank[s][:, :], (D // XH) ** -0.5, None, ALU.mult).then_inc(
                        tile_dve, 1)

            def xo_lo(h):
                for dt in range(2):
                    dve.wait_ge(xohi_ready, 2 * h + dt + 1)
                    tt(mLo[:, 2 * h + dt, :], bank[6 + dt][:, :], mHi[:, 2 * h + dt, :].bitcast(F32),
                       ALU.subtract).then_inc(xolo_ready, 1)

            NX = 4 * XH
            for n in range(NX + 3):
                if n < NX:
                    dve.wait_ge(xs_done, n + 1)
                    dve.tensor_reduce(xmax[:, n % 4:n % 4 + 1], bank[2 + n % 2][:, 0:MEM], AX.X, ALU.max,
                                      negate=True).then_inc(xmax_ready, 1)
                a = n - 1
                if 0 <= a < NX:
                    dve.wait_ge(xexp_done, a + 1)
                    link(dve.reciprocal(rinv[:, a % 4:a % 4 + 1], xsum[:, a % 4:a % 4 + 1]))
                    dve.tensor_scalar(xP[a % 2][:, :], xP[a % 2][:, :], rinv[:, a % 4:a % 4 + 1], None,
                                      ALU.mult).then_inc(xp_ready, 1)
                c = n - 2
                if 0 <= c < NX:
                    h, qi = c // 4, c % 4
                    dve.wait_ge(xt_done, c + 1)
                    if h >= 2:
                        dve.wait_ge(xo_done, 2 * (h - 1))
                    dve.tensor_copy(xPT[h % 2][:, :, P * qi:P * qi + P], bank[4 + c % 2][:, 0:MEM].rearrange(
                        "p (k n) -> p k n", k=2)).then_inc(xpt_ready, 1)
                if n % 4 == 2 and n >= 6:
                    xo_lo(n // 4 - 1)
            residual("xo")
            centre(2, xc)
            scale(2, xc, rstd)

            b0 = BLOCKS["fin"]
            with dve.Fori(0, KF // 2) as i:
                for t in range(2):
                    dve.wait_ge(w_used, i * 4 + (b0 + 2 * t + 2))
                    dve.wait_ge(sg_ready, i * 2 + (t + 1))
                    tt(sF[t][:, :], sg[t][:, :], bank[2 * t + 1][:, :], ALU.mult).then_inc(sf_ready, 1)
                    dve.wait_ge(shi_ready, i * 2 + (t + 1))
                    tt(sLo[:, i * 2 + t, :], sF[t][:, :], sHi[:, i * 2 + t, :].bitcast(F32), ALU.subtract).then_inc(
                        slo_ready, 1)
            dve.wait_ge(fout_done, 1)
            for m in range(KT):
                dve.scalar_tensor_tensor(out=hF[:, m, :], in0=hF[:, m, :], scalar=ALPHA, in1=bank[m][:, :],
                                         op0=ALU.mult, op1=ALU.add).then_inc(tile_dve, 1)
            centre(3, xc3)
            scale(3, xc3, rstd3)
            for a in range(4):
                dve.wait_ge(out_turned, 2 * a + 2)
                dve.tensor_copy(otok[a][:, 512:1024], bank[2 * (a % 2) + 1][:, :]).then_inc(out_copied_d, 1)

        @block.tensor
        def _(pe):
            def mm(o, w, a, start, stop):
                return pe.matmul(o, w, a, start=start, stop=stop)

            def mm3(o, w_hi, w_lo, a_hi, a_lo, start, stop):
                mm(o, w_hi, a_hi, start, False)
                mm(o, w_hi, a_lo, False, False)
                return mm(o, w_lo, a_hi, False, stop)

            def tile_stage(name, a_hi, a_lo, freed, base, n=T):
                b0 = BLOCKS[name]
                count = {"kq": 16, "gmix": 16}.get(name, 8)
                with pe.Fori(0, count // 2) as i:
                    for s in range(2):
                        pe.wait_ge(w_lo_ready, i * 2 + (b0 + s + 1))
                        pe.wait_ge(freed, i * 2 + (base + s - 1))
                        for k in range(KT):
                            w = slice(P * k, P * k + P)
                            last = mm3(bank[s][:, 0:n], whi[s][:, w], wlo[s][:, w], a_hi[:, k, :], a_lo[:, k, :],
                                       k == 0, k == KT - 1)
                        last.then_inc(w_used, 1)

            pe.wait_ge(ident_ready, 1)
            pe.wait_ge(vec_landed, 16 * 12)
            pe.transpose(bank[7][:, 0:72], vrows[:, :], ident[0:72, 0:72])
            pe.transpose(bank[7][0:GC, 128:128 + NG], dl[:, :], ident[0:NG, 0:NG])
            for z in range(2):
                last = pe.transpose(bank[7][:, 160 + 16 * z:176 + 16 * z], posl[:, z, :], ident[0:16, 0:16])
            last.then_inc(vec_turned, 1)
            pe.wait_ge(xn_ready, 4)
            for k in range(KT):
                if k >= 2:
                    pe.wait_ge(hf0_ready, k - 1)
                for a in range(4):
                    last = pe.transpose(bank[k % 2][:, P * a:P * a + P], xtok[:, a, P * k:P * k + P], ident[:, :])
                last.then_inc(h0_turned, 1)
            pe.wait_ge(vec_ready, 1)
            pe.wait_ge(rep_ready, 1)
            mm(bank[6][:, 0:NG], rep16[:, :, :].rearrange("p j c -> p (j c)"), dT[:, :], True, True).then_inc(dcol_done, 1)
            pe.wait_ge(powers_ready, 1)
            for ri in range(2):
                for s in range(8):
                    c = P * ri + NGP * s
                    pe.transpose(bank[2][:, c:c + NGP], FP[:, ri, 7 - s, :], ident[0:NGP, 0:NGP])
                    pe.transpose(bank[2][:, 256 + c:256 + c + NGP], LP[:, ri, s, :], ident[0:NGP, 0:NGP])
                    last = pe.transpose(bank[3][:, c:c + NGP], EP[:, ri, s, :], ident[0:NGP, 0:NGP])
            last.then_inc(lt_turned, 1)
            pe.wait_ge(c_landed, 64)
            for ri in range(2):
                for t in range(4):
                    last = pe.transpose(bank[4 + ri][:, P * t:P * t + P], Craw[:, ri, t, :, :].rearrange("p d n -> p (d n)"),
                                        ident[:, :])
                last.then_inc(ct_turned, 1)
            pe.wait_ge(pw_ready, 1)
            pe.wait_ge(cbd_ready, 1)
            for q in range(8):
                if q >= 2:
                    pe.wait_ge(m_ready, q - 1)
                for gl in range(2):
                    gp = 2 * q + gl
                    o = bank[6 + q % 2][:, 256 * gl:256 * gl + 256].rearrange("p (q j c) -> p q j c", q=2, j=8)
                    for j in range(8):
                        for ri in range(2):
                            window = Pw[:, ri, gp, 7 - j:15 - j, :].rearrange("p j c -> p (j c)")
                            last = mm(o[:, :, j, :], window, Cbd[:, ri, gp, :, :], ri == 0, ri == 1)
                last.then_inc(m_built, 1)
            for j in range(8):
                if j >= 2:
                    pe.wait_ge(wst_ready, j - 1)
                for e in range(4):
                    src = Pw[:, j // 4, 4 * (j % 4) + e, 0:8, :].rearrange("p j c -> p (j c)")
                    last = pe.transpose(bank[4 + j % 2][:, P * e:P * e + P], src, ident[:, :])
                last.then_inc(wst_turned, 1)
            pe.wait_ge(wst_ready, 8)
            pe.wait_ge(hlo_ready, KT)
            for b in range(4):
                s = b % 2
                pe.wait_ge(w_lo_ready, b + 1)
                for kk in range(2):
                    k = 2 * b + kk
                    w = slice(512 * kk, 512 * kk + 512)
                    for r in range(4):
                        a_hi, a_lo = hHi[:, k, r:T:4], hLo[:, k, r:T:4]
                        last = mm3(bank[2 + r][:, :], a_hi, a_lo, whi[s][:, w], wlo[s][:, w], k == 0, k == KT - 1)
                last.then_inc(w_used, 1)
            pe.wait_ge(u1_moved, 32)
            for j in range(4):
                for g in range(8 * j, 8 * j + 8):
                    last = pe.transpose(bank[2 + j][:, NCH * (g % 8):NCH * (g % 8) + NCH], U8[:, g, :, :].rearrange("p j c -> p (j c)"),
                                        ident[0:NCH, 0:NCH])
                last.then_inc(ut_turned, 1)
            pe.wait_ge(ut_ready, 4)
            for j in range(4):
                for gp in range(8 * (j % 2), 8 * (j % 2) + 8):
                    for q in range(2):
                        last = mm(bank[2 + j][64 * q:64 * q + 64, NCH * (gp % 8):NCH * (gp % 8) + NCH],
                                  Wst[:, j // 2, gp, 64 * q:64 * q + 64], UT[:, 2 * gp + q, :], True, True)
                last.then_inc(s_done, 1)
            tile_stage("gmix", hHi, hLo, tile_act, TA["gmix"])
            pe.wait_ge(scan_done, 1)
            pe.wait_ge(m_ready, 8)
            for q in range(4):
                if q >= 2:
                    pe.wait_ge(y_ready, 2 * (q - 1))
                for e in range(8):
                    g = 8 * q + e
                    gp, half = g // 2, slice(64 * (g % 2), 64 * (g % 2) + 64)
                    o = bank[2 + 2 * (q % 2) + e % 2][0:64, P * (e // 2):P * (e // 2) + P]
                    mm(o, UT[:, g, :], Mst[:, g, :], True, False)
                    for ri in range(2):
                        last = mm(o, H[half, ri, gp, 0:NCH], Ost[half, ri, gp].rearrange("p j c -> p (j c)"),
                                  False, ri == 1)
                last.then_inc(y_done, 1)
            pe.wait_ge(y_ready, 8)
            for ct in range(4):
                for j in range(8):
                    last = pe.transpose(bank[2 + ct][:, NCH * j:NCH * j + NCH], Yt[:, j, P * ct:P * ct + P],
                                        ident[0:NCH, 0:NCH])
                last.then_inc(yt_turned, 1)
            pe.wait_ge(glo_ready, 4)
            for b in range(2):
                pe.wait_ge(w_lo_ready, BLOCKS["glu"] + b + 1)
                for kk in range(2):
                    for m in range(4):
                        w = slice(512 * kk + P * m, 512 * kk + P * m + P)
                        k = 2 * b + kk
                        last = mm3(bank[2 + m][:, :], whi[b][:, w], wlo[b][:, w], gHi[:, k, :], gLo[:, k, :],
                                   k == 0, k == 3)
                last.then_inc(w_used, 1)
            pe.wait_ge(ylo_ready, 4)
            pe.wait_ge(tile_act, TA["gmix"] + 16)
            for t in range(KT):
                b = BLOCKS["sso"] + t // 2
                s = b % 2
                pe.wait_ge(w_lo_ready, b + 1)
                if t >= 2:
                    pe.wait_ge(tile_dve, TD["sso"] + t - 1)
                for k in range(4):
                    w = slice(256 * k + P * (t % 2), 256 * k + P * (t % 2) + P)
                    last = mm3(bank[t % 2][:, :], whi[s][:, w], wlo[s][:, w], yHi[:, k, :], yLo[:, k, :], k == 0, k == 3)
                last.then_inc(w_used if t % 2 else sso_tile, 1)
            for b in range(4):
                s = (BLOCKS["v"] + b) % 2
                pe.wait_ge(w_lo_ready, BLOCKS["v"] + b + 1)
                for kk in range(2):
                    k = 2 * b + kk
                    w = slice(512 * kk, 512 * kk + 512)
                    for a in range(4):
                        tok = slice(P * a, P * a + P)
                        last = mm3(bank[2 + a][:, :], hHi[:, k, tok], hLo[:, k, tok], whi[s][:, w], wlo[s][:, w],
                                   k == 0, k == KT - 1)
                last.then_inc(w_used, 1)
            tile_stage("kq", hHi, hLo, tile_dve, TD["kq"])
            pe.wait_ge(w1_landed, 6 * 16)
            for a in range(4):
                for k in range(KT):
                    last = mm(bank[6][:, 48 * a:48 * a + 48], hF[:, k, P * a:P * a + P], wg[:, k, :], k == 0, k == KT - 1)
            last.then_inc(gate_done, 1)
            for j in range(4):
                for r in range(16):
                    last = mm(bank[7][:, j:j + 1], w1[:, j // 2, r, P * (j % 2):P * (j % 2) + P],
                              posT[:, j // 2, r:r + 1], r == 0, r == 15)
            last.then_inc(pos_done, 1)
            pe.wait_ge(xc_landed, 64)
            pe.wait_ge(v_ready, 4)
            for j in range(4):
                for r in range(16):
                    last = mm(bank[2 + j][:, 0:NKV * NCMP], w1[:, j // 2, r, P * (j % 2):P * (j % 2) + P],
                              Xc[:, j // 2, :, 2 * r:2 * r + 16 * (NCMP - 1) + 1:16], r == 0, r == 15)
                last.then_inc(hid_done, 1)
            pe.wait_ge(hid_ready, 4)
            pe.wait_ge(hid_padded, 1)
            pe.wait_ge(gate_ready, 1)
            for kk in range(2):
                last = mm(bank[6][:, 0:P], w2[:, 0, kk, :], hidK[:, kk, :, :], kk == 0, kk == 1)
            last.then_inc(kc_done, 1)
            for h in range(NKV):
                for kk in range(2):
                    last = mm(bank[7][:, HD * h:HD * h + HD], hidV[:, kk, h, :, :].rearrange("p g n -> p (g n)"),
                              w2[:, 1, kk, 0:HD], kk == 0, kk == 1)
            last.then_inc(vc_done, 1)

            def turn_output(g):
                pe.wait_ge(os_ready, g + 1)
                if g % 2:
                    pe.wait_ge(ptc_ready, min((g + 1) // 2 + 1, 4))
                if g >= 1:
                    pe.wait_ge(ohi_ready, g)
                    pe.wait_ge(olo_ready, g)
                for i in range(4):
                    last = pe.transpose(bank[7][:, P * i:P * i + P], oS[g % 2][:, 2 * i:2 * i + 2, :].rearrange(
                        "p h d -> p (h d)"), ident[:, :])
                last.then_inc(o_turned, 1)

            def pv(w):
                g, br, h, qi = unit(w)
                pe.wait_ge(turned_act if w % 2 else turned_dve, w // 2 + 1)
                if w % 16 == 0 and g >= 1:
                    pe.wait_ge(os_ready, g)
                c = HD * (h % 8)
                vcol = 256 * br + HD * (h // 4)
                for kt in range(qi + 1):
                    last = mm(bank[4 + br][:, c:c + HD], PTr[w % 3][:, P * kt:P * kt + P], VA[:, kt, vcol:vcol + HD],
                              kt == 0, kt == qi)
                last.then_inc(pv_done, 1)

            pe.wait_ge(kc_ready, 1)
            pe.wait_ge(vc_ready, 1)
            pe.wait_ge(tile_dve, TD["nsa"])
            for u in range(UNITS + 3):
                if u % 32 == 0 and u < UNITS:
                    qi = u // 32
                    if qi >= 1:
                        pe.wait_ge(ohi_ready, 2 * qi - 1)
                        pe.wait_ge(olo_ready, 2 * qi - 1)
                    for m in range(8):
                        h = 8 * (m // 4) + m % 4
                        o = bank[7][:, :].rearrange("p (h n) -> p h n", h=NH)[:, h:h + 5:4, :]
                        last = mm(o, qT[:, m, P * qi:P * qi + P], kcT[:, m // 4, :, :], True, True)
                    last.then_inc(cscore_done, 1)
                if u < UNITS:
                    g, br, h, qi = unit(u)
                    if u >= 2:
                        pe.wait_ge(max_done, u - 1)
                    half = slice(64 * (h // 4 % 2), 64 * (h // 4 % 2) + 64)
                    mm(bank[u % 2][:, 0:P * (qi + 1)], qT[half, 4 * (h // 8) + h % 4, P * qi:P * qi + P],
                       kT[half, 2 * br + h // 8, 0:P * (qi + 1)], True, True).then_inc(score_done, 1)
                if u % 32 == CMP_TURN and u < UNITS:
                    pe.wait_ge(pc_ready, u // 32 + 1)
                    for kv in range(NKV):
                        last = pe.transpose(bank[7][:, P * kv:P * kv + P], Tc[:, 4 * kv:4 * kv + 4, :].rearrange(
                            "p h n -> p (h n)"), ident[:, :])
                    last.then_inc(cturned, 1)
                v = u - 2
                if 0 <= v < UNITS:
                    qi = unit(v)[3]
                    pe.wait_ge(exp_done, v + 1)
                    if v >= 2:
                        pe.wait_ge(turned_act if v % 2 else turned_dve, v // 2)
                    for kt in range(qi + 1):
                        last = pe.transpose(bank[2 + v % 2][:, P * kt:P * kt + P], Pr[v % 3][:, P * kt:P * kt + P],
                                            ident[:, :])
                    last.then_inc(turned, 1)
                w = u - 3
                if 0 <= w < UNITS:
                    pv(w)
                if u % 16 == CMP_PV and u < UNITS:
                    g = u // 16
                    pe.wait_ge(ptc_ready, g // 2 + 1)
                    if g >= 1:
                        pe.wait_ge(os_ready, g)
                    for e in range(2):
                        kv = 2 * (g % 2) + e
                        last = mm(bank[6][:, 256 * e:256 * e + 256], PTc[:, kv, :],
                                  Vbd[:, kv, :, :].rearrange("p g d -> p (g d)"), True, True)
                    last.then_inc(cpv_done, 1)
                if u % 16 == O_STEP and u > 16:
                    turn_output(u // 16 - 1)
            turn_output(7)

            pe.wait_ge(olo_ready, 8)
            tile_stage("nsa", hHi, hLo, tile_dve, TD["nsa"])
            pe.wait_ge(mem_landed, 16)
            for j in range(4):
                for kk in range(2):
                    for a in range(2):
                        c = 256 * kk + P * a
                        last = pe.transpose(bank[2 + j][:, c:c + P], memF[:, a, P * (2 * j + kk):P * (2 * j + kk) + P],
                                            ident[:, :])
                last.then_inc(mem_turned, 1)
            pe.wait_ge(mlo_ready, KT)
            tile_stage("wout", mHi, mLo, tile_dve, TD["wout"])

            def mean(n, residual_tiles):
                pe.wait_ge(pool_const, 1)
                pe.wait_ge(tile_dve, residual_tiles)
                for m in range(KT):
                    last = mm(bank[6][:, :], mean_w[:, :], hF[:, m, :], m == 0, m == KT - 1)
                last.then_inc(mu_ready, 1)

            def variance(n):
                for m in range(KT):
                    pe.wait_ge(sq_ready, KT * (n - 1) + m + 1)
                    last = mm(bank[7][:, :], mean_w[:, :], sq[:, m, :], m == 0, m == KT - 1)
                last.then_inc(var_done, 1)

            mean(1, TD["xk"])
            pe.wait_ge(memlo_ready, 4)
            tile_stage("xk", memHi, memLo, tile_dve, TD["xk"], MEM)
            variance(1)
            for k in range(KT):
                s = k % 2
                pe.wait_ge(w_lo_ready, BLOCKS["xv"] + k + 1)
                for a in range(2):
                    tok = slice(P * a, P * a + P)
                    for half in range(2):
                        w = slice(512 * half, 512 * half + 512)
                        last = mm3(bank[2 + 2 * a + half][:, :], memHi[:, k, tok], memLo[:, k, tok], whi[s][:, w],
                                   wlo[s][:, w], k == 0, k == KT - 1)
                last.then_inc(w_used, 1)
            pe.wait_ge(hlo_ready, 2 * KT)
            tile_stage("xq", hHi, hLo, tile_dve, TD["xq"])
            pe.wait_ge(xv_ready, 1)
            pe.wait_ge(tile_dve, TD["xo"])
            NX = 4 * XH
            for n in range(NX + 3):
                if n < NX:
                    h, qi = n // 4, n % 4
                    if n >= 2:
                        pe.wait_ge(xexp_done, n - 1)
                    for kk in range(2):
                        last = mm(bank[2 + n % 2][:, 0:MEM], qx[:, 2 * h + kk, P * qi:P * qi + P], kxT[:, 2 * h + kk, :],
                                  kk == 0, kk == 1)
                    last.then_inc(xs_done, 1)
                c = n - 2
                if 0 <= c < NX:
                    pe.wait_ge(xp_ready, c + 1)
                    if c >= 2:
                        pe.wait_ge(xpt_ready, c - 1)
                    for kt in range(2):
                        last = pe.transpose(bank[4 + c % 2][:, P * kt:P * kt + P], xP[c % 2][:, P * kt:P * kt + P],
                                            ident[:, :])
                    last.then_inc(xt_done, 1)
                if n % 4 == 2 and n >= 6:
                    h = n // 4 - 1
                    pe.wait_ge(xpt_ready, 4 * h + 4)
                    if h >= 1:
                        pe.wait_ge(xohi_ready, 2 * h)
                        pe.wait_ge(xolo_ready, 2 * h)
                    for dt in range(2):
                        for kt in range(2):
                            c0 = 256 * h + P * dt
                            last = mm(bank[6 + dt][:, :], vx[:, kt, c0:c0 + P], xPT[h % 2][:, kt, :], kt == 0, kt == 1)
                        last.then_inc(xo_done, 1)
            pe.wait_ge(xolo_ready, KT)
            tile_stage("xo", mHi, mLo, tile_dve, TD["xo"])
            mean(2, TD["fout"])
            variance(2)
            pe.wait_ge(hlo_ready, 3 * KT)
            b0 = BLOCKS["fin"]
            with pe.Fori(0, KF // 2) as i:
                for t in range(2):
                    pe.wait_ge(sf_ready, i * 2 + (t + 1))
                    for s in range(2):
                        pe.wait_ge(w_lo_ready, i * 4 + (b0 + 2 * t + s + 1))
                        for k in range(KT):
                            w = slice(P * k, P * k + P)
                            last = mm3(bank[2 * t + s][:, :], whi[s][:, w], wlo[s][:, w], hHi[:, k, :], hLo[:, k, :],
                                       k == 0, k == KT - 1)
                        last.then_inc(w_used, 1)
            pe.wait_ge(slo_ready, KF)
            b0 = BLOCKS["fout"]

            def down(k, s, start, stop, done):
                pe.wait_ge(w_lo_ready, k + (b0 + 1))
                for m in range(KT):
                    w = slice(P * m, P * m + P)
                    last = mm3(bank[m][:, :], whi[s][:, w], wlo[s][:, w], sHi[:, k, :], sLo[:, k, :], start, stop)
                last.then_inc(done, 1)

            for s in range(2):
                down(s, s, s == 0, False, w_used)
            with pe.Fori(1, KF // 2 - 1) as i:
                for s in range(2):
                    down(i * 2 + s, s, False, False, w_used)
            down(KF - 2, 0, False, False, w_used)
            down(KF - 1, 1, False, True, fout_done)
            mean(3, TD_END)
            variance(3)
            pe.wait_ge(hf_ready, 3 * KT)
            for a in range(4):
                for half in range(2):
                    if a >= 2:
                        pe.wait_ge(out_copied_d if half else out_copied_a, a - 1)
                    for kk in range(4):
                        last = pe.transpose(bank[2 * (a % 2) + half][:, P * kk:P * kk + P],
                                            hF[:, 4 * half + kk, P * a:P * a + P], ident[:, :])
                    last.then_inc(out_turned, 1)


_INS = ['x', 'mem', 'ln_emb_g', 'ln_emb_b', 'w_in', 'ssm_a_re', 'ssm_a_im', 'ssm_b_re', 'ssm_b_im', 'ssm_c_re',
        'ssm_c_im', 'ssm_d', 'ssm_log_dt', 'ssm_w_glu', 'ssm_b_glu', 'ssm_w_out', 'cmp_pos', 'cmp_w1', 'cmp_b1',
        'cmp_w2', 'nsa_w_out', 'w_out', 'ln1_g', 'ln1_b', 'xattn_w_q', 'xattn_w_kv', 'xattn_w_o', 'ln2_g', 'ln2_b',
        'ffn_w_in', 'ffn_w_out', 'ln3_g', 'ln3_b']


def kernel(**inputs):
    import numpy as np
    import concourse.bacc as bacc
    from concourse.bass_utils import run_bass_kernel_spmd as run

    nc = bacc.Bacc("TRN2", target_bir_lowering=False, num_devices=1)
    arrays, tensors = {}, {}
    for name in _INS:
        a = np.ascontiguousarray(inputs[name])
        arrays[f"in_{name}"] = a
        tensors[name] = nc.dram_tensor(f"in_{name}", a.shape, mybir.dt.from_np(a.dtype), kind="ExternalInput").ap()
    out = nc.dram_tensor("out_0", (1, T, D), F32, kind="ExternalOutput").ap()
    build(nc, tensors, out)
    r = run(nc, [arrays], core_ids=[0])
    return r.results[0]["out_0"]
```

```python
import math
from contextlib import ExitStack

import concourse.bass as bass
from concourse import mybir

ALU = mybir.AluOpType
ACT = mybir.ActivationFunctionType
AX = mybir.AxisListType
F32 = mybir.dt.float32
F32R = mybir.dt.float32r

P = 128
D = 1024
T = 512
KT = D // P
MEM = 256
NG, GC, NS = 32, 16, 64
NGP = NG // 2
CH = 8
NCH = T // CH
NH, NKV, HD = 16, 4, 64
NCMP = 31
DFF = 2816
KF = DFF // P
XH = 4
ALPHA = 2.0 ** 0.25
EPS = 1e-5
MASKED = -1e30
MAX_FLOOR = -1e25
SLOPES = [2.0 ** (-8.0 * (h + 1) / NH) for h in range(NH)]
TWO_PI = 2 * math.pi
PI_A = 6.28125
PI_B = 0.0019340515136719
PI_C = TWO_PI - PI_A - PI_B
ROUND = 1.5 * 2.0 ** 23

C_U, C_Q, C_KVC, C_KVS, C_KVW, C_GN, C_GM = 0, 512, 1536, 2048, 2560, 3072, 3120

STAGES = [("gmixa", 4), ("u", 4), ("gmixb", 8), ("gmixc", 2), ("glu", 2), ("gmixd", 2), ("sso", 4), ("v", 4), ("kq", 16), ("nsa", 8), ("wout", 8),
          ("xk", 8), ("xv", 8), ("xq", 8), ("xo", 8), ("fin", 2 * KF), ("fout", KF)]
BLOCKS = {}
UNITS = 4 * NH * 2
SCORE_BANKS = (0, 1, 6)
TURN, PV = 5, 7
O_STEP = 8
CMP_SCORE, CMP_EXP, CMP_SUM, CMP_TURN, CMP_COPY = 16, 19, 21, 25, 26


def unit(u):
    return 4 * (u // 16 % 2) + u % 16 // 4, u // 2 % 2, u % 2, u // 32


_at = 0
for _n, _c in STAGES:
    BLOCKS[_n] = _at
    _at += _c
NBLOCKS = _at


def build(nc, I, out):
    KB = 1024
    BASE = 16512
    RG = 72 * KB
    RX = 104 * KB
    RC = 202 * KB

    def at(name, shape, off, dt=F32):
        return nc.alloc_sbuf_tensor_at(name, shape, dt, offset=BASE + int(off))

    wraw = [at(f"wraw{s}", [P, 1024], s * 4 * KB) for s in range(2)]
    whi = [at(f"whi{s}", [P, 1024], (8 + s * 4) * KB, F32R) for s in range(2)]
    wlo = [at(f"wlo{s}", [P, 1024], (16 + s * 4) * KB, F32R) for s in range(2)]
    hF = at("hF", [P, KT, T], 24 * KB)
    hHi = at("hHi", [P, KT, T], 40 * KB, F32R)
    hLo = at("hLo", [P, KT, T], 56 * KB, F32R)
    G = at("G", [P, 2 * KT, T], RG)
    ident = at("ident", [P, P], RC)
    mean_w = at("mean_w", [P, P], RC + 512)
    vecT = at("vecT", [P, 72], RC + 1024)
    ET = at("ET", [P, 2, 8, NGP], RC + 1536)
    gates = at("gates", [P, 4, 3 * NH], RC + 3072)
    cdist = at("cdist", [P, 4, 32], RC + 3840)
    c2 = RC + 4352
    slope_row = at("slope_row", [P, NH], c2)
    qscale = at("qscale", [P, 8], c2 + 1248)
    posT = at("posT", [P, 2, 16], c2 + 64)
    hidb = at("hidb", [P, 4], c2 + 192)
    Dcol = at("Dcol", [P, NG], c2 + 224)
    nmax = at("nmax", [P, 8], c2 + 352)
    sums = at("sums", [P, 2, 3, NH], c2 + 384)
    cmax = at("cmax", [P, NH], c2 + 768)
    wcmp = at("wcmp", [P, NH], c2 + 832)
    winv = at("winv", [P, 4, 2], RC + 2560)
    xmax = at("xmax", [P, 4], c2 + 928)
    xsum = at("xsum", [P, 4], c2 + 960)
    bnst = at("bnst", [P, 4, 2, 6], c2 + 992)
    bnmv = at("bnmv", [P, 4, 2], c2 + 1184)
    rinv = at("rinv", [P, 4], c2 + 1216)

    xtok = at("xtok", [P, 4, D], RX + 16 * KB)
    araw = [at(f"araw{i}", [NGP, 2, NS], RX + 96 * KB + i * 512) for i in range(3)]
    ldt = at("ldt", [NGP, 2], RX + 97 * KB + 512)
    vrows = at("vrows", [72, P], RX + 73 * KB)
    dl = at("dl", [NG, GC], RX + 73 * KB + 512)
    posl = at("posl", [16, 2, P], RX + 74 * KB)
    rep16 = at("rep16", [GC, 8, GC], RX + 75 * KB)
    dT = at("dT", [GC, NG], RX + 75 * KB + 512)
    LP = at("LP", [P, 2, 8, NGP], RX + 89 * KB)
    LD = at("LD", [P, 2, 8, NGP], RX + 90 * KB)
    FP = at("FP", [P, 2, 8, NGP], RX + 91 * KB)
    LN = at("LN", [P, 2, 8, NGP], RX + 95 * KB)
    cm = [at(f"cm{i}", [P, 8, NGP], RX + 92 * KB + i * 512) for i in range(4)]
    sp = {n: at("sp_" + n, [P, NGP], RX + 94 * KB + i * 64) for i, n in enumerate(
        ["are", "aim", "dt", "th", "er", "k", "s", "s2", "den", "nr", "fr", "fi", "a", "b", "c", "d"])}
    Bt = at("Bt", [P, 2, NGP, GC], RX)
    Craw = at("Craw", [P, 2, 4, 2, NS], RX + 2 * KB)
    Ct = at("Ct", [P, 2, NGP, GC], RX + 6 * KB)
    Cbd = at("Cbd", [P, 2, NGP, 2, GC], RX + 8 * KB)
    Wst = at("Wst", [P, 2, NGP, P], RX)
    Mst = at("Mst", [P, CH, NG, GC], RX + 16 * KB)
    Ost = at("Ost", [P, 2, NGP, CH, GC], RX + 32 * KB)
    H = at("H", [P, 2, NGP, NCH + 1], RX + 48 * KB)
    Ptmp = at("Ptmp", [P, NGP, CH, GC], RX + 48 * KB)
    UT = at("UT", [P, NG, NCH], RX + 57 * KB)
    U1 = at("U1", [P, NG, 4, GC], RX + 57 * KB)
    Pw = at("Pw", [P, 2, NGP, CH, GC], RX + 65 * KB)
    Otmp = at("Otmp", [P, NGP, CH, GC], RX + 81 * KB)
    U8 = at("U8", [NCH, NG, CH, GC], RX + 81 * KB)
    st1 = at("st1", [P, 2, NGP, 8], RX + 65 * KB)
    st2 = at("st2", [P, 2, NGP, 8], RX + 66 * KB)
    Yt = at("Yt", [NCH, 8, 512], RX + 65 * KB)
    gF = at("gF", [P, 4, T], RX)
    gHi = at("gHi", [P, 4, T], RX + 8 * KB, F32R)
    gLo = at("gLo", [P, 4, T], RX + 16 * KB, F32R)
    yF = at("yF", [P, 4, T], RX + 24 * KB)
    yHi = at("yHi", [P, 4, T], RX + 32 * KB, F32R)
    yLo = at("yLo", [P, 4, T], RX + 40 * KB, F32R)
    kqT = at("kqT", [P, 16, T], RX)
    qT, kvcT, kT = kqT[:, 0:8, :], kqT[:, 8:12, :], kqT[:, 12:16, :]
    VA = at("VA", [P, 4, 512], RX + 32 * KB)
    Xc = at("Xc", [P, 2, NKV + 1, T], RX + 40 * KB)
    w1 = at("w1", [P, 2, 16, 256], RX + 60 * KB)
    w2 = at("w2", [P, 2, 2, 2 * HD], RX + 92 * KB)
    wg = at("wg", [P, KT, 3 * NH], RX + 94 * KB)
    hidK = at("hidK", [P, 2, NKV, 32], RX + 96 * KB)
    hidV = at("hidV", [P, 2, NKV, 4, 32], RX + 60 * KB)
    kS = at("kS", [P, 4, T], RX + 16 * KB)
    PTr = [at(f"PTr{i}", [P, T], RX + (40 + 2 * i) * KB) for i in range(4)]
    Tc = at("Tc", [P, NH, 32], RX + 54 * KB)
    dist = at("dist", [P, T], RX + 56 * KB)
    Sr = [at(f"Sr{i}", [P, T], RX + (64 + 2 * i) * KB) for i in range(8)]
    diag = [at(f"diag{i}", [P, P], RX + 80 * KB + 512 * i) for i in range(4)]
    kcT = at("kcT", [P, NKV, 2, 32], RX + 84 * KB)
    Vbd = at("Vbd", [P, NKV, 4, HD], RX + 88 * KB)
    PTc = [at(f"PTc{i}", [P, NKV, P], RX + (94 + 2 * i) * KB) for i in range(2)]
    mHi = at("mHi", [P, KT, T], RX, F32R)
    mLo = at("mLo", [P, KT, T], RX + 16 * KB, F32R)
    mF = [at(f"mF{i}", [P, T], RX + (32 + 2 * i) * KB) for i in range(2)]
    xc = at("xc", [P, KT, T], RX + 36 * KB)
    rstd = at("rstd", [P, T], RX + 52 * KB)
    sq = at("sq", [P, KT, T], RG)
    memHi = at("memHi", [P, KT, MEM], RX + 58 * KB, F32R)
    memLo = at("memLo", [P, KT, MEM], RX + 66 * KB, F32R)
    memF = at("memF", [P, 2, D], RX + 74 * KB)
    kxT = at("kxT", [P, KT, MEM], RX + 82 * KB)
    vx = at("vx", [P, 2, D], RX + 90 * KB)
    qx = at("qx", [P, KT, T], RG)
    xP = [at(f"xP{i}", [P, MEM], RG + (16 + i) * KB) for i in range(2)]
    xPT = [at(f"xPT{i}", [P, 2, T], RG + (18 + 4 * i) * KB) for i in range(2)]
    sHi = at("sHi", [P, KF, T], RG, F32R)
    sLo = at("sLo", [P, KF, T], RG + 44 * KB, F32R)
    sg = [at(f"sg{i}", [P, T], RX + (56 + 2 * i) * KB) for i in range(2)]
    sF = [at(f"sF{i}", [P, T], RX + (60 + 2 * i) * KB) for i in range(2)]
    xc3 = at("xc3", [P, KT, T], RX + 64 * KB)
    rstd3 = at("rstd3", [P, T], RX + 80 * KB)
    otok = [at(f"otok{i}", [P, D], (40 + 4 * i) * KB) for i in range(4)]

    ctx = ExitStack()
    with ctx:
        def sem(name):
            return ctx.enter_context(nc.semaphore(name))

        bank = [ctx.enter_context(nc.psum_tensor(f"bank{i}", [P, 512], F32)) for i in range(8)]

        w_landed = [sem("w_landed0"), sem("w_landed1")]
        w_hi_ready, w_lo_ready, w_used = sem("w_hi_ready"), sem("w_lo_ready"), sem("w_used")
        tile_act, tile_dve = sem("tile_act"), sem("tile_dve")
        hhi_ready, hlo_ready = sem("hhi_ready"), sem("hlo_ready")
        x_landed, par_landed, vec_landed = sem("x_landed"), sem("par_landed"), sem("vec_landed")
        b_landed, c_landed, w1_landed = sem("b_landed"), sem("c_landed"), sem("w1_landed")
        xc_landed, mem_landed, u1_moved = sem("xc_landed"), sem("mem_landed"), sem("u1_moved")
        ident_ready, pool_const, dve_step = sem("ident_ready"), sem("pool_const"), sem("dve_step")
        pool_step = sem("pool_step")
        rep_ready, dt_ready, er_ready, mag_ready = (
            sem("rep_ready"), sem("dt_ready"), sem("er_ready"), sem("mag_ready"))
        angle_ready, sin_ready, par_turned = sem("angle_ready"), sem("sin_ready"), sem("par_turned")
        var0_ready, sd0_ready, xn_ready, h0_turned = (
            sem("var0_ready"), sem("sd0_ready"), sem("xn_ready"), sem("h0_turned"))
        hf0_ready = sem("hf0_ready")
        vec_turned, vec_ready, dcol_done = sem("vec_turned"), sem("vec_ready"), sem("dcol_done")
        ct_turned, ct_ready, m_zero = sem("ct_turned"), sem("ct_ready"), sem("m_zero")
        pw_ready, cbd_ready, o_ready = sem("pw_ready"), sem("cbd_ready"), sem("o_ready")
        m_built, m7_ready, m_moved, wst_turned, wst_ready = sem("m_built"), sem("m7_ready"), sem("m_moved"), sem("wst_turned"), sem("wst_ready")
        u1_ready, ut_turned, ut_ready = sem("u1_ready"), sem("ut_turned"), sem("ut_ready")
        s_done, h_loaded, scan_done = sem("s_done"), sem("h_loaded"), sem("scan_done")
        y_done, y_ready, yt_turned, gelu_done = sem("y_done"), sem("y_ready"), sem("yt_turned"), sem("gelu_done")
        ghi_ready, glo_ready = sem("ghi_ready"), sem("glo_ready")
        glu_sig, yf_ready, yhi_ready, ylo_ready = (
            sem("glu_sig"), sem("yf_ready"), sem("yhi_ready"), sem("ylo_ready"))
        sso_tile = sem("sso_tile")
        v_ready, gate_done, gate_ready = sem("v_ready"), sem("gate_done"), sem("gate_ready")
        hid_done, hidb_ready, hid_ready, pos_ready = sem("hid_done"), sem("hidb_ready"), sem("hid_ready"), sem("pos_ready")
        hid_padded = sem("hid_padded")
        kc_done, kc_ready, vc_done, vc_ready = sem("kc_done"), sem("kc_ready"), sem("vc_done"), sem("vc_ready")
        dist_ready, ks_landed = sem("dist_ready"), sem("ks_landed")
        winv_ready, diag_ready = sem("winv_ready"), sem("diag_ready")
        score_done, max_done, exp_done, turned, turned_dve, turned_act, pv_done = (
            sem("score_done"), sem("max_done"), sem("exp_done"), sem("turned"), sem("turned_dve"),
            sem("turned_act"), sem("pv_done"))
        cscore_done, tc_ready, pc_ready, csum_ready, cturned, ptc_ready, cpv_done = (
            sem("cscore_done"), sem("tc_ready"), sem("pc_ready"), sem("csum_ready"), sem("cturned"),
            sem("ptc_ready"), sem("cpv_done"))
        ohi_ready, olo_ready = sem("ohi_ready"), sem("olo_ready")
        mf_ready, mhi_ready, mlo_ready = sem("mf_ready"), sem("mhi_ready"), sem("mlo_ready")
        mu_ready, xc_ready, sq_ready, var_done, var_ready, sd_ready, nrm_ready, hf_ready = (
            sem("mu_ready"), sem("xc_ready"), sem("sq_ready"), sem("var_done"), sem("var_ready"),
            sem("sd_ready"), sem("nrm_ready"), sem("hf_ready"))
        mem_turned, memhi_ready, memlo_ready, xv_ready = (
            sem("mem_turned"), sem("memhi_ready"), sem("memlo_ready"), sem("xv_ready"))
        xs_done, xmax_ready, xexp_done, xp_ready, xt_done, xpt_ready, xo_done, xohi_ready, xolo_ready = (
            sem("xs_done"), sem("xmax_ready"), sem("xexp_done"), sem("xp_ready"), sem("xt_done"),
            sem("xpt_ready"), sem("xo_done"), sem("xohi_ready"), sem("xolo_ready"))
        sg_ready, sf_ready, shi_ready, slo_ready, fout_done = (
            sem("sg_ready"), sem("sf_ready"), sem("shi_ready"), sem("slo_ready"), sem("fout_done"))
        out_turned, out_copied_a, out_copied_d, out_stored = (
            sem("out_turned"), sem("out_copied_a"), sem("out_copied_d"), sem("out_stored"))

        block = ctx.enter_context(nc.Block())

        w_in, wX = I["w_in"][0], {k: I[k][0] for k in (
            "ssm_w_glu", "ssm_w_out", "nsa_w_out", "w_out", "xattn_w_q", "xattn_w_kv", "xattn_w_o",
            "ffn_w_in", "ffn_w_out")}

        def rows(w):
            return w.rearrange("(k p) n -> p k n", p=P)

        TD = {"sso": 2, "kq": 10, "nsa": 26, "wout": 34, "xk": 42, "xq": 50, "xo": 58, "fout": 66}
        TD_END = 74

        @block.sync
        def _(sp_):
            xt = I["x"][0].rearrange("(a p) n -> p a n", p=P)
            sp_.dma_start(xtok[:, :, :], xt).then_inc(x_landed, 16)

            def load(b, s, dst, src):
                if not (isinstance(b, int) and b < 2):
                    sp_.wait_ge(w_lo_ready, b - 1)
                for half in range(2):
                    sp_.dma_start(dst[half], src[half]).then_inc(w_landed[s], 16)

            def by_k(s, src):
                nk = src.shape[1]
                dst = wraw[s][:, :].rearrange("p (k n) -> p k n", k=nk)
                return [dst[:, 0:nk // 2], dst[:, nk // 2:nk]], [src[:, 0:nk // 2], src[:, nk // 2:nk]]

            def row_block(s, w, r0, c0):
                dst = [wraw[s][:, 512 * e:512 * e + 512] for e in range(2)]
                return dst, [w[bass.ds(r0, P), c0 + 512 * e:c0 + 512 * e + 512] for e in range(2)]

            def column_tiles(name, count, w, c0):
                b0 = BLOCKS[name]
                if b0 == 0:
                    for b in range(2):
                        load(b, b, *by_k(b, rows(w)[:, :, P * b + c0:P * b + c0 + P]))
                with sp_.Fori(int(b0 == 0), count // 2) as i:
                    for s in range(2):
                        load(i * 2 + (b0 + s), s, *by_k(s, rows(w)[:, :, bass.ds(i * (2 * P) + (P * s + c0), P)]))

            def row_tiles(name, count, w, c0):
                b0 = BLOCKS[name]
                with sp_.Fori(0, count // 2) as i:
                    for s in range(2):
                        load(i * 2 + (b0 + s), s, *row_block(s, w, i * (2 * P) + P * s, c0))

            column_tiles("gmixa", 4, w_in, C_GM)
            for b in range(4):
                load(BLOCKS["u"] + b, b % 2, *by_k(b % 2, rows(w_in)[:, 2 * b:2 * b + 2, C_U:C_U + 512]))
            column_tiles("gmixb", 8, w_in, C_GM + 4 * P)
            column_tiles("gmixc", 2, w_in, C_GM + 12 * P)
            for b in range(2):
                load(BLOCKS["glu"] + b, b, *by_k(b, rows(wX["ssm_w_glu"])[:, 2 * b:2 * b + 2, :]))
            column_tiles("gmixd", 2, w_in, C_GM + 14 * P)
            for b in range(4):
                load(BLOCKS["sso"] + b, b % 2, *by_k(b % 2, rows(wX["ssm_w_out"])[:, :, 256 * b:256 * b + 256]))
            for b in range(4):
                dst = wraw[b % 2][:, :].rearrange("p (k z n) -> p z k n", k=2, z=2)
                src = [rows(w_in)[:, 2 * b:2 * b + 2, c + 256:c + 512] for c in (C_KVS, C_KVW)]
                load(BLOCKS["v"] + b, b % 2, [dst[:, 0], dst[:, 1]], src)
            column_tiles("kq", 12, w_in, C_Q)
            for t, c in enumerate((C_KVS, C_KVS + P, C_KVW, C_KVW + P)):
                load(BLOCKS["kq"] + 12 + t, t % 2, *by_k(t % 2, rows(w_in)[:, :, c:c + P]))
            column_tiles("nsa", 8, wX["nsa_w_out"], 0)
            column_tiles("wout", 8, wX["w_out"], 0)
            column_tiles("xk", 8, wX["xattn_w_kv"], 0)
            row_tiles("xv", 8, wX["xattn_w_kv"], D)
            column_tiles("xq", 8, wX["xattn_w_q"], 0)
            column_tiles("xo", 8, wX["xattn_w_o"], 0)
            b0 = BLOCKS["fin"]
            with sp_.Fori(0, KF) as i:
                for s in range(2):
                    load(i * 2 + (b0 + s), s, *by_k(s, rows(wX["ffn_w_in"])[:, :, bass.ds(i * P + s * DFF, P)]))
            row_tiles("fout", KF, wX["ffn_w_out"], 0)
            for tt in range(4):
                sp_.wait_ge(out_copied_a, tt + 1)
                sp_.wait_ge(out_copied_d, tt + 1)
                sp_.dma_start(out[0, tt * P:(tt + 1) * P, :], otok[tt][:, :]).then_inc(out_stored, 16)
            sp_.wait_ge(out_stored, 64)

        @block.scalar
        def _(act):
            act.dma_start(ldt[:, :], I["ssm_log_dt"][0].rearrange("(g q) -> g q", q=2)).then_inc(par_landed, 16)
            for i, name in enumerate(("ssm_a_re", "ssm_a_im")):
                act.dma_start(araw[i][:, :, :], I[name][0].rearrange("(g q) n -> g q n", q=2)).then_inc(par_landed, 16)
            for r0, name in ((0, "ln_emb_g"), (8, "ln_emb_b"), (16, "ln1_g"), (24, "ln1_b"), (32, "ln2_g"),
                             (40, "ln2_b"), (48, "ln3_g"), (56, "ln3_b")):
                v = I[name] if name.startswith("ln_emb") else I[name][0]
                act.dma_start(vrows[r0:r0 + 8, :], v.rearrange("(k p) -> k p", p=P)).then_inc(vec_landed, 16)
            act.dma_start(vrows[64:68, :], I["ssm_b_glu"][0].rearrange("(k p) -> k p", p=P)).then_inc(vec_landed, 16)
            act.dma_start(vrows[68:72, :], I["cmp_b1"][0].rearrange("z (k p) -> (z k) p", p=P)).then_inc(vec_landed, 16)
            act.dma_start(dl[:, :], I["ssm_d"][0].rearrange("(g c) -> g c", c=GC)).then_inc(vec_landed, 16)
            act.dma_start(posl[:, :, :], I["cmp_pos"][0].rearrange("z (r q) d -> r z (q d)", q=2)).then_inc(
                vec_landed, 16)
            for ri, name in enumerate(("ssm_b_re", "ssm_b_im")):
                act.dma_start(Bt[:, ri], I[name][0].rearrange("(g q) n c -> (q n) g c", q=2)).then_inc(b_landed, 16)
            for ri, name in enumerate(("ssm_c_re", "ssm_c_im")):
                for dup in range(2):
                    act.dma_start(Craw[:, ri, :, dup, :], I[name][0].rearrange("(t g) c n -> (g c) t n", t=4)).then_inc(
                        c_landed, 16)

            def split(b, s, pair=None):
                if pair is None:
                    pair = b // 2
                act.wait_ge(w_landed[s], pair * 32 + 32)
                if not (isinstance(b, int) and b < 2):
                    act.wait_ge(w_used, b - 1)
                act.activation(whi[s][:, :], wraw[s][:, :], ACT.Copy).then_inc(w_hi_ready, 1)

            def splits_ahead(b0, s, i):
                split(i * 2 + (b0 + s + 1), (s + 1) % 2, i + (b0 // 2 + s))

            def o_hi(a, g):
                a.wait_ge(pv_done, 16 * (g + 1))
                a.activation(hHi[:, 4 * (g % 2):4 * (g % 2) + 4, g // 2 * P:(g // 2 + 1) * P],
                             bank[4 + g % 2][:, :].rearrange("p (k n) -> p k n", k=4), ACT.Copy).then_inc(ohi_ready, 1)

            def xo_hi(a, h):
                for dt in range(2):
                    a.wait_ge(xo_done, 2 * h + dt + 1)
                    a.activation(mHi[:, 2 * h + dt, :], bank[6 + dt][:, :], ACT.Copy).then_inc(xohi_ready, 1)

            def squares(a, n, centred):
                for m in range(KT):
                    a.wait_ge(xc_ready, KT * (n - 1) + m + 1)
                    a.activation(sq[:, m, :], centred[:, m, :], ACT.Square).then_inc(sq_ready, 1)

            def affine(a, n, m, centred, col):
                c = KT * (n - 1) + m
                a.wait_ge(nrm_ready, c + 1)
                a.activation(hF[:, m, :], centred[:, m, :], ACT.Identity, scale=vecT[:, col + m:col + m + 1],
                             bias=vecT[:, col + 8 + m:col + 9 + m]).then_inc(hf_ready, 1)
                if n < 3:
                    a.wait_ge(hf_ready, c + 1)
                    a.activation(hHi[:, m, :], hF[:, m, :], ACT.Copy).then_inc(hhi_ready, 1)

            act.wait_ge(par_landed, 48)
            act.activation(araw[2][:, :, :], ldt[:, :, None].to_broadcast([NGP, 2, NS]), ACT.Exp).then_inc(dt_ready, 1)
            act.wait_ge(er_ready, 1)
            act.activation(sp["er"][:, :], sp["er"][:, :], ACT.Exp).then_inc(mag_ready, 1)
            act.wait_ge(angle_ready, 1)
            act.activation(sp["s"][:, :], sp["th"][:, :], ACT.Sin).then_inc(sin_ready, 1)
            act.activation(sp["s2"][:, :], sp["th"][:, :], ACT.Sin, scale=0.5).then_inc(sin_ready, 1)
            act.wait_ge(var0_ready, 1)
            act.activation(rinv[:, :], rinv[:, :], ACT.Sqrt).then_inc(sd0_ready, 1)
            split(0, 0)
            for k in range(KT):
                act.wait_ge(hf0_ready, k + 1)
                act.activation(hHi[:, k, :], hF[:, k, :], ACT.Copy).then_inc(hhi_ready, 1)

            def mixer_gates(name, first, loop):
                b0 = BLOCKS[name]
                with act.Fori(0, loop) as i:
                    for s in range(2):
                        splits_ahead(b0, s, i)
                        act.wait_ge(w_used, i * 2 + (b0 + s + 1))
                        act.activation(G[:, i * 2 + (first + s), :], bank[s][:, :], ACT.Sigmoid).then_inc(tile_act, 1)

            def gate_tile(b, t):
                act.wait_ge(w_used, b + 1)
                act.activation(G[:, t, :], bank[t % 2][:, :], ACT.Sigmoid).then_inc(tile_act, 1)

            for t in range(4):
                split(t + 1, (t + 1) % 2)
                gate_tile(t, t)
            for b in range(4):
                split(BLOCKS["u"] + b + 1, (b + 1) % 2)
            act.wait_ge(u1_ready, 1)
            act.wait_ge(o_ready, 2)
            act.wait_ge(pw_ready, 1)
            for half in range(2):
                act.dma_start(U8[:, :, 4 * half:4 * half + 4, :], U1[half:P:2, :, :, :]).then_inc(u1_moved, 16)
            act.wait_ge(m_zero, 1)
            act.wait_ge(m7_ready, 1)
            for j in range(CH - 1):
                act.dma_start(Mst[0:GC * (j + 1), j, :, :], Mst[GC * (7 - j):P, 7, :, :]).then_inc(m_moved, 16)
            mixer_gates("gmixb", 4, 4)
            split(BLOCKS["gmixc"] + 1, 1)
            for ct in range(4):
                act.wait_ge(yt_turned, ct + 1)
                act.activation(gF[:, ct, :], bank[2 + ct][:, :], ACT.Gelu_apprx_tanh).then_inc(gelu_done, 1)
            act.dma_start(w1[:, :, :, :], I["cmp_w1"][0].rearrange("z (r p) e -> p z r e", p=P)).then_inc(w1_landed, 16)
            for e in range(2):
                for z in range(2):
                    act.dma_start(w2[:, z, :, HD * e:HD * e + HD], I["cmp_w2"][0, z].rearrange(
                        "(k p) d -> p k d", p=P)).then_inc(w1_landed, 16)
            act.dma_start(wg[:, :, :], rows(w_in)[:, :, C_GN:C_GN + 3 * NH]).then_inc(w1_landed, 16)
            for ct in range(4):
                act.wait_ge(gelu_done, ct + 1)
                act.activation(gHi[:, ct, :], gF[:, ct, :], ACT.Copy).then_inc(ghi_ready, 1)
            gate_tile(BLOCKS["gmixc"], 12)
            split(BLOCKS["glu"], 0)
            gate_tile(BLOCKS["gmixc"] + 1, 13)
            split(BLOCKS["glu"] + 1, 1)
            split(BLOCKS["gmixd"], 0)
            split(BLOCKS["gmixd"] + 1, 1)
            act.wait_ge(vec_ready, 1)
            for m in range(4):
                act.wait_ge(w_used, BLOCKS["glu"] + 2)
                act.activation(yF[:, m, :], bank[2 + m][:, :], ACT.Sigmoid, bias=vecT[:, 64 + m:65 + m]).then_inc(glu_sig, 1)
            gate_tile(BLOCKS["gmixd"], 14)
            split(BLOCKS["sso"], 0)
            for m in range(4):
                act.wait_ge(yf_ready, m + 1)
                act.activation(yHi[:, m, :], yF[:, m, :], ACT.Copy).then_inc(yhi_ready, 1)
            gate_tile(BLOCKS["gmixd"] + 1, 15)
            for b in range(8):
                split(BLOCKS["sso"] + b + 1, (b + 1) % 2)
            b0 = BLOCKS["kq"]
            with act.Fori(0, 8) as i:
                for s in range(2):
                    splits_ahead(b0, s, i)
            act.wait_ge(tile_dve, TD["kq"] + 12)
            for z in range(2):
                for e in range(2):
                    src = kvcT[64 * e:64 * e + 64, 2 * z:2 * z + 2, :]
                    dst = Xc[:, z, e:NKV:2, :]
                    act.dma_start(dst[0:64], src).then_inc(xc_landed, 16)
                    act.dma_start(dst[64:128, :, 0:T - 1], src[:, :, 1:T]).then_inc(xc_landed, 16)
            act.wait_ge(tile_dve, TD["nsa"])
            act.wait_ge(xc_landed, 8 * 16)
            for e in range(2):
                act.dma_start(kS[64 * e:64 * e + 64, :, :], kT[64 - 64 * e:128 - 64 * e, :, :]).then_inc(ks_landed, 16)
            act.wait_ge(gate_done, 1)
            act.activation(gates[:, :, :], bank[6][:, 0:4 * 48].rearrange("p (a n) -> p a n", a=4), ACT.Sigmoid).then_inc(
                gate_ready, 1)
            for j in range(4):
                act.wait_ge(hidb_ready, j + 1)
                src = bank[2 + j][:, 0:NKV * NCMP].rearrange("p (h n) -> p h n", h=NKV)
                if j < 2:
                    dst = hidK[:, j, :, 0:NCMP]
                else:
                    dst, src = hidV[:, j - 2, :, :, 0:NCMP], src[:, :, None, :].to_broadcast([P, NKV, 4, NCMP])
                act.activation(dst, src, ACT.Gelu_apprx_tanh, bias=hidb[:, j:j + 1]).then_inc(hid_ready, 1)

            def compressed_exp(qi):
                act.wait_ge(tc_ready, qi + 1)
                act.activation(Tc[:, :, :], Tc[:, :, :], ACT.Exp).then_inc(pc_ready, 1)

            compressed_exp(0)
            for u in range(UNITS + PV):
                if u < UNITS:
                    m, br, e, qi = unit(u)
                    n, h = P * (qi + 1), 2 * m + e
                    act.wait_ge(max_done, u + 1)
                    act.activation(Sr[u % 8][:, 0:n], Sr[u % 8][:, 0:n], ACT.Exp, bias=nmax[:, u % 8:u % 8 + 1],
                                   scale=-1.0, accum_out=sums[:, qi % 2, 1 + br, h:h + 1]).then_inc(exp_done, 1)
                if u % 32 == CMP_EXP and u // 32 < 3:
                    compressed_exp(u // 32 + 1)
                v = u - TURN
                if 0 <= v < UNITS and v % 2 == 1:
                    n = P * (unit(v)[3] + 1)
                    act.wait_ge(turned, v + 1)
                    if v >= 4:
                        act.wait_ge(pv_done, v - 3)
                    act.activation(PTr[v % 4][:, 0:n], bank[3][:, 0:n], ACT.Copy).then_inc(turned_act, 1)
                if u % 16 == O_STEP and u > 16:
                    o_hi(act, (u // 16) - 1)
            o_hi(act, 7)
            act.dma_start(memF[:, :, :], I["mem"][0].rearrange("(a p) n -> p a n", p=P)).then_inc(mem_landed, 16)
            for stage in ("nsa", "wout"):
                b0 = BLOCKS[stage]
                if stage == "wout":
                    for j in range(4):
                        act.wait_ge(mem_turned, j + 1)
                        act.activation(memHi[:, 2 * j:2 * j + 2, :], bank[2 + j][:, :].rearrange(
                            "p (k n) -> p k n", k=2), ACT.Copy).then_inc(memhi_ready, 1)
                with act.Fori(0, 4) as i:
                    for s in range(2):
                        splits_ahead(b0, s, i)
                        if stage == "nsa":
                            act.wait_ge(mf_ready, i * 2 + (s + 1))
                            act.activation(mHi[:, i * 2 + s, :], mF[s][:, :], ACT.Copy).then_inc(mhi_ready, 1)
            squares(act, 1, xc)
            b0 = BLOCKS["xk"]
            with act.Fori(0, 4) as i:
                for s in range(2):
                    splits_ahead(b0, s, i)
            act.wait_ge(var_ready, 1)
            act.activation(rstd[:, :], rstd[:, :], ACT.Sqrt).then_inc(sd_ready, 1)
            for b in range(8):
                split(BLOCKS["xv"] + b + 1, (b + 1) % 2)
                affine(act, 1, b, xc, 16)
            b0 = BLOCKS["xq"]
            with act.Fori(0, 4) as i:
                for s in range(2):
                    splits_ahead(b0, s, i)
            for n in range(4 * XH):
                h, qi = n // 4, n % 4
                act.wait_ge(xmax_ready, n + 1)
                if n >= 2:
                    act.wait_ge(xt_done, n - 1)
                act.activation(xP[n % 2][:, :], bank[2 + n % 2][:, 0:MEM], ACT.Exp, bias=xmax[:, n % 4:n % 4 + 1],
                               accum_out=xsum[:, n % 4:n % 4 + 1]).then_inc(xexp_done, 1)
                if qi == 1 and h >= 1:
                    xo_hi(act, h - 1)
            xo_hi(act, XH - 1)
            b0 = BLOCKS["xo"]
            with act.Fori(0, 4) as i:
                for s in range(2):
                    splits_ahead(b0, s, i)
            squares(act, 2, xc)
            act.wait_ge(var_ready, 2)
            act.activation(rstd[:, :], rstd[:, :], ACT.Sqrt).then_inc(sd_ready, 1)
            for m in range(KT):
                affine(act, 2, m, xc, 32)
            b0 = BLOCKS["fin"]
            with act.Fori(0, KF // 2) as i:
                for t in range(2):
                    for s in range(2):
                        split(i * 4 + (b0 + 2 * t + s + 1), (s + 1) % 2, i * 2 + (b0 // 2 + t + s))
                    act.wait_ge(w_used, i * 4 + (b0 + 2 * t + 1))
                    act.wait_ge(sf_ready, i * 2 + (t + 1))
                    act.activation(sg[t][:, :], bank[2 * t][:, :], ACT.Silu).then_inc(sg_ready, 1)
                    act.wait_ge(sf_ready, i * 2 + (t + 3))
                    act.activation(sHi[:, i * 2 + t, :], sF[t][:, :], ACT.Copy).then_inc(shi_ready, 1)
            b0 = BLOCKS["fout"]
            for s in range(2):
                splits_ahead(b0, s, 0)
            with act.Fori(1, KF // 2 - 1) as i:
                for s in range(2):
                    splits_ahead(b0, s, i)
            split(NBLOCKS - 1, 1)
            squares(act, 3, xc3)
            act.wait_ge(var_ready, 3)
            act.activation(rstd3[:, :], rstd3[:, :], ACT.Sqrt).then_inc(sd_ready, 1)
            for m in range(KT):
                affine(act, 3, m, xc3, 48)
            for tt in range(4):
                act.wait_ge(out_turned, 2 * tt + 1)
                act.activation(otok[tt][:, 0:512], bank[2 * (tt % 2)][:, :], ACT.Copy).then_inc(out_copied_a, 1)

        @block.gpsimd
        def _(pool):
            steps = [0]

            def link(ins):
                steps[0] += 1
                ins.then_inc(pool_step, 1)
                pool.wait_ge(pool_step, steps[0])

            link(pool.memset(ident[:, :], 0.0))
            pool.affine_select(out=ident[:, :], in_=ident[:, :], compare_op=ALU.not_equal, fill=1.0, base=0,
                               pattern=[[-1, P]], channel_multiplier=1).then_inc(ident_ready, 1)
            pool.memset(mean_w[:, :], 1.0 / D).then_inc(pool_const, 1)
            link(pool.iota(cdist[:, :, :], [[-P, 4], [16, 32]], base=31, channel_multiplier=-1,
                           allow_small_or_imprecise_dtypes=True))
            link(pool.affine_select(out=cdist[:, :, :], in_=cdist[:, :, :], compare_op=ALU.is_ge, fill=MASKED, base=-31,
                                    pattern=[[P, 4], [-16, 32]], channel_multiplier=1))
            def lo(b, s):
                pool.wait_ge(w_hi_ready, b + 1)
                pool.tensor_tensor(wlo[s][:, :], wraw[s][:, :], whi[s][:, :].bitcast(F32), ALU.subtract).then_inc(
                    w_lo_ready, 1)

            def h_lo(m, count):
                pool.wait_ge(hhi_ready, count + m + 1)
                pool.tensor_tensor(hLo[:, m, :], hF[:, m, :], hHi[:, m, :].bitcast(F32), ALU.subtract).then_inc(
                    hlo_ready, 1)

            lo(0, 0)
            for k in range(KT):
                h_lo(k, 0)
            lo(1, 1)
            pool.wait_ge(h0_turned, KT)
            pool.memset(Mst[:, 0:CH - 1, :, :], 0.0).then_inc(m_zero, 1)
            pool.wait_ge(ct_ready, 2)
            minus_lam = [LN[:, ri].rearrange("p j g -> p g j")[:, :, :, None].to_broadcast([P, NGP, CH, GC]) for ri in range(2)]
            cc = [Ct[:, ri][:, :, None, :].to_broadcast([P, NGP, CH, GC]) for ri in range(2)]
            link(pool.tensor_tensor(Ost[:, 1], cc[0], minus_lam[1], ALU.mult))
            lo(2, 0)
            link(pool.tensor_tensor(Otmp[:, :, :, :], cc[1], minus_lam[0], ALU.mult))
            lo(3, 1)
            pool.tensor_tensor(Ost[:, 1], Ost[:, 1], Otmp[:, :, :, :], ALU.add).then_inc(o_ready, 1)
            with pool.Fori(2, BLOCKS["nsa"] // 2) as i:
                for s in range(2):
                    lo(i * 2 + s, s)
            pool.wait_ge(hid_done, 4)
            link(pool.iota(dist[:, :], [[1, T]], base=P - T, channel_multiplier=-1, allow_small_or_imprecise_dtypes=True))
            pool.affine_select(out=dist[:, :], in_=dist[:, :], compare_op=ALU.is_ge, fill=MASKED, base=T - P,
                               pattern=[[-1, T]], channel_multiplier=1).then_inc(dist_ready, 1)
            lo(BLOCKS["nsa"], 0)
            for u in range(UNITS):
                m, br, e, qi = unit(u)
                h = 2 * m + e
                pool.wait_ge(winv_ready, u // 2 + 1)
                if u >= 4:
                    pool.wait_ge(turned, u - 3)
                pool.tensor_scalar(diag[u % 4][:, :], ident[:, :], winv[:, u // 2 % 4, e:e + 1],
                                   gates[:, qi, 3 * h + 1 + br:3 * h + 2 + br], ALU.mult, ALU.mult).then_inc(diag_ready, 1)
            lo(BLOCKS["nsa"] + 1, 1)
            with pool.Fori(BLOCKS["nsa"] // 2 + 1, (BLOCKS["xv"]) // 2) as i:
                for s in range(2):
                    lo(i * 2 + s, s)
            b = BLOCKS["xv"]
            lo(b, 0)
            for m in range(KT):
                if m < KT - 1:
                    lo(b + m + 1, (m + 1) % 2)
                h_lo(m, 8)
            with pool.Fori(BLOCKS["xq"] // 2, BLOCKS["fin"] // 2) as i:
                for s in range(2):
                    lo(i * 2 + s, s)
            lo(BLOCKS["fin"], 0)
            for m in range(KT):
                h_lo(m, 16)
            lo(BLOCKS["fin"] + 1, 1)
            with pool.Fori(BLOCKS["fin"] // 2 + 1, NBLOCKS // 2) as i:
                for s in range(2):
                    lo(i * 2 + s, s)

        @block.vector
        def _(dve):
            steps = [0]

            def link(ins):
                steps[0] += 1
                ins.then_inc(dve_step, 1)
                dve.wait_ge(dve_step, steps[0])

            def tt(o, a, b, op):
                return dve.tensor_tensor(o, a, b, op)

            dve.memset(nmax[:, :], 0.0).then_inc(tile_act, 2)
            dve.memset(cmax[:, :], 0.0).then_inc(tile_dve, 2)
            dve.memset(xmax[:, :], 0.0).then_inc(sf_ready, 2)
            for h in range(NH):
                half, m = slice(64 * (h % 2), 64 * (h % 2) + 64), h // 2
                dve.memset(slope_row[:, h:h + 1], SLOPES[h])
                last = dve.memset(qscale[half, m:m + 1], HD ** -0.5 / SLOPES[h])
            link(last)
            dve.wait_ge(ident_ready, 1)
            dve.tensor_copy(rep16[:, :, :], ident[0:GC, None, 0:GC].to_broadcast([GC, 8, GC])).then_inc(rep_ready, 1)

            v = {n: t[:, :] for n, t in sp.items()}
            dve.wait_ge(par_turned, 1)
            dve.tensor_scalar(v["are"], bank[6][:, 0:NGP], -1e-4, None, ALU.min)
            dve.tensor_copy(v["aim"], bank[6][:, NGP:2 * NGP])
            link(dve.tensor_copy(v["dt"], bank[6][:, 2 * NGP:3 * NGP]))
            tt(v["er"], v["are"], v["dt"], ALU.mult).then_inc(er_ready, 1)
            link(tt(v["th"], v["aim"], v["dt"], ALU.mult))
            link(dve.tensor_scalar(v["k"], v["th"], 1.0 / TWO_PI, ROUND, ALU.mult, ALU.add))
            link(dve.tensor_scalar(v["k"], v["k"], -ROUND, None, ALU.add))
            for part in (PI_A, PI_B, PI_C):
                link(dve.scalar_tensor_tensor(out=v["th"], in0=v["k"], scalar=-part, in1=v["th"], op0=ALU.mult, op1=ALU.add))
            dve.tensor_scalar(v["th"], v["th"], 3.1415925, -3.1415925, ALU.min, ALU.max).then_inc(angle_ready, 1)
            dve.wait_ge(sin_ready, 2)
            dve.wait_ge(mag_ready, 1)
            link(tt(v["s2"], v["s2"], v["s2"], ALU.mult))
            link(dve.tensor_scalar(v["s2"], v["s2"], -2.0, 1.0, ALU.mult, ALU.add))
            tt(LP[:, 0, 0, :], v["er"], v["s2"], ALU.mult)
            tt(v["den"], v["are"], v["are"], ALU.mult)
            tt(v["k"], v["aim"], v["aim"], ALU.mult)
            link(tt(LP[:, 1, 0, :], v["er"], v["s"], ALU.mult))
            link(tt(v["den"], v["den"], v["k"], ALU.add))
            dve.tensor_scalar(v["nr"], LP[:, 0, 0, :], -1.0, None, ALU.add)
            link(dve.reciprocal(v["den"], v["den"]))
            tt(v["a"], v["nr"], v["are"], ALU.mult)
            tt(v["b"], LP[:, 1, 0, :], v["aim"], ALU.mult)
            tt(v["c"], LP[:, 1, 0, :], v["are"], ALU.mult)
            link(tt(v["d"], v["nr"], v["aim"], ALU.mult))
            tt(v["fr"], v["a"], v["b"], ALU.add)
            link(tt(v["fi"], v["c"], v["d"], ALU.subtract))
            tt(v["fr"], v["fr"], v["den"], ALU.mult)
            link(tt(v["fi"], v["fi"], v["den"], ALU.mult))

            def cmul(dst, d0, n, a, a0, y):
                x = [a[:, ri, a0:a0 + n, :] for ri in range(2)]
                y = [part[:, None, :].to_broadcast([P, n, NGP]) for part in y]
                tt(cm[0][:, 0:n, :], x[0], y[0], ALU.mult)
                tt(cm[1][:, 0:n, :], x[1], y[1], ALU.mult)
                tt(cm[2][:, 0:n, :], x[0], y[1], ALU.mult)
                link(tt(cm[3][:, 0:n, :], x[1], y[0], ALU.mult))
                tt(dst[:, 0, d0:d0 + n, :], cm[0][:, 0:n, :], cm[1][:, 0:n, :], ALU.subtract)
                link(tt(dst[:, 1, d0:d0 + n, :], cm[2][:, 0:n, :], cm[3][:, 0:n, :], ALU.add))

            def power(t, i):
                return t[:, 0, i, :], t[:, 1, i, :]

            cmul(LP, 1, 1, LP, 0, power(LP, 0))
            cmul(LP, 2, 2, LP, 0, power(LP, 1))
            cmul(LP, 4, 4, LP, 0, power(LP, 3))
            dve.memset(LD[:, 0, 7:8, :], 1.0)
            dve.memset(LD[:, 1, 7:8, :], 0.0)
            for i in range(3):
                dve.tensor_copy(LD[:, :, 6 - i, :], LP[:, :, i, :])
            link(dve.tensor_copy(ET[:, :, 0, :], LP[:, :, 7, :]))
            cmul(LD, 0, 4, LD, 4, power(LP, 3))
            cmul(FP, 0, 8, LD, 0, (v["fr"], v["fi"]))
            cmul(ET, 1, 1, ET, 0, power(ET, 0))
            cmul(ET, 2, 2, ET, 0, power(ET, 1))
            cmul(ET, 4, 4, ET, 0, power(ET, 3))
            dve.tensor_scalar(LN[:, :, :, :], LP[:, :, :, :], -1.0, None, ALU.mult)
            dve.memset(sums[:, :, :, :], 0.0)

            dve.wait_ge(x_landed, 16)
            for a in range(4):
                for half in range(2):
                    last = dve.bn_stats(bnst[:, a, half, :], xtok[:, a, 512 * half:512 * half + 512])
            link(last)
            for a in range(4):
                last = dve.bn_aggr(bnmv[:, a, :], bnst[:, a, :, :])
            link(last)
            dve.tensor_scalar(rinv[:, :], bnmv[:, :, 1], EPS, None, ALU.add).then_inc(var0_ready, 1)
            dve.wait_ge(sd0_ready, 1)
            link(dve.reciprocal(rinv[:, :], rinv[:, :]))
            for a in range(4):
                dve.tensor_scalar(xtok[:, a, :], xtok[:, a, :], bnmv[:, a, 0:1], rinv[:, a:a + 1],
                                  ALU.subtract, ALU.mult).then_inc(xn_ready, 1)
            dve.wait_ge(vec_turned, 1)
            dve.tensor_copy(dT[:, :], bank[7][0:GC, 128:128 + NG])
            dve.tensor_copy(posT[:, :, :], bank[7][:, 160:192].rearrange("p (z r) -> p z r", z=2))
            dve.tensor_copy(vecT[:, :], bank[7][:, 0:72]).then_inc(vec_ready, 1)
            dve.wait_ge(vec_ready, 1)
            for k in range(KT):
                dve.wait_ge(h0_turned, k + 1)
                dve.tensor_scalar(hF[:, k, :], bank[k % 2][:, :], vecT[:, k:k + 1], vecT[:, 8 + k:9 + k],
                                  ALU.mult, ALU.add).then_inc(hf0_ready, 1)

            dve.wait_ge(dcol_done, 1)
            dve.tensor_copy(Dcol[:, :], bank[6][:, 0:NG])
            for ri in range(2):
                dve.wait_ge(ct_turned, ri + 1)
                for q in range(2):
                    last = dve.tensor_copy(Ct[64 * q:64 * q + 64, ri, :, :], bank[4 + ri][:, :].rearrange(
                        "p (g q c) -> p q g c", q=2, c=GC)[64 * q:64 * q + 64, q])
                last.then_inc(ct_ready, 1)
            dve.wait_ge(ct_ready, 2)
            link(dve.memset(Cbd[:, :, :, :, :], 0.0))
            for q in range(2):
                rows_q = slice(64 * q, 64 * q + 64)
                dve.tensor_copy(Cbd[rows_q, 0, :, q, :], Ct[rows_q, 0, :, :])
                last = dve.tensor_scalar(Cbd[rows_q, 1, :, q, :], Ct[rows_q, 1, :, :], -1.0, None, ALU.mult)
            last.then_inc(cbd_ready, 1)
            dve.wait_ge(b_landed, 32)
            shape = [P, NGP, CH, GC]
            f = [FP[:, ri].rearrange("p s g -> p g s")[:, :, :, None].to_broadcast(shape) for ri in range(2)]
            bb = [Bt[:, ri][:, :, None, :].to_broadcast(shape) for ri in range(2)]
            for ri, (x, y, op) in enumerate(((0, 1, ALU.subtract), (1, 0, ALU.add))):
                dst = Pw[:, ri]
                tt(dst, bb[x], f[0], ALU.mult)
                link(tt(Ptmp[:, :, :, :], bb[y], f[1], ALU.mult))
                link(tt(dst, dst, Ptmp[:, :, :, :], op))
            dve.memset(nmax[:, :], 0.0).then_inc(pw_ready, 1)
            lam = [LP[:, ri].rearrange("p j g -> p g j")[:, :, :, None].to_broadcast(shape) for ri in range(2)]
            cc = [Ct[:, ri][:, :, None, :].to_broadcast(shape) for ri in range(2)]
            tt(Ost[:, 0], cc[0], lam[0], ALU.mult)
            link(tt(Ptmp[:, :, :, :], cc[1], lam[1], ALU.mult))
            tt(Ost[:, 0], Ost[:, 0], Ptmp[:, :, :, :], ALU.subtract).then_inc(o_ready, 1)
            dve.wait_ge(w_used, BLOCKS["u"] + 4)
            for r in range(4):
                last = dve.tensor_copy(U1[:, :, r, :], bank[2 + r][:, :].rearrange("p (g c) -> p g c", g=NG))
            last.then_inc(u1_ready, 1)
            skip = Ptmp[:, 0:4].rearrange("p a b c -> p (a b c)").rearrange("p (g c) -> p g c", g=NG)
            dve.wait_ge(o_ready, 2)
            link(tt(skip, Dcol[:, :, None].to_broadcast([P, NG, GC]), ident[:, None, P - GC:P].to_broadcast([P, NG, GC]),
                    ALU.mult))
            dve.wait_ge(m_built, 1)
            tt(Mst[:, 7, :, :], bank[6][:, :].rearrange("p (g c) -> p g c", g=NG), skip, ALU.add).then_inc(m7_ready, 1)
            for j in range(8):
                dve.wait_ge(wst_turned, j + 1)
                dve.tensor_copy(Wst[:, j // 4, 4 * (j % 4):4 * (j % 4) + 4, :], bank[7 - j % 2][:, :].rearrange(
                    "p (g n) -> p g n", g=4)).then_inc(wst_ready, 1)
            for j in range(4):
                dve.wait_ge(ut_turned, j + 1)
                dve.tensor_copy(UT[:, 8 * j:8 * j + 8, :], bank[2 + j][:, :].rearrange("p (g n) -> p g n", g=8)).then_inc(
                    ut_ready, 1)
            dve.memset(H[:, :, :, 0:1], 0.0)
            for j in range(4):
                dve.wait_ge(s_done, j + 1)
                last = dve.tensor_copy(H[:, j // 2, 8 * (j % 2):8 * (j % 2) + 8, 1:NCH + 1], bank[2 + j][:, :].rearrange(
                    "p (g n) -> p g n", g=8))
                last.then_inc(h_loaded, 1)
            dve.wait_ge(h_loaded, 4)

            def advance(c1, c0, n, e):
                def col(c):
                    return H[:, :, :, c:c + 8 * (n - 1) + 1:8]

                cur, prev = col(c1), col(c0)
                er = ET[:, 0, e, :][:, None, :, None].to_broadcast([P, 2, NGP, n])
                ei = ET[:, 1, e, :][:, :, None].to_broadcast([P, NGP, n])
                tt(st1[:, :, :, 0:n], prev, er, ALU.mult)
                tt(st2[:, 0, :, 0:n], prev[:, 1], ei, ALU.mult)
                link(tt(st2[:, 1, :, 0:n], prev[:, 0], ei, ALU.mult))
                link(tt(cur, cur, st1[:, :, :, 0:n], ALU.add))
                tt(cur[:, 0], cur[:, 0], st2[:, 0, :, 0:n], ALU.subtract)
                link(tt(cur[:, 1], cur[:, 1], st2[:, 1, :, 0:n], ALU.add))

            for i in range(1, 8):
                advance(1 + i, i, 8, 0)
            for s in range(1, 8):
                advance(8 * s + 8, 8 * s, 1, 7)
            for i in range(7):
                advance(9 + i, 8, 7, i)
            dve.memset(nmax[:, :], 0.0).then_inc(scan_done, 1)
            for q in range(4):
                dve.wait_ge(y_done, q + 1)
                dst = Yt[:, :, P * q:P * q + P].rearrange("p j (g e c) -> p e g j c", g=4, e=2)
                for e in range(2):
                    dve.tensor_copy(dst[:, e], bank[2 + 2 * (q % 2) + e][0:64, :].rearrange(
                        "p (g j c) -> p g j c", g=4, j=8)).then_inc(y_ready, 1)
            for ct in range(4):
                dve.wait_ge(ghi_ready, ct + 1)
                tt(gLo[:, ct, :], gF[:, ct, :], gHi[:, ct, :].bitcast(F32), ALU.subtract).then_inc(glo_ready, 1)
            for m in range(4):
                dve.wait_ge(glu_sig, m + 1)
                tt(yF[:, m, :], yF[:, m, :], gF[:, m, :], ALU.mult).then_inc(yf_ready, 1)
            for m in range(4):
                dve.wait_ge(yhi_ready, m + 1)
                tt(yLo[:, m, :], yF[:, m, :], yHi[:, m, :].bitcast(F32), ALU.subtract).then_inc(ylo_ready, 1)
            dve.wait_ge(tile_act, 2 + 16)
            for t in range(KT):
                if t % 2:
                    dve.wait_ge(w_used, BLOCKS["sso"] + t // 2 + 1)
                else:
                    dve.wait_ge(sso_tile, t // 2 + 1)
                gv = G[:, t, :].rearrange("p (c j) -> p j c", j=CH)
                tt(gv, gv, bank[t % 2][:, :].rearrange("p (j c) -> p j c", j=CH), ALU.mult).then_inc(tile_dve, 1)
            dve.wait_ge(w_used, BLOCKS["v"] + 4)
            for a in range(4):
                dve.tensor_copy(VA[:, a, :], bank[2 + a][:, :]).then_inc(v_ready, 1)
            b0 = BLOCKS["kq"]
            for t in range(8):
                dve.wait_ge(w_used, b0 + t + 1)
                dve.tensor_scalar(kqT[:, t, :], bank[t % 2][:, :], qscale[:, t:t + 1], None, ALU.mult).then_inc(tile_dve, 1)
            for z in range(2):
                last = dve.memset(Xc[:, z, NKV, :], 0.0)
            link(last)
            dve.tensor_copy(Xc[:, :, NKV, 0:32:2], posT[:, :, :]).then_inc(pos_ready, 1)
            with dve.Fori(4, 8) as i:
                for s in range(2):
                    dve.wait_ge(w_used, i * 2 + (b0 + s + 1))
                    dve.tensor_copy(kqT[:, i * 2 + s, :], bank[s][:, :]).then_inc(tile_dve, 1)
            dve.memset(hidK[:, :, :, NCMP:32], 0.0)
            for j in range(4):
                dve.wait_ge(hid_done, j + 1)
                tt(hidb[:, j:j + 1], bank[2 + j][:, NKV * NCMP:NKV * NCMP + 1], vecT[:, 68 + j:69 + j], ALU.add).then_inc(
                    hidb_ready, 1)
            dve.memset(hidV[:, :, :, :, NCMP:32], 0.0).then_inc(hid_padded, 1)
            dve.memset(kcT[:, :, :, :], 0.0)
            link(dve.memset(Vbd[:, :, :, :], 0.0))
            dve.wait_ge(kc_done, 1)
            for e in range(2):
                last = dve.tensor_copy(kcT[64 * e:64 * e + 64, :, e, :], bank[6][64 * e:64 * e + 64, 0:P].rearrange(
                    "p (h n) -> p h n", h=NKV))
            last.then_inc(kc_ready, 1)
            dve.wait_ge(vc_done, 1)
            for g in range(4):
                last = dve.tensor_copy(Vbd[32 * g:32 * g + 32, :, g, :], bank[7][32 * g:32 * g + 32, 0:256].rearrange(
                    "p (h d) -> p h d", h=NKV))
            last.then_inc(vc_ready, 1)
            dve.wait_ge(dist_ready, 1)

            def o_lo(g):
                dve.wait_ge(ohi_ready, g + 1)
                dst = slice(4 * (g % 2), 4 * (g % 2) + 4), slice(g // 2 * P, (g // 2 + 1) * P)
                tt(hLo[:, dst[0], dst[1]], bank[4 + g % 2][:, :].rearrange("p (k n) -> p k n", k=4),
                   hHi[:, dst[0], dst[1]].bitcast(F32), ALU.subtract).then_inc(olo_ready, 1)

            def compressed_scores(qi):
                dve.wait_ge(cscore_done, qi + 1)
                if qi >= 1:
                    dve.wait_ge(cturned, qi)
                link(tt(Tc[:, :, :], bank[7][:, :].rearrange("p (h n) -> p h n", h=NH),
                        cdist[:, qi, None, :].to_broadcast([P, NH, 32]), ALU.add))
                link(dve.tensor_reduce(cmax[:, :], Tc[:, :, :], AX.X, ALU.max))
                link(dve.tensor_scalar(cmax[:, :], cmax[:, :], MAX_FLOOR, None, ALU.max))
                link(tt(Tc[:, :, :], Tc[:, :, :], cmax[:, :, None].to_broadcast([P, NH, 32]), ALU.subtract))
                tt(Tc[:, :, :], Tc[:, :, :], slope_row[:, :, None].to_broadcast([P, NH, 32]), ALU.mult).then_inc(
                    tc_ready, 1)

            def compressed_sums(qi):
                dve.wait_ge(pc_ready, qi + 1)
                link(dve.tensor_reduce(wcmp[:, :], Tc[:, :, :], AX.X, ALU.add))
                link(dve.tensor_scalar(wcmp[:, :], wcmp[:, :], 1e-30, None, ALU.max))
                link(dve.reciprocal(wcmp[:, :], wcmp[:, :]))
                if qi == 0:
                    dve.wait_ge(gate_ready, 1)
                link(tt(wcmp[:, :], wcmp[:, :], gates[:, qi, 0:3 * NH:3], ALU.mult))
                tt(Tc[:, :, :], Tc[:, :, :], wcmp[:, :, None].to_broadcast([P, NH, 32]), ALU.mult).then_inc(csum_ready, 1)

            def compressed_copy(qi):
                dve.wait_ge(cturned, qi + 1)
                if qi >= 2:
                    dve.wait_ge(pv_done, 32 * (qi - 1))
                dve.tensor_copy(PTc[qi % 2][:, :, :], bank[7][:, :].rearrange("p (h n) -> p h n", h=NKV)).then_inc(ptc_ready, 1)

            compressed_scores(0)
            compressed_sums(0)
            compressed_copy(0)
            for u in range(UNITS + PV):
                if u < UNITS:
                    m, br, e, qi = unit(u)
                    n, h = P * (qi + 1), 2 * m + e
                    dve.wait_ge(score_done, u + 1)
                    if u >= 8:
                        dve.wait_ge(turned, u - 7)
                    dve.tensor_tensor_reduce(Sr[u % 8][:, 0:n], dist[:, T - n:T], bank[SCORE_BANKS[u % 3]][:, 0:n],
                                             -SLOPES[h], 3e38, ALU.add, ALU.min, nmax[:, u % 8:u % 8 + 1]).then_inc(
                                                 max_done, 1)
                if u % 2 == 1 and 3 <= u < UNITS + 2:
                    m, br, e, qi = unit(u - 3)
                    p = u // 2 - 1
                    dve.wait_ge(exp_done, u - 1)
                    if p >= 4:
                        dve.wait_ge(diag_ready, 2 * (p - 3))
                    link(dve.tensor_scalar(winv[:, p % 4, :], sums[:, qi % 2, 1 + br, 2 * m:2 * m + 2], 1e-30, None, ALU.max))
                    dve.reciprocal(winv[:, p % 4, :], winv[:, p % 4, :]).then_inc(winv_ready, 1)
                if u // 32 < 3:
                    if u % 32 == CMP_SCORE:
                        compressed_scores(u // 32 + 1)
                    elif u % 32 == CMP_SUM:
                        compressed_sums(u // 32 + 1)
                    elif u % 32 == CMP_COPY:
                        compressed_copy(u // 32 + 1)
                v = u - TURN
                if 0 <= v < UNITS and v % 2 == 0:
                    n = P * (unit(v)[3] + 1)
                    dve.wait_ge(turned, v + 1)
                    if v >= 4:
                        dve.wait_ge(pv_done, v - 3)
                    dve.tensor_copy(PTr[v % 4][:, 0:n], bank[2][:, 0:n]).then_inc(turned_dve, 1)
                if u % 16 == O_STEP and u > 16:
                    o_lo(u // 16 - 1)
            o_lo(7)

            b0 = BLOCKS["nsa"]
            with dve.Fori(0, 4) as i:
                for s in range(2):
                    dve.wait_ge(w_used, i * 2 + (b0 + s + 1))
                    tt(mF[s][:, :], bank[s][:, :], G[:, i * 2 + (s + KT), :], ALU.mult).then_inc(tile_dve, 1)
                    dve.wait_ge(tile_dve, i * 2 + (TD["nsa"] + s + 1))
                    tt(mF[s][:, :], mF[s][:, :], G[:, i * 2 + s, :], ALU.add).then_inc(mf_ready, 1)
                    dve.wait_ge(mhi_ready, i * 2 + (s + 1))
                    tt(mLo[:, i * 2 + s, :], mF[s][:, :], mHi[:, i * 2 + s, :].bitcast(F32), ALU.subtract).then_inc(
                        mlo_ready, 1)
            for j in range(4):
                dve.wait_ge(memhi_ready, j + 1)
                tt(memLo[:, 2 * j:2 * j + 2, :], bank[2 + j][:, :].rearrange("p (k n) -> p k n", k=2),
                   memHi[:, 2 * j:2 * j + 2, :].bitcast(F32), ALU.subtract).then_inc(memlo_ready, 1)

            def residual(name):
                b0 = BLOCKS[name]
                with dve.Fori(0, 4) as i:
                    for s in range(2):
                        dve.wait_ge(w_used, i * 2 + (b0 + s + 1))
                        dve.scalar_tensor_tensor(out=hF[:, i * 2 + s, :], in0=hF[:, i * 2 + s, :], scalar=ALPHA,
                                                 in1=bank[s][:, :], op0=ALU.mult, op1=ALU.add).then_inc(tile_dve, 1)

            def centre(n, centred):
                dve.wait_ge(mu_ready, n)
                for m in range(KT):
                    tt(centred[:, m, :], hF[:, m, :], bank[6][:, :], ALU.subtract).then_inc(xc_ready, 1)

            def scale(n, centred, rs):
                dve.wait_ge(var_done, n)
                dve.tensor_scalar(rs[:, :], bank[7][:, :], EPS, None, ALU.add).then_inc(var_ready, 1)
                dve.wait_ge(sd_ready, n)
                link(dve.reciprocal(rs[:, :], rs[:, :]))
                for m in range(KT):
                    tt(centred[:, m, :], centred[:, m, :], rs[:, :], ALU.mult).then_inc(nrm_ready, 1)

            residual("wout")
            centre(1, xc)
            b0 = BLOCKS["xk"]
            with dve.Fori(0, 4) as i:
                for s in range(2):
                    dve.wait_ge(w_used, i * 2 + (b0 + s + 1))
                    dve.tensor_copy(kxT[:, i * 2 + s, :], bank[s][:, 0:MEM]).then_inc(tile_dve, 1)
            scale(1, xc, rstd)
            dve.wait_ge(w_used, BLOCKS["xv"] + 8)
            for a in range(2):
                for half in range(2):
                    last = dve.tensor_copy(vx[:, a, 512 * half:512 * half + 512], bank[2 + 2 * a + half][:, :])
            last.then_inc(xv_ready, 1)
            b0 = BLOCKS["xq"]
            with dve.Fori(0, 4) as i:
                for s in range(2):
                    dve.wait_ge(w_used, i * 2 + (b0 + s + 1))
                    dve.tensor_scalar(qx[:, i * 2 + s, :], bank[s][:, :], (D // XH) ** -0.5, None, ALU.mult).then_inc(
                        tile_dve, 1)

            def xo_lo(h):
                for dt in range(2):
                    dve.wait_ge(xohi_ready, 2 * h + dt + 1)
                    tt(mLo[:, 2 * h + dt, :], bank[6 + dt][:, :], mHi[:, 2 * h + dt, :].bitcast(F32),
                       ALU.subtract).then_inc(xolo_ready, 1)

            NX = 4 * XH
            for n in range(NX + 3):
                if n < NX:
                    dve.wait_ge(xs_done, n + 1)
                    dve.tensor_reduce(xmax[:, n % 4:n % 4 + 1], bank[2 + n % 2][:, 0:MEM], AX.X, ALU.max,
                                      negate=True).then_inc(xmax_ready, 1)
                a = n - 1
                if 0 <= a < NX:
                    dve.wait_ge(xexp_done, a + 1)
                    link(dve.reciprocal(rinv[:, a % 4:a % 4 + 1], xsum[:, a % 4:a % 4 + 1]))
                    dve.tensor_scalar(xP[a % 2][:, :], xP[a % 2][:, :], rinv[:, a % 4:a % 4 + 1], None,
                                      ALU.mult).then_inc(xp_ready, 1)
                c = n - 2
                if 0 <= c < NX:
                    h, qi = c // 4, c % 4
                    dve.wait_ge(xt_done, c + 1)
                    if h >= 2:
                        dve.wait_ge(xo_done, 2 * (h - 1))
                    dve.tensor_copy(xPT[h % 2][:, :, P * qi:P * qi + P], bank[4 + c % 2][:, 0:MEM].rearrange(
                        "p (k n) -> p k n", k=2)).then_inc(xpt_ready, 1)
                if n % 4 == 2 and n >= 6:
                    xo_lo(n // 4 - 1)
            residual("xo")
            centre(2, xc)
            scale(2, xc, rstd)

            b0 = BLOCKS["fin"]
            with dve.Fori(0, KF // 2) as i:
                for t in range(2):
                    dve.wait_ge(w_used, i * 4 + (b0 + 2 * t + 2))
                    dve.wait_ge(sg_ready, i * 2 + (t + 1))
                    tt(sF[t][:, :], sg[t][:, :], bank[2 * t + 1][:, :], ALU.mult).then_inc(sf_ready, 1)
                    dve.wait_ge(shi_ready, i * 2 + (t + 1))
                    tt(sLo[:, i * 2 + t, :], sF[t][:, :], sHi[:, i * 2 + t, :].bitcast(F32), ALU.subtract).then_inc(
                        slo_ready, 1)
            dve.wait_ge(fout_done, 1)
            for m in range(KT):
                dve.scalar_tensor_tensor(out=hF[:, m, :], in0=hF[:, m, :], scalar=ALPHA, in1=bank[m][:, :],
                                         op0=ALU.mult, op1=ALU.add).then_inc(tile_dve, 1)
            centre(3, xc3)
            scale(3, xc3, rstd3)
            for a in range(4):
                dve.wait_ge(out_turned, 2 * a + 2)
                dve.tensor_copy(otok[a][:, 512:1024], bank[2 * (a % 2) + 1][:, :]).then_inc(out_copied_d, 1)

        @block.tensor
        def _(pe):
            def mm(o, w, a, start, stop):
                return pe.matmul(o, w, a, start=start, stop=stop)

            def mm3(o, w_hi, w_lo, a_hi, a_lo, start, stop):
                mm(o, w_hi, a_hi, start, False)
                mm(o, w_hi, a_lo, False, False)
                return mm(o, w_lo, a_hi, False, stop)

            def tile_stage(name, a_hi, a_lo, freed, base, n=T):
                b0 = BLOCKS[name]
                count = dict(STAGES)[name]
                with pe.Fori(0, count // 2) as i:
                    for s in range(2):
                        pe.wait_ge(w_lo_ready, i * 2 + (b0 + s + 1))
                        pe.wait_ge(freed, i * 2 + (base + s - 1))
                        for k in range(KT):
                            w = slice(P * k, P * k + P)
                            last = mm3(bank[s][:, 0:n], whi[s][:, w], wlo[s][:, w], a_hi[:, k, :], a_lo[:, k, :],
                                       k == 0, k == KT - 1)
                        last.then_inc(w_used, 1)

            pe.wait_ge(ident_ready, 1)
            pe.wait_ge(par_landed, 48)
            pe.wait_ge(dt_ready, 1)
            for i in range(3):
                last = pe.transpose(bank[6][:, NGP * i:NGP * i + NGP], araw[i][:, :, :].rearrange("g q n -> g (q n)"),
                                    ident[0:NGP, 0:NGP])
            last.then_inc(par_turned, 1)
            pe.wait_ge(vec_landed, 16 * 12)
            pe.transpose(bank[7][:, 0:72], vrows[:, :], ident[0:72, 0:72])
            pe.transpose(bank[7][0:GC, 128:128 + NG], dl[:, :], ident[0:NG, 0:NG])
            for z in range(2):
                last = pe.transpose(bank[7][:, 160 + 16 * z:176 + 16 * z], posl[:, z, :], ident[0:16, 0:16])
            last.then_inc(vec_turned, 1)
            pe.wait_ge(xn_ready, 4)
            for k in range(KT):
                if k >= 2:
                    pe.wait_ge(hf0_ready, k - 1)
                for a in range(4):
                    last = pe.transpose(bank[k % 2][:, P * a:P * a + P], xtok[:, a, P * k:P * k + P], ident[:, :])
                last.then_inc(h0_turned, 1)
            pe.wait_ge(vec_ready, 1)
            pe.wait_ge(rep_ready, 1)
            mm(bank[6][:, 0:NG], rep16[:, :, :].rearrange("p j c -> p (j c)"), dT[:, :], True, True).then_inc(dcol_done, 1)
            pe.wait_ge(c_landed, 64)
            for ri in range(2):
                for t in range(4):
                    last = pe.transpose(bank[4 + ri][:, P * t:P * t + P], Craw[:, ri, t, :, :].rearrange("p d n -> p (d n)"),
                                        ident[:, :])
                last.then_inc(ct_turned, 1)
            pe.wait_ge(hlo_ready, KT)
            tile_stage("gmixa", hHi, hLo, tile_act, 2)
            pe.wait_ge(ct_ready, 2)
            for b in range(4):
                s = b % 2
                pe.wait_ge(w_lo_ready, BLOCKS["u"] + b + 1)
                for kk in range(2):
                    k = 2 * b + kk
                    w = slice(512 * kk, 512 * kk + 512)
                    for r in range(4):
                        a_hi, a_lo = hHi[:, k, r:T:4], hLo[:, k, r:T:4]
                        last = mm3(bank[2 + r][:, :], a_hi, a_lo, whi[s][:, w], wlo[s][:, w], k == 0, k == KT - 1)
                last.then_inc(w_used, 1)
            pe.wait_ge(pw_ready, 1)
            pe.wait_ge(cbd_ready, 1)
            for gp in range(NGP):
                for ri in range(2):
                    last = mm(bank[6][:, 2 * GC * gp:2 * GC * gp + 2 * GC], Pw[:, ri, gp].rearrange("p j c -> p (j c)"),
                              Cbd[:, ri, gp, :, :], ri == 0, ri == 1)
            last.then_inc(m_built, 1)
            pe.wait_ge(o_ready, 2)
            for j in range(8):
                if j == 1:
                    pe.wait_ge(m7_ready, 1)
                if j >= 2:
                    pe.wait_ge(wst_ready, j - 1)
                for e in range(4):
                    src = Pw[:, j // 4, 4 * (j % 4) + e].rearrange("p j c -> p (j c)")
                    last = pe.transpose(bank[7 - j % 2][:, P * e:P * e + P], src, ident[:, :])
                last.then_inc(wst_turned, 1)
            pe.wait_ge(wst_ready, 8)
            pe.wait_ge(u1_moved, 32)
            for j in range(4):
                for g in range(8 * j, 8 * j + 8):
                    last = pe.transpose(bank[2 + j][:, NCH * (g % 8):NCH * (g % 8) + NCH],
                                        U8[:, g, :, :].rearrange("p j c -> p (j c)"), ident[0:NCH, 0:NCH])
                last.then_inc(ut_turned, 1)
            pe.wait_ge(ut_ready, 4)
            for j in range(4):
                for gp in range(8 * (j % 2), 8 * (j % 2) + 8):
                    for q in range(2):
                        last = mm(bank[2 + j][64 * q:64 * q + 64, NCH * (gp % 8):NCH * (gp % 8) + NCH],
                                  Wst[:, j // 2, gp, 64 * q:64 * q + 64], UT[:, 2 * gp + q, :], True, True)
                last.then_inc(s_done, 1)
            tile_stage("gmixb", hHi, hLo, tile_act, 2 + 4)
            pe.wait_ge(scan_done, 1)
            pe.wait_ge(m_moved, 16 * (CH - 1))
            for q in range(4):
                if q >= 2:
                    pe.wait_ge(y_ready, 2 * (q - 1))
                for e in range(8):
                    g = 8 * q + e
                    gp, half = g // 2, slice(64 * (g % 2), 64 * (g % 2) + 64)
                    o = bank[2 + 2 * (q % 2) + e % 2][0:64, P * (e // 2):P * (e // 2) + P]
                    mm(o, UT[:, g, :], Mst[:, :, g, :], True, False)
                    for ri in range(2):
                        last = mm(o, H[half, ri, gp, 0:NCH], Ost[half, ri, gp].rearrange("p j c -> p (j c)"),
                                  False, ri == 1)
                last.then_inc(y_done, 1)
            pe.wait_ge(y_ready, 8)
            for ct in range(4):
                for j in range(8):
                    last = pe.transpose(bank[2 + ct][:, NCH * j:NCH * j + NCH], Yt[:, j, P * ct:P * ct + P],
                                        ident[0:NCH, 0:NCH])
                last.then_inc(yt_turned, 1)
            tile_stage("gmixc", hHi, hLo, tile_act, 2 + 12)
            pe.wait_ge(glo_ready, 4)
            for b in range(2):
                pe.wait_ge(w_lo_ready, BLOCKS["glu"] + b + 1)
                for kk in range(2):
                    for m in range(4):
                        w = slice(512 * kk + P * m, 512 * kk + P * m + P)
                        k = 2 * b + kk
                        last = mm3(bank[2 + m][:, :], whi[b][:, w], wlo[b][:, w], gHi[:, k, :], gLo[:, k, :],
                                   k == 0, k == 3)
                last.then_inc(w_used, 1)
            tile_stage("gmixd", hHi, hLo, tile_act, 2 + 14)
            pe.wait_ge(ylo_ready, 4)
            pe.wait_ge(tile_act, 2 + 16)
            for t in range(KT):
                b = BLOCKS["sso"] + t // 2
                s = b % 2
                pe.wait_ge(w_lo_ready, b + 1)
                if t >= 2:
                    pe.wait_ge(tile_dve, TD["sso"] + t - 1)
                for k in range(4):
                    w = slice(256 * k + P * (t % 2), 256 * k + P * (t % 2) + P)
                    last = mm3(bank[t % 2][:, :], whi[s][:, w], wlo[s][:, w], yHi[:, k, :], yLo[:, k, :], k == 0, k == 3)
                last.then_inc(w_used if t % 2 else sso_tile, 1)
            for b in range(4):
                s = (BLOCKS["v"] + b) % 2
                pe.wait_ge(w_lo_ready, BLOCKS["v"] + b + 1)
                for kk in range(2):
                    k = 2 * b + kk
                    w = slice(512 * kk, 512 * kk + 512)
                    for a in range(4):
                        tok = slice(P * a, P * a + P)
                        last = mm3(bank[2 + a][:, :], hHi[:, k, tok], hLo[:, k, tok], whi[s][:, w], wlo[s][:, w],
                                   k == 0, k == KT - 1)
                last.then_inc(w_used, 1)
            tile_stage("kq", hHi, hLo, tile_dve, TD["kq"])
            pe.wait_ge(w1_landed, 6 * 16)
            for a in range(4):
                for k in range(KT):
                    last = mm(bank[6][:, 48 * a:48 * a + 48], hF[:, k, P * a:P * a + P], wg[:, k, :], k == 0, k == KT - 1)
            last.then_inc(gate_done, 1)
            pe.wait_ge(xc_landed, 8 * 16)
            pe.wait_ge(pos_ready, 1)
            pe.wait_ge(v_ready, 4)
            for j in range(4):
                for r in range(16):
                    last = mm(bank[2 + j][:, 0:(NKV + 1) * NCMP], w1[:, j // 2, r, P * (j % 2):P * (j % 2) + P],
                              Xc[:, j // 2, :, 2 * r:2 * r + 16 * (NCMP - 1) + 1:16], r == 0, r == 15)
                last.then_inc(hid_done, 1)
            pe.wait_ge(hid_ready, 4)
            pe.wait_ge(hid_padded, 1)
            pe.wait_ge(gate_ready, 1)
            for kk in range(2):
                last = mm(bank[6][:, 0:P], w2[:, 0, kk, :], hidK[:, kk, :, :], kk == 0, kk == 1)
            last.then_inc(kc_done, 1)
            for h in range(NKV):
                for kk in range(2):
                    last = mm(bank[7][:, HD * h:HD * h + HD], hidV[:, kk, h, :, :].rearrange("p g n -> p (g n)"),
                              w2[:, 1, kk, 0:HD], kk == 0, kk == 1)
            last.then_inc(vc_done, 1)

            def compressed_scores(qi):
                if qi >= 1:
                    pe.wait_ge(ptc_ready, qi)
                for m in range(8):
                    last = mm(bank[7][:, 64 * m:64 * m + 64], qT[:, m, P * qi:P * qi + P], kcT[:, m // 2, :, :], True, True)
                last.then_inc(cscore_done, 1)

            def compressed_turn(qi):
                pe.wait_ge(csum_ready, qi + 1)
                for kv in range(NKV):
                    last = pe.transpose(bank[7][:, P * kv:P * kv + P], Tc[:, 4 * kv:4 * kv + 4, :].rearrange(
                        "p h n -> p (h n)"), ident[:, :])
                last.then_inc(cturned, 1)

            pe.wait_ge(kc_ready, 1)
            pe.wait_ge(vc_ready, 1)
            pe.wait_ge(tile_dve, TD["nsa"])
            compressed_scores(0)
            pe.wait_ge(ks_landed, 32)
            for u in range(UNITS + PV):
                if u < UNITS:
                    m, br, e, qi = unit(u)
                    if u >= 3:
                        pe.wait_ge(max_done, u - 2)
                    half, kv = slice(64 * e, 64 * e + 64), m // 2
                    keys = kT if kv % 2 == e else kS
                    mm(bank[SCORE_BANKS[u % 3]][:, 0:P * (qi + 1)], qT[half, m, P * qi:P * qi + P],
                       keys[half, 2 * br + kv // 2, 0:P * (qi + 1)], True, True).then_inc(score_done, 1)
                if u == 1:
                    compressed_turn(0)
                if u // 32 < 3:
                    if u % 32 == CMP_SCORE:
                        compressed_scores(u // 32 + 1)
                    elif u % 32 == CMP_TURN:
                        compressed_turn(u // 32 + 1)
                v = u - TURN
                if 0 <= v < UNITS:
                    qi = unit(v)[3]
                    pe.wait_ge(exp_done, v + 1)
                    pe.wait_ge(diag_ready, v + 1)
                    if v >= 2:
                        pe.wait_ge(turned_act if v % 2 else turned_dve, v // 2)
                    for kt in range(qi + 1):
                        last = mm(bank[2 + v % 2][:, P * kt:P * kt + P], Sr[v % 8][:, P * kt:P * kt + P],
                                  diag[v % 4][:, :], True, True)
                    last.then_inc(turned, 1)
                w = u - PV
                if 0 <= w < UNITS and w % 2 == 1:
                    m, br, _, qi = unit(w)
                    pe.wait_ge(turned_dve, w // 2 + 1)
                    pe.wait_ge(turned_act, w // 2 + 1)
                    c, vcol = P * (m % 4), 256 * br + HD * (m // 2)
                    if w % 16 == 1 and w > 32:
                        pe.wait_ge(ohi_ready, w // 16 - 1)
                        pe.wait_ge(olo_ready, w // 16 - 1)
                    if br == 0:
                        pe.wait_ge(ptc_ready, qi + 1)
                        for e in range(2):
                            mm(bank[4 + w // 16 % 2][64 * e:64 * e + 64, c:c + P], Vbd[:, m // 2, (2 * m + e) % 4, :],
                               PTc[qi % 2][:, m // 2, :], True, False)
                    for kt in range(qi + 1):
                        for e in range(2):
                            last = mm(bank[4 + w // 16 % 2][64 * e:64 * e + 64, c:c + P], VA[:, kt, vcol:vcol + HD],
                                      PTr[(w - 1 + e) % 4][:, P * kt:P * kt + P], False, br == 1 and kt == qi)
                    last.then_inc(pv_done, 2)

            pe.wait_ge(olo_ready, 8)
            tile_stage("nsa", hHi, hLo, tile_dve, TD["nsa"])
            pe.wait_ge(mem_landed, 16)
            for j in range(4):
                for kk in range(2):
                    for a in range(2):
                        c = 256 * kk + P * a
                        last = pe.transpose(bank[2 + j][:, c:c + P], memF[:, a, P * (2 * j + kk):P * (2 * j + kk) + P],
                                            ident[:, :])
                last.then_inc(mem_turned, 1)
            pe.wait_ge(mlo_ready, KT)
            tile_stage("wout", mHi, mLo, tile_dve, TD["wout"])

            def mean(n, residual_tiles):
                pe.wait_ge(pool_const, 1)
                pe.wait_ge(tile_dve, residual_tiles)
                for m in range(KT):
                    last = mm(bank[6][:, :], mean_w[:, :], hF[:, m, :], m == 0, m == KT - 1)
                last.then_inc(mu_ready, 1)

            def variance(n):
                for m in range(KT):
                    pe.wait_ge(sq_ready, KT * (n - 1) + m + 1)
                    last = mm(bank[7][:, :], mean_w[:, :], sq[:, m, :], m == 0, m == KT - 1)
                last.then_inc(var_done, 1)

            mean(1, TD["xk"])
            pe.wait_ge(memlo_ready, 4)
            tile_stage("xk", memHi, memLo, tile_dve, TD["xk"], MEM)
            variance(1)
            for k in range(KT):
                s = k % 2
                pe.wait_ge(w_lo_ready, BLOCKS["xv"] + k + 1)
                for a in range(2):
                    tok = slice(P * a, P * a + P)
                    for half in range(2):
                        w = slice(512 * half, 512 * half + 512)
                        last = mm3(bank[2 + 2 * a + half][:, :], memHi[:, k, tok], memLo[:, k, tok], whi[s][:, w],
                                   wlo[s][:, w], k == 0, k == KT - 1)
                last.then_inc(w_used, 1)
            pe.wait_ge(hlo_ready, 2 * KT)
            tile_stage("xq", hHi, hLo, tile_dve, TD["xq"])
            pe.wait_ge(xv_ready, 1)
            pe.wait_ge(tile_dve, TD["xo"])
            NX = 4 * XH
            for n in range(NX + 3):
                if n < NX:
                    h, qi = n // 4, n % 4
                    if n >= 2:
                        pe.wait_ge(xexp_done, n - 1)
                    for kk in range(2):
                        last = mm(bank[2 + n % 2][:, 0:MEM], qx[:, 2 * h + kk, P * qi:P * qi + P], kxT[:, 2 * h + kk, :],
                                  kk == 0, kk == 1)
                    last.then_inc(xs_done, 1)
                c = n - 2
                if 0 <= c < NX:
                    pe.wait_ge(xp_ready, c + 1)
                    if c >= 2:
                        pe.wait_ge(xpt_ready, c - 1)
                    for kt in range(2):
                        last = pe.transpose(bank[4 + c % 2][:, P * kt:P * kt + P], xP[c % 2][:, P * kt:P * kt + P],
                                            ident[:, :])
                    last.then_inc(xt_done, 1)
                if n % 4 == 2 and n >= 6:
                    h = n // 4 - 1
                    pe.wait_ge(xpt_ready, 4 * h + 4)
                    if h >= 1:
                        pe.wait_ge(xohi_ready, 2 * h)
                        pe.wait_ge(xolo_ready, 2 * h)
                    for dt in range(2):
                        for kt in range(2):
                            c0 = 256 * h + P * dt
                            last = mm(bank[6 + dt][:, :], vx[:, kt, c0:c0 + P], xPT[h % 2][:, kt, :], kt == 0, kt == 1)
                        last.then_inc(xo_done, 1)
            pe.wait_ge(xolo_ready, KT)
            tile_stage("xo", mHi, mLo, tile_dve, TD["xo"])
            mean(2, TD["fout"])
            variance(2)
            pe.wait_ge(hlo_ready, 3 * KT)
            b0 = BLOCKS["fin"]
            with pe.Fori(0, KF // 2) as i:
                for t in range(2):
                    pe.wait_ge(sf_ready, i * 2 + (t + 1))
                    for s in range(2):
                        pe.wait_ge(w_lo_ready, i * 4 + (b0 + 2 * t + s + 1))
                        for k in range(KT):
                            w = slice(P * k, P * k + P)
                            last = mm3(bank[2 * t + s][:, :], whi[s][:, w], wlo[s][:, w], hHi[:, k, :], hLo[:, k, :],
                                       k == 0, k == KT - 1)
                        last.then_inc(w_used, 1)
            pe.wait_ge(slo_ready, KF)
            b0 = BLOCKS["fout"]

            def down(k, s, start, stop, done):
                pe.wait_ge(w_lo_ready, k + (b0 + 1))
                for m in range(KT):
                    w = slice(P * m, P * m + P)
                    last = mm3(bank[m][:, :], whi[s][:, w], wlo[s][:, w], sHi[:, k, :], sLo[:, k, :], start, stop)
                last.then_inc(done, 1)

            for s in range(2):
                down(s, s, s == 0, False, w_used)
            with pe.Fori(1, KF // 2 - 1) as i:
                for s in range(2):
                    down(i * 2 + s, s, False, False, w_used)
            down(KF - 2, 0, False, False, w_used)
            down(KF - 1, 1, False, True, fout_done)
            mean(3, TD_END)
            variance(3)
            pe.wait_ge(hf_ready, 3 * KT)
            for a in range(4):
                for half in range(2):
                    if a >= 2:
                        pe.wait_ge(out_copied_d if half else out_copied_a, a - 1)
                    for kk in range(4):
                        last = pe.transpose(bank[2 * (a % 2) + half][:, P * kk:P * kk + P],
                                            hF[:, 4 * half + kk, P * a:P * a + P], ident[:, :])
                    last.then_inc(out_turned, 1)


_INS = ['x', 'mem', 'ln_emb_g', 'ln_emb_b', 'w_in', 'ssm_a_re', 'ssm_a_im', 'ssm_b_re', 'ssm_b_im', 'ssm_c_re',
        'ssm_c_im', 'ssm_d', 'ssm_log_dt', 'ssm_w_glu', 'ssm_b_glu', 'ssm_w_out', 'cmp_pos', 'cmp_w1', 'cmp_b1',
        'cmp_w2', 'nsa_w_out', 'w_out', 'ln1_g', 'ln1_b', 'xattn_w_q', 'xattn_w_kv', 'xattn_w_o', 'ln2_g', 'ln2_b',
        'ffn_w_in', 'ffn_w_out', 'ln3_g', 'ln3_b']


def kernel(**inputs):
    import numpy as np
    import concourse.bacc as bacc
    from concourse.bass_utils import run_bass_kernel_spmd as run

    nc = bacc.Bacc("TRN2", target_bir_lowering=False, num_devices=1)
    arrays, tensors = {}, {}
    for name in _INS:
        a = np.ascontiguousarray(inputs[name])
        arrays[f"in_{name}"] = a
        tensors[name] = nc.dram_tensor(f"in_{name}", a.shape, mybir.dt.from_np(a.dtype), kind="ExternalInput").ap()
    out = nc.dram_tensor("out_0", (1, T, D), F32, kind="ExternalOutput").ap()
    build(nc, tensors, out)
    r = run(nc, [arrays], core_ids=[0])
    return r.results[0]["out_0"]
```

```python
import math
from contextlib import ExitStack

import concourse.bass as bass
from concourse import mybir

ALU = mybir.AluOpType
ACT = mybir.ActivationFunctionType
AX = mybir.AxisListType
F32 = mybir.dt.float32
F32R = mybir.dt.float32r

P = 128
D = 1024
T = 512
KT = D // P
MEM = 256
NG, GC, NS = 32, 16, 64
NGP = NG // 2
CH = 8
NCH = T // CH
NH, NKV, HD = 16, 4, 64
NCMP = 31
DFF = 2816
KF = DFF // P
XH = 4
ALPHA = 2.0 ** 0.25
EPS = 1e-5
MASKED = -1e30
MAX_FLOOR = -1e25
SLOPES = [2.0 ** (-8.0 * (h + 1) / NH) for h in range(NH)]
TWO_PI = 2 * math.pi
PI_A = 6.28125
PI_B = 0.0019340515136719
PI_C = TWO_PI - PI_A - PI_B
ROUND = 1.5 * 2.0 ** 23

C_U, C_Q, C_KVC, C_KVS, C_KVW, C_GN, C_GM = 0, 512, 1536, 2048, 2560, 3072, 3120

STAGES = [("gmixa", 4), ("u", 4), ("gmixe", 2), ("gmixb", 6), ("gmixc", 2), ("glu", 2), ("gmixd", 2),
          ("sso", 4), ("v", 4), ("kvc", 4), ("q", 8), ("k", 4), ("nsa", 8), ("wout", 8),
          ("xk", 8), ("xv", 8), ("xq", 8), ("xo", 8), ("fin", 2 * KF), ("fout", KF)]
BLOCKS = {}
UNITS = 4 * NH * 2
SCORE_BANKS = (0, 1, 6)
XSCORE_BANKS, XTURN = (2, 3, 0, 1), 3
LAST_ORDER = (0, 2, 4, 6, 1, 3, 5, 7)
TURN, PV = 5, 7
O_STEP = 8
CMP_SCORE, CMP_EXP, CMP_SUM, CMP_TURN, CMP_COPY = 16, 19, 21, 25, 26
FIRST_SUM, FIRST_TURN, FIRST_COPY = 2, 5, 6


def unit(u):
    return 4 * (u // 16 % 2) + u % 16 // 4, u // 2 % 2, u % 2, u // 32


_at = 0
for _n, _c in STAGES:
    BLOCKS[_n] = _at
    _at += _c
NBLOCKS = _at


def build(nc, I, out):
    KB = 1024
    BASE = 16512
    RG = 72 * KB
    RX = 104 * KB
    RC = 202 * KB

    def at(name, shape, off, dt=F32):
        return nc.alloc_sbuf_tensor_at(name, shape, dt, offset=BASE + int(off))

    wraw = [at(f"wraw{r}", [P, 1024], r * 4 * KB) for r in range(4)]
    wlo = [at(f"wlo{r}", [P, 1024], r * 4 * KB, F32R) for r in range(4)]
    whi = [at(f"whi{s}", [P, 1024], (16 + s * 4) * KB, F32R) for s in range(2)]
    hF = at("hF", [P, KT, T], 24 * KB)
    hHi = at("hHi", [P, KT, T], 40 * KB, F32R)
    hLo = at("hLo", [P, KT, T], 56 * KB, F32R)
    G = at("G", [P, 2 * KT, T], RG)
    ident = at("ident", [P, P], RC)
    mean_w = at("mean_w", [P, P], RC + 512)
    vecT = at("vecT", [P, 72], RC + 1024)
    ET = at("ET", [P, 2, 8, NGP], RC + 1536)
    gates = at("gates", [P, 4, 3 * NH], RC + 3072)
    cdist = at("cdist", [P, 4, 32], RC + 3840)
    c2 = RC + 4352
    slope_row = at("slope_row", [P, NH], c2)
    qscale = at("qscale", [P, 8], c2 + 1248)
    posT = at("posT", [P, 2, 16], c2 + 64)
    hidb = at("hidb", [P, 4], c2 + 192)
    Dcol = at("Dcol", [P, NG], c2 + 224)
    nmax = at("nmax", [P, 8], c2 + 352)
    sums = at("sums", [P, 2, 3, NH], c2 + 384)
    cmax = at("cmax", [P, NH], c2 + 768)
    wcmp = at("wcmp", [P, NH], c2 + 832)
    winv = at("winv", [P, 4, 2], RC + 2560)
    xmax = at("xmax", [P, 4], c2 + 928)
    xsum = at("xsum", [P, 4], c2 + 960)
    bnst = at("bnst", [P, 4, 2, 6], c2 + 992)
    bnmv = at("bnmv", [P, 4, 2], c2 + 1184)
    rinv = at("rinv", [P, 4], c2 + 1216)

    xtok = at("xtok", [P, 4, D], RX + 16 * KB)
    araw = [at(f"araw{i}", [NGP, 2, NS], RX + 96 * KB + i * 512) for i in range(3)]
    ldt = at("ldt", [NGP, 2], RX + 97 * KB + 512)
    vrows = at("vrows", [72, P], RX + 73 * KB)
    dl = at("dl", [NG, GC], RX + 73 * KB + 512)
    posl = at("posl", [16, 2, P], RX + 74 * KB)
    rep16 = at("rep16", [GC, 8, GC], RX + 75 * KB)
    dT = at("dT", [GC, NG], RX + 75 * KB + 512)
    LP = at("LP", [P, 2, 8, NGP], RX + 89 * KB)
    LD = at("LD", [P, 2, 8, NGP], RX + 90 * KB)
    FP = at("FP", [P, 2, 8, NGP], RX + 91 * KB)
    cm = [at(f"cm{i}", [P, 8, NGP], RX + 92 * KB + i * 512) for i in range(4)]
    sp = {n: at("sp_" + n, [P, NGP], RX + 94 * KB + i * 64) for i, n in enumerate(
        ["are", "aim", "dt", "th", "er", "k", "s", "s2", "den", "nr", "fr", "fi", "a", "b", "c", "d"])}
    Bt = at("Bt", [P, 2, NGP, GC], RX)
    Craw = at("Craw", [P, 2, 4, 2, NS], RX + 2 * KB)
    Ct = at("Ct", [P, 2, NGP, GC], RX + 6 * KB)
    Cbd = at("Cbd", [P, 2, NGP, 2, GC], RX + 8 * KB)
    Wst = at("Wst", [P, 2, NGP, P], RX)
    Mst = at("Mst", [P, CH, NG, GC], RX + 16 * KB)
    Ost = at("Ost", [P, 2, NGP, CH, GC], RX + 32 * KB)
    H = at("H", [P, 2, NGP, NCH + 1], RX + 48 * KB)
    Ptmp = at("Ptmp", [P, NGP, CH, GC], RX + 48 * KB)
    UT = at("UT", [P, NG, NCH], RX + 57 * KB)
    U1 = at("U1", [P, NG, 4, GC], RX + 57 * KB)
    Pw = at("Pw", [P, 2, NGP, CH, GC], RX + 65 * KB)
    Otmp = at("Otmp", [P, NGP, CH, GC], RX + 57 * KB)
    U8 = at("U8", [NCH, NG, CH, GC], RX + 81 * KB)
    st1 = at("st1", [P, 2, NGP, 8], RX + 65 * KB)
    st2 = at("st2", [P, 2, NGP, 8], RX + 66 * KB)
    Yt = at("Yt", [NCH, 8, 512], RX + 65 * KB)
    gF = at("gF", [P, 4, T], RX)
    gHi = at("gHi", [P, 4, T], RX + 8 * KB, F32R)
    gLo = at("gLo", [P, 4, T], RX + 16 * KB, F32R)
    yF = at("yF", [P, 4, T], RX + 24 * KB)
    yHi = at("yHi", [P, 4, T], RX + 32 * KB, F32R)
    yLo = at("yLo", [P, 4, T], RX + 40 * KB, F32R)
    kqT = at("kqT", [P, 16, T], RX)
    qT, kvcT, kT = kqT[:, 0:8, :], kqT[:, 8:12, :], kqT[:, 12:16, :]
    gateT = kqT[0:3 * NH, 15, :]
    VA = at("VA", [P, 4, 512], RX + 32 * KB)
    Xc = at("Xc", [P, 2, NKV + 1, T], RX + 40 * KB)
    w1 = at("w1", [P, 2, 16, 256], RX + 60 * KB)
    w2 = at("w2", [P, 2, 2, 2 * HD], RX + 92 * KB)
    wg = at("wg", [P, KT, 3 * NH], RX + 94 * KB)
    hidK = at("hidK", [P, 2, NKV, 32], RX + 96 * KB)
    hidV = at("hidV", [P, 2, NKV, 4, 32], RX + 60 * KB)
    kS = at("kS", [P, 4, T], RX + 16 * KB)
    PTr = [at(f"PTr{i}", [P, T], RX + (40 + 2 * i) * KB) for i in range(4)]
    Tc = at("Tc", [P, NH, 32], RX + 54 * KB)
    dist = at("dist", [P, T], RX + 56 * KB)
    Sr = [at(f"Sr{i}", [P, T], RX + (64 + 2 * i) * KB) for i in range(8)]
    diag = [at(f"diag{i}", [P, P], RX + 80 * KB + 512 * i) for i in range(4)]
    kcT = at("kcT", [P, NKV, 2, 32], RX + 84 * KB)
    Vbd = at("Vbd", [P, NKV, 4, HD], RX + 88 * KB)
    PTc = [at(f"PTc{i}", [P, NKV, P], RX + (94 + 2 * i) * KB) for i in range(2)]
    mHi = at("mHi", [P, KT, T], RX, F32R)
    mLo = at("mLo", [P, KT, T], RX + 16 * KB, F32R)
    mF = [at(f"mF{i}", [P, T], RX + (32 + 2 * i) * KB) for i in range(2)]
    xc = at("xc", [P, KT, T], RX + 36 * KB)
    rstd = at("rstd", [P, T], RX + 52 * KB)
    hsum = at("hsum", [P, T], RX + 54 * KB)
    sq = at("sq", [P, KT, T], RG)
    memHi = at("memHi", [P, KT, MEM], RX + 58 * KB, F32R)
    memLo = at("memLo", [P, KT, MEM], RX + 66 * KB, F32R)
    memF = at("memF", [P, 2, D], RX + 74 * KB)
    kxT = at("kxT", [P, KT, MEM], RX + 82 * KB)
    vx = at("vx", [P, 2, D], RX + 90 * KB)
    qx = at("qx", [P, KT, T], RG)
    xP = [at(f"xP{i}", [P, MEM], RG + (16 + i) * KB) for i in range(4)]
    xPT = [at(f"xPT{i}", [P, 2, T], RG + (20 + 4 * i) * KB) for i in range(2)]
    sHi = at("sHi", [P, KF, T], RG, F32R)
    sLo = at("sLo", [P, KF, T], RG + 44 * KB, F32R)
    sg = [at(f"sg{i}", [P, T], RX + (56 + 2 * i) * KB) for i in range(2)]
    sF = [at(f"sF{i}", [P, T], RX + (60 + 2 * i) * KB) for i in range(2)]
    row3 = [at(f"row3{i}", [P, D], RX + (64 + 4 * i) * KB) for i in range(2)]
    st3 = at("st3", [P, 4, 2, 6], RX + 72 * KB)
    mv3 = at("mv3", [P, 4, 2], RX + 72 * KB + 192)
    sd3 = at("sd3", [P, 4], RX + 72 * KB + 224)
    shift3 = at("shift3", [P, 4], RX + 72 * KB + 256)
    otok = [at(f"otok{i}", [P, D], (40 + 4 * i) * KB) for i in range(4)]

    ctx = ExitStack()
    with ctx:
        def sem(name):
            return ctx.enter_context(nc.semaphore(name))

        bank = [ctx.enter_context(nc.psum_tensor(f"bank{i}", [P, 512], F32)) for i in range(8)]

        w_landed = [sem(f"w_landed{r}") for r in range(4)]
        w_hi_ready, w_lo_ready, w_used = sem("w_hi_ready"), sem("w_lo_ready"), sem("w_used")
        tile_act, tile_dve = sem("tile_act"), sem("tile_dve")
        hhi_ready, hlo_ready = sem("hhi_ready"), sem("hlo_ready")
        x_landed = [sem(f"x_landed{a}") for a in range(4)]
        par_landed, vec_landed = sem("par_landed"), sem("vec_landed")
        b_landed, c_landed, w1_landed = sem("b_landed"), sem("c_landed"), sem("w1_landed")
        xc_landed, mem_landed, u1_moved = sem("xc_landed"), sem("mem_landed"), sem("u1_moved")
        ident_ready, pool_const, dve_step = sem("ident_ready"), sem("pool_const"), sem("dve_step")
        pool_step = sem("pool_step")
        rep_ready, dt_ready, er_ready, mag_ready = (
            sem("rep_ready"), sem("dt_ready"), sem("er_ready"), sem("mag_ready"))
        angle_ready, sin_ready, par_turned = sem("angle_ready"), sem("sin_ready"), sem("par_turned")
        var0_ready, sd0_ready, xn_ready, h0_turned = (
            sem("var0_ready"), sem("sd0_ready"), sem("xn_ready"), sem("h0_turned"))
        hf0_ready = sem("hf0_ready")
        vec_turned, vec_ready, dcol_done = sem("vec_turned"), sem("vec_ready"), sem("dcol_done")
        ct_turned, ct_ready, m_zero = sem("ct_turned"), sem("ct_ready"), sem("m_zero")
        pw_ready, cbd_ready, o_ready = sem("pw_ready"), sem("cbd_ready"), sem("o_ready")
        m_built, m7_ready, m_moved, wst_turned, wst_ready = sem("m_built"), sem("m7_ready"), sem("m_moved"), sem("wst_turned"), sem("wst_ready")
        u1_ready, ut_turned, ut_ready = sem("u1_ready"), sem("ut_turned"), sem("ut_ready")
        s_done, h_loaded, scan_done = sem("s_done"), sem("h_loaded"), sem("scan_done")
        y_done, y_ready, yt_turned, gelu_done = sem("y_done"), sem("y_ready"), sem("yt_turned"), sem("gelu_done")
        ghi_ready, glo_ready = sem("ghi_ready"), sem("glo_ready")
        glu_sig, yf_ready, yhi_ready, ylo_ready = (
            sem("glu_sig"), sem("yf_ready"), sem("yhi_ready"), sem("ylo_ready"))
        sso_tile = sem("sso_tile")
        v_ready, gate_done, gate_ready = sem("v_ready"), sem("gate_done"), sem("gate_ready")
        gate_sig, gate_turned = sem("gate_sig"), sem("gate_turned")
        hid_done, hidb_ready, hid_ready, pos_ready = sem("hid_done"), sem("hidb_ready"), sem("hid_ready"), sem("pos_ready")
        hid_padded = sem("hid_padded")
        kc_done, kc_ready, vc_done, vc_ready = sem("kc_done"), sem("kc_ready"), sem("vc_done"), sem("vc_ready")
        dist_ready, ks_landed = sem("dist_ready"), sem("ks_landed")
        winv_ready, diag_ready = sem("winv_ready"), sem("diag_ready")
        score_done, max_done, exp_done, turned, turned_dve, turned_act, pv_done = (
            sem("score_done"), sem("max_done"), sem("exp_done"), sem("turned"), sem("turned_dve"),
            sem("turned_act"), sem("pv_done"))
        cscore_done, tc_ready, pc_ready, csum_ready, cturned, ptc_ready = (
            sem("cscore_done"), sem("tc_ready"), sem("pc_ready"), sem("csum_ready"), sem("cturned"),
            sem("ptc_ready"))
        ohi_ready, olo_ready = sem("ohi_ready"), sem("olo_ready")
        mf_ready, mhi_ready, mlo_ready = sem("mf_ready"), sem("mhi_ready"), sem("mlo_ready")
        mu_ready, xc_ready, sq_ready, var_done, var_ready, sd_ready, nrm_ready, hf_ready = (
            sem("mu_ready"), sem("xc_ready"), sem("sq_ready"), sem("var_done"), sem("var_ready"),
            sem("sd_ready"), sem("nrm_ready"), sem("hf_ready"))
        mem_turned, memhi_ready, memlo_ready, xv_ready = (
            sem("mem_turned"), sem("memhi_ready"), sem("memlo_ready"), sem("xv_ready"))
        xs_done, xmax_ready, xexp_done, xp_ready, xt_done, xpt_ready, xo_done, xohi_ready, xolo_ready = (
            sem("xs_done"), sem("xmax_ready"), sem("xexp_done"), sem("xp_ready"), sem("xt_done"),
            sem("xpt_ready"), sem("xo_done"), sem("xohi_ready"), sem("xolo_ready"))
        sg_ready, sf_ready, shi_ready, slo_ready, fout_done = (
            sem("sg_ready"), sem("sf_ready"), sem("shi_ready"), sem("slo_ready"), sem("fout_done"))
        hsum_ready, last_ready, tok_turned, row3_landed = (
            sem("hsum_ready"), sem("last_ready"), sem("tok_turned"), sem("row3_landed"))
        var3_ready, sd3_ready, shift3_ready, norm3_done, gain3_done = (
            sem("var3_ready"), sem("sd3_ready"), sem("shift3_ready"), sem("norm3_done"), sem("gain3_done"))
        out_ready, out_stored = [sem("out_ready0"), sem("out_ready1")], sem("out_stored")

        block = ctx.enter_context(nc.Block())

        w_in, wX = I["w_in"][0], {k: I[k][0] for k in (
            "ssm_w_glu", "ssm_w_out", "nsa_w_out", "w_out", "xattn_w_q", "xattn_w_kv", "xattn_w_o",
            "ffn_w_in", "ffn_w_out")}

        def rows(w):
            return w.rearrange("(k p) n -> p k n", p=P)

        TD = {"sso": 2, "kvc": 10, "q": 14, "k": 22, "nsa": 26, "wout": 34, "xk": 42, "xq": 50, "xo": 58, "fout": 66}

        def at_step(i, times, c):
            return c if i is None else i * times + c

        @block.sync
        def _(sp_):
            for a in range(4):
                sp_.dma_start(xtok[:, a, :], I["x"][0, a * P:(a + 1) * P, :]).then_inc(x_landed[a], 16)

            def load(c, i, dst, src):
                if i is not None or c >= 4:
                    sp_.wait_ge(w_used, at_step(i, 4, c - 3))
                for half in range(2):
                    sp_.dma_start(dst[half], src[half]).then_inc(w_landed[c % 4], 16)

            def by_k(c, src):
                nk = src.shape[1]
                dst = wraw[c % 4][:, :].rearrange("p (k n) -> p k n", k=nk)
                return [dst[:, 0:nk // 2], dst[:, nk // 2:nk]], [src[:, 0:nk // 2], src[:, nk // 2:nk]]

            def column_tile(c, i, w, c0):
                load(c, i, *by_k(c, rows(w)[:, :, bass.ds(c0, P)]))

            def row_tile(c, i, w, r0, c0):
                dst = [wraw[c % 4][:, 512 * e:512 * e + 512] for e in range(2)]
                load(c, i, dst, [w[bass.ds(r0, P), c0 + 512 * e:c0 + 512 * e + 512] for e in range(2)])

            def column_tiles(name, w, c0, tiles=None):
                b0 = BLOCKS[name]
                if tiles is None and dict(STAGES)[name] == 8:
                    with sp_.Fori(0, 2) as i:
                        for j in range(4):
                            column_tile(b0 + j, i, w, i * (4 * P) + (P * j + c0))
                else:
                    for t in tiles or range(dict(STAGES)[name]):
                        column_tile(b0 + t, None, w, P * t + c0)

            def row_tiles(name, w, c0):
                b0, count = BLOCKS[name], dict(STAGES)[name]
                with sp_.Fori(0, count // 4) as i:
                    for j in range(4):
                        row_tile(b0 + j, i, w, i * (4 * P) + P * j, c0)
                for t in range(count // 4 * 4, count):
                    row_tile(b0 + t, None, w, P * t, c0)

            column_tiles("gmixa", w_in, C_GM, tiles=(0, 1))
            sp_.dma_start(ldt[:, :], I["ssm_log_dt"][0].rearrange("(g q) -> g q", q=2)).then_inc(par_landed, 16)
            for i, name in enumerate(("ssm_a_re", "ssm_a_im")):
                sp_.dma_start(araw[i][:, :, :], I[name][0].rearrange("(g q) n -> g q n", q=2)).then_inc(par_landed, 16)
            for ri, name in enumerate(("ssm_b_re", "ssm_b_im")):
                sp_.dma_start(Bt[:, ri], I[name][0].rearrange("(g q) n c -> (q n) g c", q=2)).then_inc(b_landed, 16)
            for ri, name in enumerate(("ssm_c_re", "ssm_c_im")):
                for dup in range(2):
                    sp_.dma_start(Craw[:, ri, :, dup, :], I[name][0].rearrange("(t g) c n -> (g c) t n", t=4)).then_inc(
                        c_landed, 16)
            sp_.wait_ge(x_landed[3], 16)
            column_tiles("gmixa", w_in, C_GM, tiles=(2, 3))
            for b in range(4):
                c = BLOCKS["u"] + b
                load(c, None, *by_k(c, rows(w_in)[:, 2 * b:2 * b + 2, C_U:C_U + 512]))
            column_tiles("gmixe", w_in, C_GM + 4 * P)
            column_tiles("gmixb", w_in, C_GM + 6 * P, tiles=(0, 1))
            sp_.wait_ge(u1_ready, 1)
            sp_.wait_ge(o_ready, 1)
            sp_.wait_ge(pw_ready, 1)
            for half in range(2):
                sp_.dma_start(U8[:, :, 4 * half:4 * half + 4, :], U1[half:P:2, :, :, :]).then_inc(u1_moved, 16)
            sp_.wait_ge(m_zero, 1)
            sp_.wait_ge(m7_ready, 1)
            for j in range(CH - 1):
                sp_.dma_start(Mst[0:GC * (j + 1), j, :, :], Mst[GC * (7 - j):P, 7, :, :]).then_inc(m_moved, 16)
            column_tiles("gmixb", w_in, C_GM + 6 * P, tiles=(2, 3, 4, 5))
            column_tiles("gmixc", w_in, C_GM + 12 * P)
            for b in range(2):
                c = BLOCKS["glu"] + b
                load(c, None, *by_k(c, rows(wX["ssm_w_glu"])[:, 2 * b:2 * b + 2, :]))
            column_tiles("gmixd", w_in, C_GM + 14 * P)
            for b in range(4):
                c = BLOCKS["sso"] + b
                load(c, None, *by_k(c, rows(wX["ssm_w_out"])[:, :, 256 * b:256 * b + 256]))
            for b in range(4):
                c = BLOCKS["v"] + b
                dst = wraw[c % 4][:, :].rearrange("p (k z n) -> p z k n", k=2, z=2)
                src = [rows(w_in)[:, 2 * b:2 * b + 2, v + 256:v + 512] for v in (C_KVS, C_KVW)]
                load(c, None, [dst[:, 0], dst[:, 1]], src)
            column_tiles("kvc", w_in, C_KVC)
            column_tiles("q", w_in, C_Q, tiles=(0, 1, 2, 3))
            sp_.wait_ge(tile_dve, TD["q"])
            for z in range(2):
                for e in range(2):
                    src = kvcT[64 * e:64 * e + 64, 2 * z:2 * z + 2, :]
                    dst = Xc[:, z, e:NKV:2, :]
                    sp_.dma_start(dst[0:64], src).then_inc(xc_landed, 16)
                    sp_.dma_start(dst[64:128, :, 0:T - 1], src[:, :, 1:T]).then_inc(xc_landed, 16)
            column_tiles("q", w_in, C_Q, tiles=(4, 5, 6, 7))
            for t, v in enumerate((C_KVS, C_KVS + P, C_KVW, C_KVW + P)):
                column_tile(BLOCKS["k"] + t, None, w_in, v)
            sp_.wait_ge(tile_dve, TD["nsa"])
            sp_.wait_ge(xc_landed, 8 * 16)
            for e in range(2):
                sp_.dma_start(kS[64 * e:64 * e + 64, :, :], kT[64 - 64 * e:128 - 64 * e, :, :]).then_inc(ks_landed, 16)
            column_tiles("nsa", wX["nsa_w_out"], 0)
            column_tiles("wout", wX["w_out"], 0)
            column_tiles("xk", wX["xattn_w_kv"], 0)
            row_tiles("xv", wX["xattn_w_kv"], D)
            column_tiles("xq", wX["xattn_w_q"], 0)
            column_tiles("xo", wX["xattn_w_o"], 0)
            with sp_.Fori(0, KF // 2) as i:
                for j in range(4):
                    column_tile(BLOCKS["fin"] + j, i, wX["ffn_w_in"], i * (2 * P) + (P * (j // 2) + DFF * (j % 2)))
            row_tiles("fout", wX["ffn_w_out"], 0)
            for a in range(4):
                for half in range(2):
                    sp_.wait_ge(out_ready[half], a + 1)
                    c = slice(512 * half, 512 * half + 512)
                    sp_.dma_start(out[0, a * P:(a + 1) * P, c], otok[a][:, c]).then_inc(out_stored, 16)
            sp_.wait_ge(out_stored, 8 * 16)

        @block.scalar
        def _(act):
            for r0, name in ((0, "ln_emb_g"), (8, "ln_emb_b"), (16, "ln1_g"), (24, "ln1_b"), (32, "ln2_g"),
                             (40, "ln2_b"), (48, "ln3_g"), (56, "ln3_b")):
                v = I[name] if name.startswith("ln_emb") else I[name][0]
                act.dma_start(vrows[r0:r0 + 8, :], v.rearrange("(k p) -> k p", p=P)).then_inc(vec_landed, 16)
            act.dma_start(vrows[64:68, :], I["ssm_b_glu"][0].rearrange("(k p) -> k p", p=P)).then_inc(vec_landed, 16)
            act.dma_start(vrows[68:72, :], I["cmp_b1"][0].rearrange("z (k p) -> (z k) p", p=P)).then_inc(vec_landed, 16)
            act.dma_start(dl[:, :], I["ssm_d"][0].rearrange("(g c) -> g c", c=GC)).then_inc(vec_landed, 16)
            act.dma_start(posl[:, :, :], I["cmp_pos"][0].rearrange("z (r q) d -> r z (q d)", q=2)).then_inc(
                vec_landed, 16)
            def split(c, i=None):
                act.wait_ge(w_landed[c % 4], at_step(i, 32, c // 4 * 32 + 32))
                if i is not None or c >= 2:
                    act.wait_ge(w_used, at_step(i, 4, c - 1))
                act.activation(whi[c % 2][:, :], wraw[c % 4][:, :], ACT.Copy).then_inc(w_hi_ready, 1)

            def split_ahead(name, first=0, end=None):
                b0, end = BLOCKS[name] + 1, end or dict(STAGES)[name]
                with act.Fori(first // 4, end // 4) as i:
                    for j in range(4):
                        split(b0 + j, i)

            def o_hi(a, g):
                a.wait_ge(pv_done, 16 * (g + 1))
                a.activation(hHi[:, 4 * (g % 2):4 * (g % 2) + 4, g // 2 * P:(g // 2 + 1) * P],
                             bank[4 + g % 2][:, :].rearrange("p (k n) -> p k n", k=4), ACT.Copy).then_inc(ohi_ready, 1)

            def xo_hi(a, h):
                for dt in range(2):
                    a.wait_ge(xo_done, 2 * h + dt + 1)
                    a.activation(mHi[:, 2 * h + dt, :], bank[6 + dt][:, :], ACT.Copy).then_inc(xohi_ready, 1)

            def squares(a, n):
                for m in range(KT):
                    a.wait_ge(xc_ready, KT * (n - 1) + m + 1)
                    a.activation(sq[:, m, :], xc[:, m, :], ACT.Square).then_inc(sq_ready, 1)

            def h_hi(a, n, m, col):
                a.wait_ge(nrm_ready, KT * (n - 1) + m + 1)
                a.activation(hHi[:, m, :], xc[:, m, :], ACT.Identity, scale=vecT[:, col + m:col + m + 1],
                             bias=vecT[:, col + 8 + m:col + 9 + m]).then_inc(hhi_ready, 1)

            act.wait_ge(var0_ready, 1)
            act.activation(rinv[:, :], rinv[:, :], ACT.Sqrt).then_inc(sd0_ready, 1)
            split(0)
            act.wait_ge(par_landed, 48)
            act.activation(araw[2][:, :, :], ldt[:, :, None].to_broadcast([NGP, 2, NS]), ACT.Exp).then_inc(dt_ready, 1)
            for k in range(KT):
                act.wait_ge(hf0_ready, k + 1)
                act.activation(hHi[:, k, :], hF[:, k, :], ACT.Copy).then_inc(hhi_ready, 1)

            def gate_tile(b, t):
                act.wait_ge(w_used, b + 1)
                act.activation(G[:, t, :], bank[t % 2][:, :], ACT.Sigmoid).then_inc(tile_act, 1)

            split(1)
            act.wait_ge(er_ready, 1)
            act.activation(sp["er"][:, :], sp["er"][:, :], ACT.Exp).then_inc(mag_ready, 1)
            act.wait_ge(angle_ready, 1)
            act.activation(sp["s"][:, :], sp["th"][:, :], ACT.Sin).then_inc(sin_ready, 1)
            act.activation(sp["s2"][:, :], sp["th"][:, :], ACT.Sin, scale=0.5).then_inc(sin_ready, 1)
            gate_tile(0, 0)
            for t in range(1, dict(STAGES)["gmixa"]):
                split(t + 1)
                gate_tile(t, t)
            for b in range(4):
                split(BLOCKS["u"] + b + 1)
            split(BLOCKS["gmixe"] + 1)
            gate_tile(BLOCKS["gmixe"], 4)
            split(BLOCKS["gmixb"])
            gate_tile(BLOCKS["gmixe"] + 1, 5)
            for t in range(6):
                split(BLOCKS["gmixb"] + t + 1)
                gate_tile(BLOCKS["gmixb"] + t, 6 + t)
            split(BLOCKS["gmixc"] + 1)
            for ct in range(4):
                act.wait_ge(yt_turned, ct + 1)
                act.activation(gF[:, ct, :], bank[2 + ct][:, :], ACT.Gelu_apprx_tanh).then_inc(gelu_done, 1)
            act.dma_start(w1[:, :, :, :], I["cmp_w1"][0].rearrange("z (r p) e -> p z r e", p=P)).then_inc(w1_landed, 16)
            for e in range(2):
                for z in range(2):
                    act.dma_start(w2[:, z, :, HD * e:HD * e + HD], I["cmp_w2"][0, z].rearrange(
                        "(k p) d -> p k d", p=P)).then_inc(w1_landed, 16)
            act.dma_start(wg[:, :, :], rows(w_in)[:, :, C_GN:C_GN + 3 * NH]).then_inc(w1_landed, 16)
            for ct in range(4):
                act.wait_ge(gelu_done, ct + 1)
                act.activation(gHi[:, ct, :], gF[:, ct, :], ACT.Copy).then_inc(ghi_ready, 1)
            gate_tile(BLOCKS["gmixc"], 12)
            split(BLOCKS["glu"])
            gate_tile(BLOCKS["gmixc"] + 1, 13)
            split(BLOCKS["glu"] + 1)
            split(BLOCKS["gmixd"])
            split(BLOCKS["gmixd"] + 1)
            act.wait_ge(vec_ready, 1)
            for m in range(4):
                act.wait_ge(w_used, BLOCKS["glu"] + 2)
                act.activation(yF[:, m, :], bank[2 + m][:, :], ACT.Sigmoid,
                               bias=vecT[:, 64 + m:65 + m]).then_inc(glu_sig, 1)
            gate_tile(BLOCKS["gmixd"], 14)
            split(BLOCKS["sso"])
            for m in range(4):
                act.wait_ge(yf_ready, m + 1)
                act.activation(yHi[:, m, :], yF[:, m, :], ACT.Copy).then_inc(yhi_ready, 1)
            gate_tile(BLOCKS["gmixd"] + 1, 15)
            for b in range(8):
                split(BLOCKS["sso"] + b + 1)
            split(BLOCKS["kvc"] + 1)
            act.wait_ge(gate_done, 1)
            act.activation(gateT, bank[6][0:3 * NH, :], ACT.Sigmoid).then_inc(gate_sig, 1)
            for t in range(1, 4):
                split(BLOCKS["kvc"] + t + 1)
            split_ahead("q")
            split_ahead("k")
            for j in range(4):
                act.wait_ge(hidb_ready, j + 1)
                src = bank[2 + j][:, 0:NKV * NCMP].rearrange("p (h n) -> p h n", h=NKV)
                if j < 2:
                    dst = hidK[:, j, :, 0:NCMP]
                else:
                    dst, src = hidV[:, j - 2, :, :, 0:NCMP], src[:, :, None, :].to_broadcast([P, NKV, 4, NCMP])
                act.activation(dst, src, ACT.Gelu_apprx_tanh, bias=hidb[:, j:j + 1]).then_inc(hid_ready, 1)

            def compressed_exp(qi):
                act.wait_ge(tc_ready, qi + 1)
                act.activation(Tc[:, :, :], Tc[:, :, :], ACT.Exp).then_inc(pc_ready, 1)

            compressed_exp(0)
            for u in range(UNITS + PV):
                if u < UNITS:
                    m, br, e, qi = unit(u)
                    n, h = P * (qi + 1), 2 * m + e
                    act.wait_ge(max_done, u + 1)
                    act.activation(Sr[u % 8][:, 0:n], Sr[u % 8][:, 0:n], ACT.Exp, bias=nmax[:, u % 8:u % 8 + 1],
                                   scale=-1.0, accum_out=sums[:, qi % 2, 1 + br, h:h + 1]).then_inc(exp_done, 1)
                if u % 32 == CMP_EXP and u // 32 < 3:
                    compressed_exp(u // 32 + 1)
                v = u - TURN
                if 0 <= v < UNITS and v % 2 == 1:
                    n = P * (unit(v)[3] + 1)
                    act.wait_ge(turned, v + 1)
                    if v >= 4:
                        act.wait_ge(pv_done, v - 3)
                    act.activation(PTr[v % 4][:, 0:n], bank[3][:, 0:n], ACT.Copy).then_inc(turned_act, 1)
                if u % 16 == O_STEP and u > 16:
                    o_hi(act, (u // 16) - 1)
            o_hi(act, 7)
            act.dma_start(memF[:, :, :], I["mem"][0].rearrange("(a p) n -> p a n", p=P)).then_inc(mem_landed, 16)
            for stage in ("nsa", "wout"):
                if stage == "wout":
                    for j in range(4):
                        act.wait_ge(mem_turned, j + 1)
                        act.activation(memHi[:, 2 * j:2 * j + 2, :], bank[2 + j][:, :].rearrange(
                            "p (k n) -> p k n", k=2), ACT.Copy).then_inc(memhi_ready, 1)
                    split_ahead("wout")
                else:
                    for t in range(KT + 1):
                        if t < KT:
                            split(BLOCKS["nsa"] + t + 1)
                        if t >= 1:
                            act.wait_ge(mf_ready, t)
                            act.activation(mHi[:, t - 1, :], mF[(t - 1) % 2][:, :], ACT.Copy).then_inc(mhi_ready, 1)
            for t in range(6):
                split(BLOCKS["xk"] + t + 1)
            squares(act, 1)
            for t in range(6, 8):
                split(BLOCKS["xk"] + t + 1)
            act.wait_ge(var_ready, 1)
            act.activation(rstd[:, :], rstd[:, :], ACT.Sqrt).then_inc(sd_ready, 1)
            for b in range(8):
                split(BLOCKS["xv"] + b + 1)
                h_hi(act, 1, b, 16)
            split_ahead("xq")
            for n in range(4 * XH):
                h, qi = n // 4, n % 4
                act.wait_ge(xmax_ready, n + 1)
                if n >= 4:
                    act.wait_ge(xt_done, n - 3)
                act.activation(xP[n % 4][:, :], bank[XSCORE_BANKS[n % 4]][:, 0:MEM], ACT.Exp, bias=xmax[:, n % 4:n % 4 + 1],
                               accum_out=xsum[:, n % 4:n % 4 + 1]).then_inc(xexp_done, 1)
                if qi == 3 and h >= 1:
                    xo_hi(act, h - 1)
            xo_hi(act, XH - 1)
            split_ahead("xo")
            squares(act, 2)
            act.wait_ge(var_ready, 2)
            act.activation(rstd[:, :], rstd[:, :], ACT.Sqrt).then_inc(sd_ready, 1)
            for m in range(KT):
                h_hi(act, 2, m, 32)
            for i, name in enumerate(("ln3_g", "ln3_b")):
                act.dma_start(row3[i][:, :], I[name][0:1, :].to_broadcast([P, D])).then_inc(row3_landed, 16)
            b0 = BLOCKS["fin"]

            def gate_split(i, t):
                split(b0 + 2 * t + 1, i)

            def hidden_hi(i, t, which):
                act.wait_ge(sf_ready, i * 2 + (t + 3))
                act.activation(sHi[:, i * 2 + t, :], sF[which][:, :], ACT.Copy).then_inc(shi_ready, 1)

            def silu(i, t):
                split(b0 + 2 * t + 2, i)
                act.wait_ge(w_used, at_step(i, 4, b0 + 2 * t + 1))
                act.wait_ge(sf_ready, at_step(i, 2, t + 1))
                act.activation(sg[t][:, :], bank[2 * t][:, :], ACT.Silu).then_inc(sg_ready, 1)

            gate_split(None, 0)
            silu(None, 0)
            gate_split(None, 1)
            hidden_hi(0, 0, 0)
            silu(None, 1)
            with act.Fori(1, KF // 2) as i:
                for t in range(2):
                    gate_split(i, t)
                    hidden_hi(i, t - 1, (t - 1) % 2)
                    silu(i, t)
            hidden_hi(KF // 2 - 1, 1, 1)
            split_ahead("fout")
            split(NBLOCKS - 1)
            for a in range(4):
                act.wait_ge(var3_ready, a + 1)
                act.activation(sd3[:, a:a + 1], sd3[:, a:a + 1], ACT.Sqrt).then_inc(sd3_ready, 1)
            for a in range(4):
                act.wait_ge(shift3_ready, a + 1)
                act.activation(otok[a][:, 0:512], bank[2 * a][:, :], ACT.Identity, scale=sd3[:, a:a + 1],
                               bias=shift3[:, a:a + 1]).then_inc(norm3_done, 1)

        @block.gpsimd
        def _(pool):
            steps = [0]

            def link(ins):
                steps[0] += 1
                ins.then_inc(pool_step, 1)
                pool.wait_ge(pool_step, steps[0])

            link(pool.memset(ident[:, :], 0.0))
            pool.affine_select(out=ident[:, :], in_=ident[:, :], compare_op=ALU.not_equal, fill=1.0, base=0,
                               pattern=[[-1, P]], channel_multiplier=1).then_inc(ident_ready, 1)
            pool.memset(mean_w[:, :], 1.0 / D).then_inc(pool_const, 1)
            link(pool.iota(cdist[:, :, :], [[-P, 4], [16, 32]], base=31, channel_multiplier=-1,
                           allow_small_or_imprecise_dtypes=True))
            link(pool.affine_select(out=cdist[:, :, :], in_=cdist[:, :, :], compare_op=ALU.is_ge, fill=MASKED, base=-31,
                                    pattern=[[P, 4], [-16, 32]], channel_multiplier=1))
            def lo(c, i=None):
                pool.wait_ge(w_hi_ready, at_step(i, 4, c + 1))
                pool.tensor_tensor(wlo[c % 4][:, :], wraw[c % 4][:, :], whi[c % 2][:, :].bitcast(F32),
                                   ALU.subtract).then_inc(w_lo_ready, 1)

            def lo_range(first, end):
                with pool.Fori(0, (end - first) // 4) as i:
                    for j in range(4):
                        lo(first + j, i)
                for c in range(end - (end - first) % 4, end):
                    lo(c)

            def h_lo(m, count):
                pool.wait_ge(hhi_ready, count + m + 1)
                if count:
                    pool.wait_ge(hf_ready, count - KT + m + 1)
                pool.tensor_tensor(hLo[:, m, :], hF[:, m, :], hHi[:, m, :].bitcast(F32), ALU.subtract).then_inc(
                    hlo_ready, 1)

            lo(0)
            for k in range(KT):
                h_lo(k, 0)
            lo(1)
            pool.wait_ge(h0_turned, KT)
            pool.memset(Mst[:, 0:CH - 1, :, :], 0.0).then_inc(m_zero, 1)
            lo_range(2, BLOCKS["nsa"])
            pool.wait_ge(hid_done, 4)
            link(pool.iota(dist[:, :], [[1, T]], base=P - T, channel_multiplier=-1, allow_small_or_imprecise_dtypes=True))
            pool.affine_select(out=dist[:, :], in_=dist[:, :], compare_op=ALU.is_ge, fill=MASKED, base=T - P,
                               pattern=[[-1, T]], channel_multiplier=1).then_inc(dist_ready, 1)
            lo(BLOCKS["nsa"])
            for u in range(UNITS):
                m, br, e, qi = unit(u)
                h = 2 * m + e
                pool.wait_ge(winv_ready, u // 2 + 1)
                if u >= 4:
                    pool.wait_ge(turned, u - 3)
                pool.tensor_scalar(diag[u % 4][:, :], ident[:, :], winv[:, u // 2 % 4, e:e + 1],
                                   gates[:, qi, 3 * h + 1 + br:3 * h + 2 + br], ALU.mult, ALU.mult).then_inc(diag_ready, 1)
            lo(BLOCKS["nsa"] + 1)
            lo_range(BLOCKS["nsa"] + 2, BLOCKS["fin"])
            lo(BLOCKS["fin"])
            for m in range(KT):
                h_lo(m, 16)
            lo(BLOCKS["fin"] + 1)
            lo_range(BLOCKS["fin"] + 2, NBLOCKS)
            for a in range(4):
                pool.wait_ge(gain3_done, a + 1)
                pool.tensor_tensor(otok[a][:, 0:512], otok[a][:, 0:512], row3[1][:, 0:512], ALU.add).then_inc(
                    out_ready[0], 1)

        @block.vector
        def _(dve):
            steps = [0]

            def link(ins):
                steps[0] += 1
                ins.then_inc(dve_step, 1)
                dve.wait_ge(dve_step, steps[0])

            def tt(o, a, b, op):
                return dve.tensor_tensor(o, a, b, op)

            dve.memset(nmax[:, :], 0.0).then_inc(tile_act, 2)
            dve.memset(cmax[:, :], 0.0).then_inc(tile_dve, 2)
            dve.memset(xmax[:, :], 0.0).then_inc(sf_ready, 2)
            for h in range(NH):
                half, m = slice(64 * (h % 2), 64 * (h % 2) + 64), h // 2
                dve.memset(slope_row[:, h:h + 1], SLOPES[h])
                last = dve.memset(qscale[half, m:m + 1], HD ** -0.5 / SLOPES[h])
            link(last)
            dve.wait_ge(ident_ready, 1)
            dve.tensor_copy(rep16[:, :, :], ident[0:GC, None, 0:GC].to_broadcast([GC, 8, GC])).then_inc(rep_ready, 1)

            for a in range(4):
                dve.wait_ge(x_landed[a], 16)
                for half in range(2):
                    last = dve.bn_stats(bnst[:, a, half, :], xtok[:, a, 512 * half:512 * half + 512])
            link(last)
            for a in range(4):
                last = dve.bn_aggr(bnmv[:, a, :], bnst[:, a, :, :])
            link(last)
            dve.tensor_scalar(rinv[:, :], bnmv[:, :, 1], EPS, None, ALU.add).then_inc(var0_ready, 1)
            dve.wait_ge(sd0_ready, 1)
            link(dve.reciprocal(rinv[:, :], rinv[:, :]))
            for a in range(4):
                dve.tensor_scalar(xtok[:, a, :], xtok[:, a, :], bnmv[:, a, 0:1], rinv[:, a:a + 1],
                                  ALU.subtract, ALU.mult).then_inc(xn_ready, 1)
            dve.wait_ge(vec_turned, 1)
            dve.tensor_copy(dT[:, :], bank[7][0:GC, 128:128 + NG])
            dve.tensor_copy(posT[:, :, :], bank[7][:, 160:192].rearrange("p (z r) -> p z r", z=2))
            dve.tensor_copy(vecT[:, :], bank[7][:, 0:72]).then_inc(vec_ready, 1)
            dve.wait_ge(vec_ready, 1)
            for k in range(KT):
                dve.wait_ge(h0_turned, k + 1)
                dve.tensor_scalar(hF[:, k, :], bank[2 + k % 4][:, :], vecT[:, k:k + 1], vecT[:, 8 + k:9 + k],
                                  ALU.mult, ALU.add).then_inc(hf0_ready, 1)

            v = {n: t[:, :] for n, t in sp.items()}
            dve.wait_ge(par_turned, 1)
            dve.tensor_scalar(v["are"], bank[6][:, 0:NGP], -1e-4, None, ALU.min)
            dve.tensor_copy(v["aim"], bank[6][:, NGP:2 * NGP])
            link(dve.tensor_copy(v["dt"], bank[6][:, 2 * NGP:3 * NGP]))
            tt(v["er"], v["are"], v["dt"], ALU.mult).then_inc(er_ready, 1)
            link(tt(v["th"], v["aim"], v["dt"], ALU.mult))
            link(dve.tensor_scalar(v["k"], v["th"], 1.0 / TWO_PI, ROUND, ALU.mult, ALU.add))
            link(dve.tensor_scalar(v["k"], v["k"], -ROUND, None, ALU.add))
            for part in (PI_A, PI_B, PI_C):
                link(dve.scalar_tensor_tensor(out=v["th"], in0=v["k"], scalar=-part, in1=v["th"],
                                              op0=ALU.mult, op1=ALU.add))
            dve.tensor_scalar(v["th"], v["th"], 3.1415925, -3.1415925, ALU.min, ALU.max).then_inc(angle_ready, 1)
            dve.wait_ge(sin_ready, 2)
            dve.wait_ge(mag_ready, 1)
            link(tt(v["s2"], v["s2"], v["s2"], ALU.mult))
            link(dve.tensor_scalar(v["s2"], v["s2"], -2.0, 1.0, ALU.mult, ALU.add))
            tt(LP[:, 0, 0, :], v["er"], v["s2"], ALU.mult)
            tt(v["den"], v["are"], v["are"], ALU.mult)
            tt(v["k"], v["aim"], v["aim"], ALU.mult)
            link(tt(LP[:, 1, 0, :], v["er"], v["s"], ALU.mult))
            link(tt(v["den"], v["den"], v["k"], ALU.add))
            dve.tensor_scalar(v["nr"], LP[:, 0, 0, :], -1.0, None, ALU.add)
            link(dve.reciprocal(v["den"], v["den"]))
            tt(v["a"], v["nr"], v["are"], ALU.mult)
            tt(v["b"], LP[:, 1, 0, :], v["aim"], ALU.mult)
            tt(v["c"], LP[:, 1, 0, :], v["are"], ALU.mult)
            link(tt(v["d"], v["nr"], v["aim"], ALU.mult))
            tt(v["fr"], v["a"], v["b"], ALU.add)
            link(tt(v["fi"], v["c"], v["d"], ALU.subtract))
            tt(v["fr"], v["fr"], v["den"], ALU.mult)
            link(tt(v["fi"], v["fi"], v["den"], ALU.mult))

            def cmul(dst, d0, n, a, a0, y):
                x = [a[:, ri, a0:a0 + n, :] for ri in range(2)]
                y = [part[:, None, :].to_broadcast([P, n, NGP]) for part in y]
                tt(cm[0][:, 0:n, :], x[0], y[0], ALU.mult)
                tt(cm[1][:, 0:n, :], x[1], y[1], ALU.mult)
                tt(cm[2][:, 0:n, :], x[0], y[1], ALU.mult)
                link(tt(cm[3][:, 0:n, :], x[1], y[0], ALU.mult))
                tt(dst[:, 0, d0:d0 + n, :], cm[0][:, 0:n, :], cm[1][:, 0:n, :], ALU.subtract)
                link(tt(dst[:, 1, d0:d0 + n, :], cm[2][:, 0:n, :], cm[3][:, 0:n, :], ALU.add))

            def power(t, i):
                return t[:, 0, i, :], t[:, 1, i, :]

            cmul(LP, 1, 1, LP, 0, power(LP, 0))
            cmul(LP, 2, 2, LP, 0, power(LP, 1))
            cmul(LP, 4, 4, LP, 0, power(LP, 3))
            dve.memset(LD[:, 0, 7:8, :], 1.0)
            dve.memset(LD[:, 1, 7:8, :], 0.0)
            for i in range(3):
                dve.tensor_copy(LD[:, :, 6 - i, :], LP[:, :, i, :])
            link(dve.tensor_copy(ET[:, :, 0, :], LP[:, :, 7, :]))
            cmul(LD, 0, 4, LD, 4, power(LP, 3))
            cmul(FP, 0, 8, LD, 0, (v["fr"], v["fi"]))
            cmul(ET, 1, 1, ET, 0, power(ET, 0))
            cmul(ET, 2, 2, ET, 0, power(ET, 1))
            cmul(ET, 4, 4, ET, 0, power(ET, 3))
            dve.memset(sums[:, :, :, :], 0.0)

            dve.wait_ge(dcol_done, 1)
            dve.tensor_copy(Dcol[:, :], bank[7][:, 0:NG])
            for ri in range(2):
                dve.wait_ge(ct_turned, ri + 1)
                for q in range(2):
                    last = dve.tensor_copy(Ct[64 * q:64 * q + 64, ri, :, :], bank[4 + ri][:, :].rearrange(
                        "p (g q c) -> p q g c", q=2, c=GC)[64 * q:64 * q + 64, q])
                last.then_inc(ct_ready, 1)
            dve.wait_ge(ct_ready, 2)
            link(dve.memset(Cbd[:, :, :, :, :], 0.0))
            for q in range(2):
                rows_q = slice(64 * q, 64 * q + 64)
                dve.tensor_copy(Cbd[rows_q, 0, :, q, :], Ct[rows_q, 0, :, :])
                last = dve.tensor_scalar(Cbd[rows_q, 1, :, q, :], Ct[rows_q, 1, :, :], -1.0, None, ALU.mult)
            last.then_inc(cbd_ready, 1)
            dve.wait_ge(b_landed, 32)
            shape = [P, NGP, CH, GC]
            f = [FP[:, ri].rearrange("p s g -> p g s")[:, :, :, None].to_broadcast(shape) for ri in range(2)]
            bb = [Bt[:, ri][:, :, None, :].to_broadcast(shape) for ri in range(2)]
            for ri, (x, y, op) in enumerate(((0, 1, ALU.subtract), (1, 0, ALU.add))):
                dst = Pw[:, ri]
                tt(dst, bb[x], f[0], ALU.mult)
                link(tt(Ptmp[:, :, :, :], bb[y], f[1], ALU.mult))
                link(tt(dst, dst, Ptmp[:, :, :, :], op))
            dve.memset(nmax[:, :], 0.0).then_inc(pw_ready, 1)
            lam = [LP[:, ri].rearrange("p j g -> p g j")[:, :, :, None].to_broadcast(shape) for ri in range(2)]
            cc = [Ct[:, ri][:, :, None, :].to_broadcast(shape) for ri in range(2)]
            tt(Ost[:, 0], cc[0], lam[0], ALU.mult)
            link(tt(Ptmp[:, :, :, :], cc[1], lam[1], ALU.mult))
            tt(Ost[:, 0], Ost[:, 0], Ptmp[:, :, :, :], ALU.subtract)
            tt(Ost[:, 1], cc[0], lam[1], ALU.mult)
            link(tt(Otmp[:, :, :, :], cc[1], lam[0], ALU.mult))
            dve.scalar_tensor_tensor(out=Ost[:, 1], in0=Ost[:, 1], scalar=-1.0, in1=Otmp[:, :, :, :], op0=ALU.mult,
                                     op1=ALU.subtract).then_inc(o_ready, 1)
            dve.wait_ge(w_used, BLOCKS["u"] + 4)
            dve.wait_ge(o_ready, 1)
            for r in range(4):
                last = dve.tensor_copy(U1[:, :, r, :], bank[2 + r][:, :].rearrange("p (g c) -> p g c", g=NG))
            last.then_inc(u1_ready, 1)
            skip = Ptmp[:, 0:4].rearrange("p a b c -> p (a b c)").rearrange("p (g c) -> p g c", g=NG)
            link(tt(skip, Dcol[:, :, None].to_broadcast([P, NG, GC]), ident[:, None, P - GC:P].to_broadcast([P, NG, GC]),
                    ALU.mult))
            dve.wait_ge(m_built, 1)
            tt(Mst[:, 7, :, :], bank[6][:, :].rearrange("p (g c) -> p g c", g=NG), skip, ALU.add).then_inc(m7_ready, 1)
            for j in range(8):
                dve.wait_ge(wst_turned, j + 1)
                dve.tensor_copy(Wst[:, j // 4, 4 * (j % 4):4 * (j % 4) + 4, :], bank[7 - j % 2][:, :].rearrange(
                    "p (g n) -> p g n", g=4)).then_inc(wst_ready, 1)
            for j in range(4):
                dve.wait_ge(ut_turned, j + 1)
                dve.tensor_copy(UT[:, 8 * j:8 * j + 8, :], bank[2 + j][:, :].rearrange("p (g n) -> p g n", g=8)).then_inc(
                    ut_ready, 1)
            dve.memset(H[:, :, :, 0:1], 0.0)
            for j in range(4):
                dve.wait_ge(s_done, j + 1)
                last = dve.tensor_copy(H[:, j // 2, 8 * (j % 2):8 * (j % 2) + 8, 1:NCH + 1], bank[2 + j][:, :].rearrange(
                    "p (g n) -> p g n", g=8))
                last.then_inc(h_loaded, 1)
            dve.wait_ge(h_loaded, 4)

            def advance(c1, c0, n, e):
                def col(c):
                    return H[:, :, :, c:c + 8 * (n - 1) + 1:8]

                cur, prev = col(c1), col(c0)
                er = ET[:, 0, e, :][:, None, :, None].to_broadcast([P, 2, NGP, n])
                ei = ET[:, 1, e, :][:, :, None].to_broadcast([P, NGP, n])
                tt(st1[:, :, :, 0:n], prev, er, ALU.mult)
                tt(st2[:, 0, :, 0:n], prev[:, 1], ei, ALU.mult)
                link(tt(st2[:, 1, :, 0:n], prev[:, 0], ei, ALU.mult))
                link(tt(cur, cur, st1[:, :, :, 0:n], ALU.add))
                tt(cur[:, 0], cur[:, 0], st2[:, 0, :, 0:n], ALU.subtract)
                link(tt(cur[:, 1], cur[:, 1], st2[:, 1, :, 0:n], ALU.add))

            for i in range(1, 8):
                advance(1 + i, i, 8, 0)
            for s in range(1, 8):
                advance(8 * s + 8, 8 * s, 1, 7)
            for i in range(7):
                advance(9 + i, 8, 7, i)
            dve.memset(nmax[:, :], 0.0).then_inc(scan_done, 1)
            for q in range(4):
                dve.wait_ge(y_done, q + 1)
                dst = Yt[:, :, P * q:P * q + P].rearrange("p j (g e c) -> p e g j c", g=4, e=2)
                for e in range(2):
                    dve.tensor_copy(dst[:, e], bank[2 + 2 * (q % 2) + e][0:64, :].rearrange(
                        "p (g j c) -> p g j c", g=4, j=8)).then_inc(y_ready, 1)
            for ct in range(4):
                dve.wait_ge(ghi_ready, ct + 1)
                tt(gLo[:, ct, :], gF[:, ct, :], gHi[:, ct, :].bitcast(F32), ALU.subtract).then_inc(glo_ready, 1)
            for m in range(4):
                dve.wait_ge(glu_sig, m + 1)
                tt(yF[:, m, :], yF[:, m, :], gF[:, m, :], ALU.mult).then_inc(yf_ready, 1)
            for m in range(4):
                dve.wait_ge(yhi_ready, m + 1)
                tt(yLo[:, m, :], yF[:, m, :], yHi[:, m, :].bitcast(F32), ALU.subtract).then_inc(ylo_ready, 1)
            dve.wait_ge(tile_act, 2 + 16)
            for t in range(KT):
                if t % 2:
                    dve.wait_ge(w_used, BLOCKS["sso"] + t // 2 + 1)
                else:
                    dve.wait_ge(sso_tile, t // 2 + 1)
                gv = G[:, t, :].rearrange("p (c j) -> p j c", j=CH)
                tt(gv, gv, bank[t % 2][:, :].rearrange("p (j c) -> p j c", j=CH), ALU.mult).then_inc(tile_dve, 1)
            dve.wait_ge(w_used, BLOCKS["v"] + 4)
            for a in range(4):
                dve.tensor_copy(VA[:, a, :], bank[2 + a][:, :]).then_inc(v_ready, 1)
            def tiles_out(name, first, count):
                b0 = BLOCKS[name]
                with dve.Fori(0, count // 2) as i:
                    for s in range(2):
                        dve.wait_ge(w_used, i * 2 + (b0 + s + 1))
                        dve.tensor_copy(kqT[:, i * 2 + (first + s), :], bank[s][:, :]).then_inc(tile_dve, 1)

            tiles_out("kvc", 8, 4)
            dve.wait_ge(gate_turned, 1)
            dve.tensor_copy(gates[:, :, :], bank[7][:, 0:4 * 3 * NH].rearrange("p (a n) -> p a n", a=4)).then_inc(
                gate_ready, 1)
            for z in range(2):
                last = dve.memset(Xc[:, z, NKV, :], 0.0)
            link(last)
            dve.tensor_copy(Xc[:, :, NKV, 0:32:2], posT[:, :, :]).then_inc(pos_ready, 1)
            for t in range(8):
                dve.wait_ge(w_used, BLOCKS["q"] + t + 1)
                dve.tensor_scalar(kqT[:, t, :], bank[t % 2][:, :], qscale[:, t:t + 1], None, ALU.mult).then_inc(tile_dve, 1)
            tiles_out("k", 12, 4)
            dve.memset(hidK[:, :, :, NCMP:32], 0.0)
            for j in range(4):
                dve.wait_ge(hid_done, j + 1)
                tt(hidb[:, j:j + 1], bank[2 + j][:, NKV * NCMP:NKV * NCMP + 1], vecT[:, 68 + j:69 + j], ALU.add).then_inc(
                    hidb_ready, 1)
            dve.memset(hidV[:, :, :, :, NCMP:32], 0.0).then_inc(hid_padded, 1)
            dve.memset(kcT[:, :, :, :], 0.0)
            link(dve.memset(Vbd[:, :, :, :], 0.0))
            dve.wait_ge(kc_done, 1)
            for e in range(2):
                last = dve.tensor_copy(kcT[64 * e:64 * e + 64, :, e, :], bank[6][64 * e:64 * e + 64, 0:P].rearrange(
                    "p (h n) -> p h n", h=NKV))
            last.then_inc(kc_ready, 1)
            dve.wait_ge(vc_done, 1)
            for g in range(4):
                last = dve.tensor_copy(Vbd[32 * g:32 * g + 32, :, g, :], bank[7][32 * g:32 * g + 32, 0:256].rearrange(
                    "p (h d) -> p h d", h=NKV))
            last.then_inc(vc_ready, 1)
            dve.wait_ge(dist_ready, 1)

            def o_lo(g):
                dve.wait_ge(ohi_ready, g + 1)
                dst = slice(4 * (g % 2), 4 * (g % 2) + 4), slice(g // 2 * P, (g // 2 + 1) * P)
                tt(hLo[:, dst[0], dst[1]], bank[4 + g % 2][:, :].rearrange("p (k n) -> p k n", k=4),
                   hHi[:, dst[0], dst[1]].bitcast(F32), ALU.subtract).then_inc(olo_ready, 1)

            def compressed_scores(qi):
                dve.wait_ge(cscore_done, qi + 1)
                if qi >= 1:
                    dve.wait_ge(cturned, qi)
                link(tt(Tc[:, :, :], bank[7][:, :].rearrange("p (h n) -> p h n", h=NH),
                        cdist[:, qi, None, :].to_broadcast([P, NH, 32]), ALU.add))
                link(dve.tensor_reduce(cmax[:, :], Tc[:, :, :], AX.X, ALU.max))
                link(dve.tensor_scalar(cmax[:, :], cmax[:, :], MAX_FLOOR, None, ALU.max))
                link(tt(Tc[:, :, :], Tc[:, :, :], cmax[:, :, None].to_broadcast([P, NH, 32]), ALU.subtract))
                tt(Tc[:, :, :], Tc[:, :, :], slope_row[:, :, None].to_broadcast([P, NH, 32]), ALU.mult).then_inc(
                    tc_ready, 1)

            def compressed_sums(qi):
                dve.wait_ge(pc_ready, qi + 1)
                link(dve.tensor_reduce(wcmp[:, :], Tc[:, :, :], AX.X, ALU.add))
                link(dve.tensor_scalar(wcmp[:, :], wcmp[:, :], 1e-30, None, ALU.max))
                link(dve.reciprocal(wcmp[:, :], wcmp[:, :]))
                if qi == 0:
                    dve.wait_ge(gate_ready, 1)
                link(tt(wcmp[:, :], wcmp[:, :], gates[:, qi, 0:3 * NH:3], ALU.mult))
                tt(Tc[:, :, :], Tc[:, :, :], wcmp[:, :, None].to_broadcast([P, NH, 32]), ALU.mult).then_inc(csum_ready, 1)

            def compressed_copy(qi):
                dve.wait_ge(cturned, qi + 1)
                if qi >= 2:
                    dve.wait_ge(pv_done, 32 * (qi - 1))
                dve.tensor_copy(PTc[qi % 2][:, :, :],
                                bank[7][:, :].rearrange("p (h n) -> p h n", h=NKV)).then_inc(ptc_ready, 1)

            compressed_scores(0)
            for u in range(UNITS + PV):
                if u < UNITS:
                    m, br, e, qi = unit(u)
                    n, h = P * (qi + 1), 2 * m + e
                    dve.wait_ge(score_done, u + 1)
                    if u >= 8:
                        dve.wait_ge(turned, u - 7)
                    dve.tensor_tensor_reduce(Sr[u % 8][:, 0:n], dist[:, T - n:T], bank[SCORE_BANKS[u % 3]][:, 0:n],
                                             -SLOPES[h], 3e38, ALU.add, ALU.min, nmax[:, u % 8:u % 8 + 1]).then_inc(
                                                 max_done, 1)
                if u % 2 == 1 and 3 <= u < UNITS + 2:
                    m, br, e, qi = unit(u - 3)
                    p = u // 2 - 1
                    dve.wait_ge(exp_done, u - 1)
                    if p >= 4:
                        dve.wait_ge(diag_ready, 2 * (p - 3))
                    link(dve.tensor_scalar(winv[:, p % 4, :], sums[:, qi % 2, 1 + br, 2 * m:2 * m + 2], 1e-30, None,
                                           ALU.max))
                    dve.reciprocal(winv[:, p % 4, :], winv[:, p % 4, :]).then_inc(winv_ready, 1)
                if u == FIRST_SUM:
                    compressed_sums(0)
                elif u == FIRST_COPY:
                    compressed_copy(0)
                if u // 32 < 3:
                    if u % 32 == CMP_SCORE:
                        compressed_scores(u // 32 + 1)
                    elif u % 32 == CMP_SUM:
                        compressed_sums(u // 32 + 1)
                    elif u % 32 == CMP_COPY:
                        compressed_copy(u // 32 + 1)
                v = u - TURN
                if 0 <= v < UNITS and v % 2 == 0:
                    n = P * (unit(v)[3] + 1)
                    dve.wait_ge(turned, v + 1)
                    if v >= 4:
                        dve.wait_ge(pv_done, v - 3)
                    dve.tensor_copy(PTr[v % 4][:, 0:n], bank[2][:, 0:n]).then_inc(turned_dve, 1)
                if u % 16 == O_STEP and u > 16:
                    o_lo(u // 16 - 1)
            o_lo(7)

            b0 = BLOCKS["nsa"]
            with dve.Fori(0, 4) as i:
                for s in range(2):
                    dve.wait_ge(w_used, i * 2 + (b0 + s + 1))
                    tt(mF[s][:, :], bank[s][:, :], G[:, i * 2 + (s + KT), :], ALU.mult).then_inc(tile_dve, 1)
                    dve.wait_ge(tile_dve, i * 2 + (TD["nsa"] + s + 1))
                    tt(mF[s][:, :], mF[s][:, :], G[:, i * 2 + s, :], ALU.add).then_inc(mf_ready, 1)
                    dve.wait_ge(mhi_ready, i * 2 + (s + 1))
                    tt(mLo[:, i * 2 + s, :], mF[s][:, :], mHi[:, i * 2 + s, :].bitcast(F32), ALU.subtract).then_inc(
                        mlo_ready, 1)
            for j in range(4):
                dve.wait_ge(memhi_ready, j + 1)
                tt(memLo[:, 2 * j:2 * j + 2, :], bank[2 + j][:, :].rearrange("p (k n) -> p k n", k=2),
                   memHi[:, 2 * j:2 * j + 2, :].bitcast(F32), ALU.subtract).then_inc(memlo_ready, 1)

            def residual(name, n):
                b0 = BLOCKS[name]
                dve.memset(hsum[:, :], 0.0).then_inc(hsum_ready, 1)
                with dve.Fori(0, 4) as i:
                    for s in range(2):
                        dve.wait_ge(w_used, i * 2 + (b0 + s + 1))
                        dve.scalar_tensor_tensor(out=hF[:, i * 2 + s, :], in0=hF[:, i * 2 + s, :], scalar=ALPHA,
                                                 in1=bank[s][:, :], op0=ALU.mult, op1=ALU.add).then_inc(tile_dve, 1)
                        dve.wait_ge(tile_dve, i * 2 + (TD[name] + s + 1))
                        dve.wait_ge(hsum_ready, i * 2 + (9 * (n - 1) + s + 1))
                        tt(hsum[:, :], hsum[:, :], hF[:, i * 2 + s, :], ALU.add).then_inc(hsum_ready, 1)

            def centre(n):
                dve.wait_ge(mu_ready, n)
                for m in range(KT):
                    tt(xc[:, m, :], hF[:, m, :], bank[6][:, :], ALU.subtract).then_inc(xc_ready, 1)

            def scale(n, col):
                dve.wait_ge(var_done, n)
                dve.tensor_scalar(rstd[:, :], bank[7][:, :], EPS, None, ALU.add).then_inc(var_ready, 1)
                dve.wait_ge(sd_ready, n)
                link(dve.reciprocal(rstd[:, :], rstd[:, :]))
                for m in range(KT + 1):
                    if m < KT:
                        tt(xc[:, m, :], xc[:, m, :], rstd[:, :], ALU.mult).then_inc(nrm_ready, 1)
                    if m >= 1:
                        dve.wait_ge(nrm_ready, KT * (n - 1) + m)
                        dve.tensor_scalar(hF[:, m - 1, :], xc[:, m - 1, :], vecT[:, col + m - 1:col + m],
                                          vecT[:, col + 7 + m:col + 8 + m], ALU.mult, ALU.add).then_inc(hf_ready, 1)
                    if n == 1 and m >= 2:
                        stream_lo(m - 2)
                if n == 1:
                    stream_lo(KT - 1)

            def stream_lo(m):
                dve.wait_ge(hf_ready, m + 1)
                dve.wait_ge(hhi_ready, KT + m + 1)
                tt(hLo[:, m, :], hF[:, m, :], hHi[:, m, :].bitcast(F32), ALU.subtract).then_inc(hlo_ready, 1)

            residual("wout", 1)
            b0 = BLOCKS["xk"]

            def keys_out(i, s):
                dve.wait_ge(w_used, i * 2 + (b0 + s + 1))
                dve.tensor_copy(kxT[:, i * 2 + s, :], bank[s][:, 0:MEM]).then_inc(tile_dve, 1)

            for t in range(4):
                keys_out(t // 2, t % 2)
            centre(1)
            with dve.Fori(2, 4) as i:
                for s in range(2):
                    keys_out(i, s)
            scale(1, 16)
            dve.wait_ge(w_used, BLOCKS["xv"] + 8)
            for a in range(2):
                for half in range(2):
                    last = dve.tensor_copy(vx[:, a, 512 * half:512 * half + 512], bank[2 + 2 * a + half][:, :])
            last.then_inc(xv_ready, 1)
            b0 = BLOCKS["xq"]
            with dve.Fori(0, 4) as i:
                for s in range(2):
                    dve.wait_ge(w_used, i * 2 + (b0 + s + 1))
                    dve.tensor_scalar(qx[:, i * 2 + s, :], bank[s][:, :], (D // XH) ** -0.5, None, ALU.mult).then_inc(
                        tile_dve, 1)

            def xo_lo(h):
                for dt in range(2):
                    dve.wait_ge(xohi_ready, 2 * h + dt + 1)
                    tt(mLo[:, 2 * h + dt, :], bank[6 + dt][:, :], mHi[:, 2 * h + dt, :].bitcast(F32),
                       ALU.subtract).then_inc(xolo_ready, 1)

            NX = 4 * XH
            for n in range(NX + XTURN + 1):
                if n < NX:
                    dve.wait_ge(xs_done, n + 1)
                    dve.tensor_reduce(xmax[:, n % 4:n % 4 + 1], bank[XSCORE_BANKS[n % 4]][:, 0:MEM], AX.X, ALU.max,
                                      negate=True).then_inc(xmax_ready, 1)
                a = n - 1
                if 0 <= a < NX:
                    dve.wait_ge(xexp_done, a + 1)
                    link(dve.reciprocal(rinv[:, a % 4:a % 4 + 1], xsum[:, a % 4:a % 4 + 1]))
                    dve.tensor_scalar(xP[a % 4][:, :], xP[a % 4][:, :], rinv[:, a % 4:a % 4 + 1], None,
                                      ALU.mult).then_inc(xp_ready, 1)
                c = n - XTURN
                if 0 <= c < NX:
                    h, qi = c // 4, c % 4
                    dve.wait_ge(xt_done, c + 1)
                    if h >= 2:
                        dve.wait_ge(xo_done, 2 * (h - 1))
                    dve.tensor_copy(xPT[h % 2][:, :, P * qi:P * qi + P], bank[4 + c % 2][:, 0:MEM].rearrange(
                        "p (k n) -> p k n", k=2)).then_inc(xpt_ready, 1)
                if n % 4 == 3 and n >= 7:
                    xo_lo(n // 4 - 1)
            residual("xo", 2)
            centre(2)
            scale(2, 32)

            b0 = BLOCKS["fin"]
            with dve.Fori(0, KF // 2) as i:
                for t in range(2):
                    dve.wait_ge(w_used, i * 4 + (b0 + 2 * t + 2))
                    dve.wait_ge(sg_ready, i * 2 + (t + 1))
                    tt(sF[t][:, :], sg[t][:, :], bank[2 * t + 1][:, :], ALU.mult).then_inc(sf_ready, 1)
                    dve.wait_ge(shi_ready, i * 2 + (t + 1))
                    tt(sLo[:, i * 2 + t, :], sF[t][:, :], sHi[:, i * 2 + t, :].bitcast(F32), ALU.subtract).then_inc(
                        slo_ready, 1)
            for i, m in enumerate(LAST_ORDER):
                dve.wait_ge(fout_done, i + 1)
                dve.scalar_tensor_tensor(out=hF[:, m, :], in0=hF[:, m, :], scalar=ALPHA, in1=bank[m][:, :],
                                         op0=ALU.mult, op1=ALU.add).then_inc(last_ready, 1)
            dve.wait_ge(tok_turned, 1)
            for a in range(4):
                dve.bn_stats(st3[:, a, 0, :], bank[2 * a][:, :])
            for a in range(4):
                dve.wait_ge(tok_turned, a + 2)
                link(dve.bn_stats(st3[:, a, 1, :], bank[2 * a + 1][:, :]))
                link(dve.bn_aggr(mv3[:, a, :], st3[:, a, :, :]))
                dve.tensor_scalar(sd3[:, a:a + 1], mv3[:, a, 1:2], EPS, None, ALU.add).then_inc(var3_ready, 1)
            for a in range(4):
                dve.wait_ge(sd3_ready, a + 1)
                link(dve.reciprocal(sd3[:, a:a + 1], sd3[:, a:a + 1]))
                dve.tensor_scalar(shift3[:, a:a + 1], mv3[:, a, 0:1], sd3[:, a:a + 1], -1.0, ALU.mult, ALU.mult).then_inc(
                    shift3_ready, 1)
            dve.wait_ge(row3_landed, 32)
            for a in range(4):
                second = otok[a][:, 512:1024]
                link(dve.scalar_tensor_tensor(out=second, in0=bank[2 * a + 1][:, :], scalar=mv3[:, a, 0:1],
                                              in1=row3[0][:, 512:1024], op0=ALU.subtract, op1=ALU.mult))
                dve.scalar_tensor_tensor(out=second, in0=second, scalar=sd3[:, a:a + 1], in1=row3[1][:, 512:1024],
                                         op0=ALU.mult, op1=ALU.add).then_inc(out_ready[1], 1)
                dve.wait_ge(norm3_done, a + 1)
                tt(otok[a][:, 0:512], otok[a][:, 0:512], row3[0][:, 0:512], ALU.mult).then_inc(gain3_done, 1)

        @block.tensor
        def _(pe):
            def mm(o, w, a, start, stop):
                return pe.matmul(o, w, a, start=start, stop=stop)

            def mm3(o, w_hi, w_lo, a_hi, a_lo, start, stop):
                mm(o, w_hi, a_hi, start, False)
                mm(o, w_hi, a_lo, False, False)
                return mm(o, w_lo, a_hi, False, stop)

            def tile_stage(name, a_hi, a_lo, freed, base, n=T, made=None, after_first=None):
                b0, count = BLOCKS[name], dict(STAGES)[name]

                def tile(i, t):
                    c = b0 + t
                    pe.wait_ge(w_lo_ready, at_step(i, 4, c + 1))
                    pe.wait_ge(freed, at_step(i, 4, base + t - 1))
                    for k in range(KT):
                        if made and t == 0:
                            pe.wait_ge(*made(k))
                        w = slice(P * k, P * k + P)
                        last = mm3(bank[t % 2][:, 0:n], whi[c % 2][:, w], wlo[c % 4][:, w], a_hi[:, k, :],
                                   a_lo[:, k, :], k == 0, k == KT - 1)
                    last.then_inc(w_used, 1)

                looped = count if count == 8 and not after_first else 0
                if looped:
                    with pe.Fori(0, looped // 4) as i:
                        for t in range(4):
                            tile(i, t)
                for t in range(looped, count):
                    tile(None, t)
                    if after_first and t == 1:
                        after_first()

            pe.wait_ge(ident_ready, 1)
            pe.wait_ge(vec_landed, 16 * 12)
            pe.transpose(bank[7][:, 0:72], vrows[:, :], ident[0:72, 0:72])
            pe.transpose(bank[7][0:GC, 128:128 + NG], dl[:, :], ident[0:NG, 0:NG])
            for z in range(2):
                last = pe.transpose(bank[7][:, 160 + 16 * z:176 + 16 * z], posl[:, z, :], ident[0:16, 0:16])
            last.then_inc(vec_turned, 1)
            pe.wait_ge(xn_ready, 4)
            for k in range(KT):
                if k >= 4:
                    pe.wait_ge(hf0_ready, k - 3)
                for a in range(4):
                    last = pe.transpose(bank[2 + k % 4][:, P * a:P * a + P], xtok[:, a, P * k:P * k + P], ident[:, :])
                last.then_inc(h0_turned, 1)
            pe.wait_ge(par_landed, 48)
            pe.wait_ge(dt_ready, 1)
            for i in range(3):
                last = pe.transpose(bank[6][:, NGP * i:NGP * i + NGP], araw[i][:, :, :].rearrange("g q n -> g (q n)"),
                                    ident[0:NGP, 0:NGP])
            last.then_inc(par_turned, 1)
            pe.wait_ge(vec_ready, 1)
            pe.wait_ge(rep_ready, 1)
            mm(bank[7][:, 0:NG], rep16[:, :, :].rearrange("p j c -> p (j c)"), dT[:, :], True, True).then_inc(dcol_done, 1)
            pe.wait_ge(c_landed, 64)
            pe.wait_ge(hf0_ready, KT)
            for ri in range(2):
                for t in range(4):
                    last = pe.transpose(bank[4 + ri][:, P * t:P * t + P],
                                        Craw[:, ri, t, :, :].rearrange("p d n -> p (d n)"), ident[:, :])
                last.then_inc(ct_turned, 1)
            tile_stage("gmixa", hHi, hLo, tile_act, 2, made=lambda k: (hlo_ready, k + 1))
            pe.wait_ge(ct_ready, 2)
            for b in range(4):
                hi, lo = whi[(BLOCKS["u"] + b) % 2], wlo[(BLOCKS["u"] + b) % 4]
                pe.wait_ge(w_lo_ready, BLOCKS["u"] + b + 1)
                for kk in range(2):
                    k = 2 * b + kk
                    w = slice(512 * kk, 512 * kk + 512)
                    for r in range(4):
                        a_hi, a_lo = hHi[:, k, r:T:4], hLo[:, k, r:T:4]
                        last = mm3(bank[2 + r][:, :], a_hi, a_lo, hi[:, w], lo[:, w], k == 0, k == KT - 1)
                last.then_inc(w_used, 1)
            tile_stage("gmixe", hHi, hLo, tile_act, 2 + 4)
            pe.wait_ge(pw_ready, 1)
            pe.wait_ge(cbd_ready, 1)
            for gp in range(NGP):
                for ri in range(2):
                    last = mm(bank[6][:, 2 * GC * gp:2 * GC * gp + 2 * GC], Pw[:, ri, gp].rearrange("p j c -> p (j c)"),
                              Cbd[:, ri, gp, :, :], ri == 0, ri == 1)
            last.then_inc(m_built, 1)
            pe.wait_ge(o_ready, 1)
            for j in range(8):
                if j == 1:
                    pe.wait_ge(m7_ready, 1)
                if j >= 2:
                    pe.wait_ge(wst_ready, j - 1)
                for e in range(4):
                    src = Pw[:, j // 4, 4 * (j % 4) + e].rearrange("p j c -> p (j c)")
                    last = pe.transpose(bank[7 - j % 2][:, P * e:P * e + P], src, ident[:, :])
                last.then_inc(wst_turned, 1)
            pe.wait_ge(wst_ready, 8)
            pe.wait_ge(u1_moved, 32)
            for j in range(4):
                for g in range(8 * j, 8 * j + 8):
                    last = pe.transpose(bank[2 + j][:, NCH * (g % 8):NCH * (g % 8) + NCH],
                                        U8[:, g, :, :].rearrange("p j c -> p (j c)"), ident[0:NCH, 0:NCH])
                last.then_inc(ut_turned, 1)
            for j in range(4):
                pe.wait_ge(ut_ready, 4 if j else 2)
                for gp in range(8 * (j % 2), 8 * (j % 2) + 8):
                    for q in range(2):
                        last = mm(bank[2 + j][64 * q:64 * q + 64, NCH * (gp % 8):NCH * (gp % 8) + NCH],
                                  Wst[:, j // 2, gp, 64 * q:64 * q + 64], UT[:, 2 * gp + q, :], True, True)
                last.then_inc(s_done, 1)
            tile_stage("gmixb", hHi, hLo, tile_act, 2 + 6)
            pe.wait_ge(scan_done, 1)
            pe.wait_ge(m_moved, 16 * (CH - 1))
            for q in range(4):
                if q >= 2:
                    pe.wait_ge(y_ready, 2 * (q - 1))
                for e in range(8):
                    g = 8 * q + e
                    gp, half = g // 2, slice(64 * (g % 2), 64 * (g % 2) + 64)
                    o = bank[2 + 2 * (q % 2) + e % 2][0:64, P * (e // 2):P * (e // 2) + P]
                    mm(o, UT[:, g, :], Mst[:, :, g, :], True, False)
                    for ri in range(2):
                        last = mm(o, H[half, ri, gp, 0:NCH], Ost[half, ri, gp].rearrange("p j c -> p (j c)"),
                                  False, ri == 1)
                last.then_inc(y_done, 1)
            pe.wait_ge(y_ready, 8)
            for ct in range(4):
                for j in range(8):
                    last = pe.transpose(bank[2 + ct][:, NCH * j:NCH * j + NCH], Yt[:, j, P * ct:P * ct + P],
                                        ident[0:NCH, 0:NCH])
                last.then_inc(yt_turned, 1)
            tile_stage("gmixc", hHi, hLo, tile_act, 2 + 12)
            pe.wait_ge(glo_ready, 4)
            for b in range(2):
                hi, lo = whi[(BLOCKS["glu"] + b) % 2], wlo[(BLOCKS["glu"] + b) % 4]
                pe.wait_ge(w_lo_ready, BLOCKS["glu"] + b + 1)
                for kk in range(2):
                    for m in range(4):
                        w = slice(512 * kk + P * m, 512 * kk + P * m + P)
                        k = 2 * b + kk
                        last = mm3(bank[2 + m][:, :], hi[:, w], lo[:, w], gHi[:, k, :], gLo[:, k, :],
                                   k == 0, k == 3)
                last.then_inc(w_used, 1)
            tile_stage("gmixd", hHi, hLo, tile_act, 2 + 14)
            pe.wait_ge(ylo_ready, 4)
            pe.wait_ge(tile_act, 2 + 16)
            for t in range(KT):
                b = BLOCKS["sso"] + t // 2
                hi, lo = whi[b % 2], wlo[b % 4]
                pe.wait_ge(w_lo_ready, b + 1)
                if t >= 2:
                    pe.wait_ge(tile_dve, TD["sso"] + t - 1)
                for k in range(4):
                    w = slice(256 * k + P * (t % 2), 256 * k + P * (t % 2) + P)
                    last = mm3(bank[t % 2][:, :], hi[:, w], lo[:, w], yHi[:, k, :], yLo[:, k, :], k == 0, k == 3)
                last.then_inc(w_used if t % 2 else sso_tile, 1)
            for b in range(4):
                hi, lo = whi[(BLOCKS["v"] + b) % 2], wlo[(BLOCKS["v"] + b) % 4]
                pe.wait_ge(w_lo_ready, BLOCKS["v"] + b + 1)
                for kk in range(2):
                    k = 2 * b + kk
                    w = slice(512 * kk, 512 * kk + 512)
                    for a in range(4):
                        tok = slice(P * a, P * a + P)
                        last = mm3(bank[2 + a][:, :], hHi[:, k, tok], hLo[:, k, tok], hi[:, w], lo[:, w],
                                   k == 0, k == KT - 1)
                last.then_inc(w_used, 1)
            pe.wait_ge(w1_landed, 6 * 16)
            for k in range(KT):
                last = mm(bank[6][0:3 * NH, :], wg[:, k, :], hF[:, k, :], k == 0, k == KT - 1)
            last.then_inc(gate_done, 1)
            tile_stage("kvc", hHi, hLo, tile_dve, TD["kvc"])
            pe.wait_ge(gate_sig, 1)
            for a in range(4):
                last = pe.transpose(bank[7][:, 3 * NH * a:3 * NH * a + 3 * NH], gateT[:, P * a:P * a + P],
                                    ident[0:3 * NH, 0:3 * NH])
            last.then_inc(gate_turned, 1)
            for name in ("q", "k"):
                tile_stage(name, hHi, hLo, tile_dve, TD[name])
            pe.wait_ge(xc_landed, 8 * 16)
            pe.wait_ge(pos_ready, 1)
            pe.wait_ge(v_ready, 4)
            for j in range(4):
                for r in range(16):
                    last = mm(bank[2 + j][:, 0:(NKV + 1) * NCMP], w1[:, j // 2, r, P * (j % 2):P * (j % 2) + P],
                              Xc[:, j // 2, :, 2 * r:2 * r + 16 * (NCMP - 1) + 1:16], r == 0, r == 15)
                last.then_inc(hid_done, 1)
            pe.wait_ge(hid_ready, 4)
            pe.wait_ge(hid_padded, 1)
            pe.wait_ge(gate_ready, 1)
            for kk in range(2):
                last = mm(bank[6][:, 0:P], w2[:, 0, kk, :], hidK[:, kk, :, :], kk == 0, kk == 1)
            last.then_inc(kc_done, 1)
            for h in range(NKV):
                for kk in range(2):
                    last = mm(bank[7][:, HD * h:HD * h + HD], hidV[:, kk, h, :, :].rearrange("p g n -> p (g n)"),
                              w2[:, 1, kk, 0:HD], kk == 0, kk == 1)
            last.then_inc(vc_done, 1)

            def compressed_scores(qi):
                if qi >= 1:
                    pe.wait_ge(ptc_ready, qi)
                for m in range(8):
                    last = mm(bank[7][:, 64 * m:64 * m + 64], qT[:, m, P * qi:P * qi + P], kcT[:, m // 2, :, :], True, True)
                last.then_inc(cscore_done, 1)

            def compressed_turn(qi):
                pe.wait_ge(csum_ready, qi + 1)
                for kv in range(NKV):
                    last = pe.transpose(bank[7][:, P * kv:P * kv + P], Tc[:, 4 * kv:4 * kv + 4, :].rearrange(
                        "p h n -> p (h n)"), ident[:, :])
                last.then_inc(cturned, 1)

            pe.wait_ge(kc_ready, 1)
            pe.wait_ge(vc_ready, 1)
            pe.wait_ge(tile_dve, TD["nsa"])
            compressed_scores(0)
            pe.wait_ge(ks_landed, 32)
            for u in range(UNITS + PV):
                for v in (u, u + 1) if u < UNITS and u % 2 == 0 else ():
                    m, br, e, qi = unit(v)
                    if v >= 3:
                        pe.wait_ge(max_done, v - 2)
                    half, kv = slice(64 * e, 64 * e + 64), m // 2
                    keys = kT if kv % 2 == e else kS
                    mm(bank[SCORE_BANKS[v % 3]][:, 0:P * (qi + 1)], qT[half, m, P * qi:P * qi + P],
                       keys[half, 2 * br + kv // 2, 0:P * (qi + 1)], True, True).then_inc(score_done, 1)
                if u == FIRST_TURN:
                    compressed_turn(0)
                if u // 32 < 3:
                    if u % 32 == CMP_SCORE:
                        compressed_scores(u // 32 + 1)
                    elif u % 32 == CMP_TURN:
                        compressed_turn(u // 32 + 1)
                v = u - TURN
                if 0 <= v < UNITS:
                    qi = unit(v)[3]
                    pe.wait_ge(exp_done, v + 1)
                    pe.wait_ge(diag_ready, v + 1)
                    if v >= 2:
                        pe.wait_ge(turned_act if v % 2 else turned_dve, v // 2)
                    for kt in range(qi + 1):
                        last = mm(bank[2 + v % 2][:, P * kt:P * kt + P], Sr[v % 8][:, P * kt:P * kt + P],
                                  diag[v % 4][:, :], True, True)
                    last.then_inc(turned, 1)
                w = u - PV
                if 0 <= w < UNITS and w % 2 == 1:
                    m, br, _, qi = unit(w)
                    pe.wait_ge(turned_dve, w // 2 + 1)
                    pe.wait_ge(turned_act, w // 2 + 1)
                    c, vcol = P * (m % 4), 256 * br + HD * (m // 2)
                    if w % 16 == 1 and w > 32:
                        pe.wait_ge(ohi_ready, w // 16 - 1)
                        pe.wait_ge(olo_ready, w // 16 - 1)
                    if br == 0:
                        pe.wait_ge(ptc_ready, qi + 1)
                        for e in range(2):
                            mm(bank[4 + w // 16 % 2][64 * e:64 * e + 64, c:c + P], Vbd[:, m // 2, (2 * m + e) % 4, :],
                               PTc[qi % 2][:, m // 2, :], True, False)
                    for kt in range(qi + 1):
                        for e in range(2):
                            last = mm(bank[4 + w // 16 % 2][64 * e:64 * e + 64, c:c + P], VA[:, kt, vcol:vcol + HD],
                                      PTr[(w - 1 + e) % 4][:, P * kt:P * kt + P], False, br == 1 and kt == qi)
                    last.then_inc(pv_done, 2)

            tile_stage("nsa", hHi, hLo, tile_dve, TD["nsa"], made=lambda k: (olo_ready, 7 + k // 4))
            pe.wait_ge(mem_landed, 16)
            for j in range(4):
                for kk in range(2):
                    for a in range(2):
                        c = 256 * kk + P * a
                        last = pe.transpose(bank[2 + j][:, c:c + P], memF[:, a, P * (2 * j + kk):P * (2 * j + kk) + P],
                                            ident[:, :])
                last.then_inc(mem_turned, 1)
            tile_stage("wout", mHi, mLo, tile_dve, TD["wout"], made=lambda k: (mlo_ready, k + 1))

            def mean(n):
                pe.wait_ge(pool_const, 1)
                pe.wait_ge(hsum_ready, 9 * n)
                mm(bank[6][:, :], mean_w[:, :], hsum[:, :], True, True).then_inc(mu_ready, 1)

            def variance(n):
                for m in range(KT):
                    pe.wait_ge(sq_ready, KT * (n - 1) + m + 1)
                    last = mm(bank[7][:, :], mean_w[:, :], sq[:, m, :], m == 0, m == KT - 1)
                last.then_inc(var_done, 1)

            pe.wait_ge(memlo_ready, 4)
            tile_stage("xk", memHi, memLo, tile_dve, TD["xk"], MEM, after_first=lambda: mean(1))
            variance(1)
            for k in range(KT):
                hi, lo = whi[(BLOCKS["xv"] + k) % 2], wlo[(BLOCKS["xv"] + k) % 4]
                pe.wait_ge(w_lo_ready, BLOCKS["xv"] + k + 1)
                for a in range(2):
                    tok = slice(P * a, P * a + P)
                    for half in range(2):
                        w = slice(512 * half, 512 * half + 512)
                        last = mm3(bank[2 + 2 * a + half][:, :], memHi[:, k, tok], memLo[:, k, tok], hi[:, w],
                                   lo[:, w], k == 0, k == KT - 1)
                last.then_inc(w_used, 1)
            tile_stage("xq", hHi, hLo, tile_dve, TD["xq"], made=lambda k: (hlo_ready, KT + k + 1))
            pe.wait_ge(xv_ready, 1)
            pe.wait_ge(tile_dve, TD["xo"])
            NX = 4 * XH
            for n in range(NX + XTURN + 1):
                if n < NX:
                    h, qi = n // 4, n % 4
                    if n >= 4:
                        pe.wait_ge(xexp_done, n - 3)
                    for kk in range(2):
                        last = mm(bank[XSCORE_BANKS[n % 4]][:, 0:MEM], qx[:, 2 * h + kk, P * qi:P * qi + P],
                                  kxT[:, 2 * h + kk, :], kk == 0, kk == 1)
                    last.then_inc(xs_done, 1)
                c = n - XTURN
                if 0 <= c < NX:
                    pe.wait_ge(xp_ready, c + 1)
                    if c >= 2:
                        pe.wait_ge(xpt_ready, c - 1)
                    for kt in range(2):
                        last = pe.transpose(bank[4 + c % 2][:, P * kt:P * kt + P], xP[c % 4][:, P * kt:P * kt + P],
                                            ident[:, :])
                    last.then_inc(xt_done, 1)
                if n % 4 == 3 and n >= 7:
                    h = n // 4 - 1
                    pe.wait_ge(xpt_ready, 4 * h + 4)
                    if h >= 1:
                        pe.wait_ge(xohi_ready, 2 * h)
                        pe.wait_ge(xolo_ready, 2 * h)
                    for dt in range(2):
                        for kt in range(2):
                            c0 = 256 * h + P * dt
                            last = mm(bank[6 + dt][:, :], vx[:, kt, c0:c0 + P], xPT[h % 2][:, kt, :], kt == 0, kt == 1)
                        last.then_inc(xo_done, 1)
            tile_stage("xo", mHi, mLo, tile_dve, TD["xo"], made=lambda k: (xolo_ready, k + 1))
            mean(2)
            variance(2)
            b0 = BLOCKS["fin"]

            def gate_up(i, t):
                pe.wait_ge(sf_ready, i * 2 + (t + 1))
                for s in range(2):
                    c = b0 + 2 * t + s
                    pe.wait_ge(w_lo_ready, i * 4 + (c + 1))
                    for k in range(KT):
                        if t == 0 and s == 0:
                            pe.wait_ge(hlo_ready, 2 * KT + k + 1)
                        w = slice(P * k, P * k + P)
                        last = mm3(bank[2 * t + s][:, :], whi[c % 2][:, w], wlo[c % 4][:, w], hHi[:, k, :], hLo[:, k, :],
                                   k == 0, k == KT - 1)
                    last.then_inc(w_used, 1)

            with pe.Fori(0, KF // 2) as i:
                for t in range(2):
                    gate_up(i, t)
            pe.wait_ge(slo_ready, KF)
            b0 = BLOCKS["fout"]

            def down(k, i=None):
                c = b0 + k
                pe.wait_ge(w_lo_ready, at_step(i, 4, c + 1))
                hidden = slice(k, k + 1) if i is None else bass.ds(i * 4 + k, 1)
                for m in range(KT):
                    w = slice(P * m, P * m + P)
                    last = mm3(bank[m][:, :], whi[c % 2][:, w], wlo[c % 4][:, w], sHi[:, hidden, :], sLo[:, hidden, :],
                               i is None and k == 0, False)
                last.then_inc(w_used, 1)

            down(0)
            with pe.Fori(0, (KF - 2) // 4) as i:
                for k in range(1, 5):
                    down(k, i)
            pe.wait_ge(w_lo_ready, NBLOCKS)
            hi, lo = whi[(NBLOCKS - 1) % 2], wlo[(NBLOCKS - 1) % 4]
            for m in LAST_ORDER:
                w = slice(P * m, P * m + P)
                mm3(bank[m][:, :], hi[:, w], lo[:, w], sHi[:, KF - 1, :], sLo[:, KF - 1, :], False, True).then_inc(
                    fout_done, 1)
            for m in (0, 2, 1, 3):
                pe.wait_ge(last_ready, max(4, LAST_ORDER.index(m) + 1))
                for a in range(4):
                    last = pe.transpose(bank[2 * a][:, P * m:P * m + P], hF[:, m, P * a:P * a + P], ident[:, :])
            last.then_inc(tok_turned, 1)
            pe.wait_ge(last_ready, KT)
            for a in range(4):
                for m in range(4):
                    last = pe.transpose(bank[2 * a + 1][:, P * m:P * m + P], hF[:, 4 + m, P * a:P * a + P], ident[:, :])
                last.then_inc(tok_turned, 1)


_INS = ['x', 'mem', 'ln_emb_g', 'ln_emb_b', 'w_in', 'ssm_a_re', 'ssm_a_im', 'ssm_b_re', 'ssm_b_im', 'ssm_c_re',
        'ssm_c_im', 'ssm_d', 'ssm_log_dt', 'ssm_w_glu', 'ssm_b_glu', 'ssm_w_out', 'cmp_pos', 'cmp_w1', 'cmp_b1',
        'cmp_w2', 'nsa_w_out', 'w_out', 'ln1_g', 'ln1_b', 'xattn_w_q', 'xattn_w_kv', 'xattn_w_o', 'ln2_g', 'ln2_b',
        'ffn_w_in', 'ffn_w_out', 'ln3_g', 'ln3_b']


def kernel(**inputs):
    import numpy as np
    import concourse.bacc as bacc
    from concourse.bass_utils import run_bass_kernel_spmd as run

    nc = bacc.Bacc("TRN2", target_bir_lowering=False, num_devices=1)
    arrays, tensors = {}, {}
    for name in _INS:
        a = np.ascontiguousarray(inputs[name])
        arrays[f"in_{name}"] = a
        tensors[name] = nc.dram_tensor(f"in_{name}", a.shape, mybir.dt.from_np(a.dtype), kind="ExternalInput").ap()
    out = nc.dram_tensor("out_0", (1, T, D), F32, kind="ExternalOutput").ap()
    build(nc, tensors, out)
    r = run(nc, [arrays], core_ids=[0])
    return r.results[0]["out_0"]
```
